# Optimizing a Trainium2 kernel written in Bass

```python
import jax, jax.numpy as jnp
from jax import lax
import numpy as np

D_MODEL = 1024
BATCH = 1
SEQ = 512
DEPTH = 2
DEC_BATCH = 8
DEC_SEQ = 1
PAST_LEN = 256
PAGE_SIZE = 128

HEAD_DIM = 64
N_SB_HEADS = 3 * D_MODEL // (4 * HEAD_DIM)
SB_WIDTH = N_SB_HEADS * HEAD_DIM
N_CONV_CH = SB_WIDTH
N_MEM_HEADS = 4
MEM_WIDTH = N_MEM_HEADS * HEAD_DIM
MIX_WIDTH = SB_WIDTH + MEM_WIDTH
N_MEM = 256
CONV_WIDTH = 31
D_FF = 2816
N_EXPERTS = 8
TOP_K = 2
D_FF_EXPERT = 1408
Q_BLOCK = 128
SB_BIAS_INIT = -6.0
N_A_LAYERS = DEPTH // 2
N_B_LAYERS = DEPTH - N_A_LAYERS
N_DENSE = (DEPTH + 1) // 2
N_MOE = DEPTH // 2
EPS = 1e-6

kernel_name = 'yoco_conformer_stickbreaking_decoder_step'

def rmsnorm(x, g):
    x32 = x.astype(jnp.float32)
    y = x32 * lax.rsqrt(jnp.mean(x32 * x32, axis=-1, keepdims=True) + EPS)
    return (y * g.astype(jnp.float32)).astype(x.dtype)

def layernorm(x, g, b):
    x32 = x.astype(jnp.float32)
    mu = jnp.mean(x32, axis=-1, keepdims=True)
    xc = x32 - mu
    y = xc * lax.rsqrt(jnp.mean(xc * xc, axis=-1, keepdims=True) + EPS)
    return (y * g.astype(jnp.float32) + b.astype(jnp.float32)).astype(x.dtype)

def swiglu(h, wg, wu, wd):
    return (jax.nn.silu(h @ wg) * (h @ wu)) @ wd

def moe_ffn(h, w_router, b_router, wg, wu, wd):
    logits = jnp.einsum('btd,de->bte', h, w_router, preferred_element_type=jnp.float32) + b_router.astype(jnp.float32)
    probs = jax.nn.softmax(logits, axis=-1)
    top_p, top_i = lax.top_k(probs, TOP_K)
    top_p = top_p / jnp.sum(top_p, axis=-1, keepdims=True)
    gates = jnp.sum(jax.nn.one_hot(top_i, N_EXPERTS, dtype=jnp.float32) * top_p[..., None], axis=-2)
    gates = gates.astype(h.dtype)
    y = jnp.zeros_like(h)
    for e in range(N_EXPERTS):
        y = y + gates[..., e:e + 1] * swiglu(h, wg[e], wu[e], wd[e])
    return y

def mem_attention(q, mem_k, mem_v):
    s = jnp.einsum('bthd,bmhd->bhtm', q, mem_k, preferred_element_type=jnp.float32) * HEAD_DIM ** -0.5
    p = jax.nn.softmax(s, axis=-1).astype(mem_v.dtype)
    return jnp.einsum('bhtm,bmhd->bthd', p, mem_v)

def _stick_breaking_block(q, k, v, bias, q_pos, k_pos):
    z = jnp.einsum('bthd,bshd->bhts', q, k, preferred_element_type=jnp.float32) * HEAD_DIM ** -0.5
    z = z + bias.astype(jnp.float32)[None, :, None, None]
    causal = k_pos[None, :] < q_pos[:, None]
    log_keep = jnp.where(causal, jax.nn.log_sigmoid(-z), 0.0)
    between = lax.cumsum(log_keep, axis=3, reverse=True) - log_keep
    w = jnp.where(causal, jnp.exp(jax.nn.log_sigmoid(z) + between), 0.0)
    return jnp.einsum('bhts,bshd->bthd', w.astype(v.dtype), v)

def stick_breaking_attention(q, k, v, bias):
    B, T, H, Dh = q.shape
    S = k.shape[1]
    k_pos = jnp.arange(S)
    q_pos = jnp.arange(T) + (S - T)
    if T % Q_BLOCK != 0:
        return _stick_breaking_block(q, k, v, bias, q_pos, k_pos)
    nb = T // Q_BLOCK
    qb = jnp.moveaxis(q.reshape(B, nb, Q_BLOCK, H, Dh), 1, 0)
    pb = q_pos.reshape(nb, Q_BLOCK)
    ob = lax.map(lambda a: _stick_breaking_block(a[0], k, v, bias, a[1], k_pos), (qb, pb))
    return jnp.moveaxis(ob, 0, 1).reshape(B, T, H, Dh)

def conv_module_tail(u_ext, conv_w, conv_b, ln_g, ln_b):
    c = lax.conv_general_dilated(u_ext, conv_w[:, None, :], (1,), 'VALID',
                                 dimension_numbers=('NWC', 'WIO', 'NWC'),
                                 feature_group_count=N_CONV_CH) + conv_b
    return jax.nn.silu(layernorm(c, ln_g, ln_b))

def mem_kv_projection(mem, g_mem, w_mem_kv):
    ks, vs = [], []
    B = mem.shape[0]
    for layer in range(DEPTH):
        kv = rmsnorm(mem, g_mem[layer]) @ w_mem_kv[layer]
        mk, mv = jnp.split(kv, [MEM_WIDTH], axis=-1)
        ks.append(mk.reshape(B, N_MEM, N_MEM_HEADS, HEAD_DIM))
        vs.append(mv.reshape(B, N_MEM, N_MEM_HEADS, HEAD_DIM))
    return jnp.stack(ks), jnp.stack(vs)

def trunk(x, mem_k, mem_v, conv_prev, kv_past, prm):
    B, T, _ = x.shape
    new_conv = []
    k_new = v_new = k_all = v_all = None
    for layer in range(DEPTH):
        h = rmsnorm(x, prm['g_pre_mix'][layer])
        if layer < N_A_LAYERS:
            a = layer
            proj = h @ prm['w_in_a'][a]
            ga, gb, qm = jnp.split(proj, [N_CONV_CH, 2 * N_CONV_CH], axis=-1)
            u = ga * jax.nn.sigmoid(gb)
            u_ext = jnp.concatenate([conv_prev[a], u], axis=1)
            new_conv.append(u_ext[:, -(CONV_WIDTH - 1):])
            o_main = conv_module_tail(u_ext, prm['conv_w'][a], prm['conv_b'][a],
                                      prm['conv_ln_g'][a], prm['conv_ln_b'][a])
            w_out = prm['w_out_a'][a]
        else:
            bi = layer - N_A_LAYERS
            proj = h @ prm['w_q_b'][bi]
            q, qm = jnp.split(proj, [SB_WIDTH], axis=-1)
            q = q.reshape(B, T, N_SB_HEADS, HEAD_DIM)
            o_main = stick_breaking_attention(q, k_all, v_all, prm['sb_bias'][bi]).reshape(B, T, SB_WIDTH)
            w_out = prm['w_out_b'][bi]
        o_mem = mem_attention(qm.reshape(B, T, N_MEM_HEADS, HEAD_DIM), mem_k[layer], mem_v[layer])
        mix = jnp.concatenate([o_main, o_mem.reshape(B, T, MEM_WIDTH)], axis=-1) @ w_out
        x = x + rmsnorm(mix, prm['g_post_mix'][layer])
        h = rmsnorm(x, prm['g_pre_ffn'][layer])
        i = layer // 2
        if layer % 2 == 0:
            f = swiglu(h, prm['w_gate_d'][i], prm['w_up_d'][i], prm['w_down_d'][i])
        else:
            f = moe_ffn(h, prm['w_router'][i], prm['b_router'][i],
                        prm['w_gate_e'][i], prm['w_up_e'][i], prm['w_down_e'][i])
        x = x + rmsnorm(f, prm['g_post_ffn'][layer])
        if layer == N_A_LAYERS - 1:
            kv = rmsnorm(x, prm['g_kv']) @ prm['w_kv']
            k_new, v_new = jnp.split(kv, [SB_WIDTH], axis=-1)
            k_new = k_new.reshape(B, T, N_SB_HEADS, HEAD_DIM)
            v_new = v_new.reshape(B, T, N_SB_HEADS, HEAD_DIM)
            if kv_past is None:
                k_all, v_all = k_new, v_new
            else:
                k_all = jnp.concatenate([kv_past[0], k_new], axis=1)
                v_all = jnp.concatenate([kv_past[1], v_new], axis=1)
    return x, new_conv, k_new, v_new

def setup_inputs(seed: int = 0) -> dict:
    key = jax.random.key(seed)
    ks = iter(jax.random.split(key, 48))
    f32 = jnp.float32

    def nrm(shape, scale):
        return jax.random.normal(next(ks), shape, f32) * scale

    def gain(shape):
        return 1.0 + nrm(shape, 0.02)

    n_pages = PAST_LEN // PAGE_SIZE
    n_used = DEC_BATCH * n_pages
    n_phys = n_used + n_used // 4
    page_table = jax.random.permutation(next(ks), n_phys)[:n_used].reshape(DEC_BATCH, n_pages).astype(jnp.int32)

    return {
        'x_prompt': nrm((BATCH, SEQ, D_MODEL), 1.0),
        'x_sample': nrm((DEC_BATCH, DEC_SEQ, D_MODEL), 1.0),
        'mem_prompt': nrm((BATCH, N_MEM, D_MODEL), 1.0),
        'cache_k': nrm((n_phys, PAGE_SIZE, N_SB_HEADS, HEAD_DIM), 1.0),
        'cache_v': nrm((n_phys, PAGE_SIZE, N_SB_HEADS, HEAD_DIM), 1.0),
        'page_table': page_table,
        'cache_mem_k': nrm((DEPTH, DEC_BATCH, N_MEM, N_MEM_HEADS, HEAD_DIM), 1.0),
        'cache_mem_v': nrm((DEPTH, DEC_BATCH, N_MEM, N_MEM_HEADS, HEAD_DIM), 1.0),
        'state_conv': nrm((N_A_LAYERS, DEC_BATCH, CONV_WIDTH - 1, N_CONV_CH), 0.5),
        'w_in_a': nrm((N_A_LAYERS, D_MODEL, 2 * N_CONV_CH + MEM_WIDTH), D_MODEL ** -0.5),
        'conv_w': nrm((N_A_LAYERS, CONV_WIDTH, N_CONV_CH), CONV_WIDTH ** -0.5),
        'conv_b': nrm((N_A_LAYERS, N_CONV_CH), 0.02),
        'conv_ln_g': gain((N_A_LAYERS, N_CONV_CH)),
        'conv_ln_b': nrm((N_A_LAYERS, N_CONV_CH), 0.02),
        'w_out_a': nrm((N_A_LAYERS, MIX_WIDTH, D_MODEL), MIX_WIDTH ** -0.5),
        'w_q_b': nrm((N_B_LAYERS, D_MODEL, SB_WIDTH + MEM_WIDTH), D_MODEL ** -0.5),
        'w_out_b': nrm((N_B_LAYERS, MIX_WIDTH, D_MODEL), MIX_WIDTH ** -0.5),
        'sb_bias': SB_BIAS_INIT + nrm((N_B_LAYERS, N_SB_HEADS), 0.1),
        'g_kv': gain((D_MODEL,)),
        'w_kv': nrm((D_MODEL, 2 * SB_WIDTH), D_MODEL ** -0.5),
        'g_mem': gain((DEPTH, D_MODEL)),
        'w_mem_kv': nrm((DEPTH, D_MODEL, 2 * MEM_WIDTH), D_MODEL ** -0.5),
        'g_pre_mix': gain((DEPTH, D_MODEL)),
        'g_post_mix': gain((DEPTH, D_MODEL)),
        'g_pre_ffn': gain((DEPTH, D_MODEL)),
        'g_post_ffn': gain((DEPTH, D_MODEL)),
        'w_gate_d': nrm((N_DENSE, D_MODEL, D_FF), D_MODEL ** -0.5),
        'w_up_d': nrm((N_DENSE, D_MODEL, D_FF), D_MODEL ** -0.5),
        'w_down_d': nrm((N_DENSE, D_FF, D_MODEL), D_FF ** -0.5),
        'w_router': nrm((N_MOE, D_MODEL, N_EXPERTS), D_MODEL ** -0.5),
        'b_router': nrm((N_MOE, N_EXPERTS), 0.01),
        'w_gate_e': nrm((N_MOE, N_EXPERTS, D_MODEL, D_FF_EXPERT), D_MODEL ** -0.5),
        'w_up_e': nrm((N_MOE, N_EXPERTS, D_MODEL, D_FF_EXPERT), D_MODEL ** -0.5),
        'w_down_e': nrm((N_MOE, N_EXPERTS, D_FF_EXPERT, D_MODEL), D_FF_EXPERT ** -0.5),
    }

def reference(x_prompt, x_sample, mem_prompt, cache_k, cache_v, page_table, cache_mem_k, cache_mem_v,
              state_conv, w_in_a, conv_w, conv_b, conv_ln_g, conv_ln_b, w_out_a, w_q_b, w_out_b,
              sb_bias, g_kv, w_kv, g_mem, w_mem_kv, g_pre_mix, g_post_mix, g_pre_ffn, g_post_ffn,
              w_gate_d, w_up_d, w_down_d, w_router, b_router, w_gate_e, w_up_e, w_down_e):
    prm = dict(w_in_a=w_in_a, conv_w=conv_w, conv_b=conv_b, conv_ln_g=conv_ln_g, conv_ln_b=conv_ln_b,
               w_out_a=w_out_a, w_q_b=w_q_b, w_out_b=w_out_b, sb_bias=sb_bias, g_kv=g_kv, w_kv=w_kv,
               g_pre_mix=g_pre_mix, g_post_mix=g_post_mix, g_pre_ffn=g_pre_ffn, g_post_ffn=g_post_ffn,
               w_gate_d=w_gate_d, w_up_d=w_up_d, w_down_d=w_down_d, w_router=w_router,
               b_router=b_router, w_gate_e=w_gate_e, w_up_e=w_up_e, w_down_e=w_down_e)

    mem_k_prompt, mem_v_prompt = mem_kv_projection(mem_prompt, g_mem, w_mem_kv)
    b_p = x_prompt.shape[0]
    conv0 = [jnp.zeros((b_p, CONV_WIDTH - 1, N_CONV_CH), x_prompt.dtype) for _ in range(N_A_LAYERS)]
    y_prompt, conv_p, k_prompt, v_prompt = trunk(x_prompt, mem_k_prompt, mem_v_prompt, conv0, None, prm)

    b_s, n_pages = page_table.shape
    past = n_pages * PAGE_SIZE
    k_past = cache_k[page_table].reshape(b_s, past, N_SB_HEADS, HEAD_DIM)
    v_past = cache_v[page_table].reshape(b_s, past, N_SB_HEADS, HEAD_DIM)
    conv_prev = [state_conv[a] for a in range(N_A_LAYERS)]
    y_sample, conv_s, k_sample, v_sample = trunk(x_sample, cache_mem_k, cache_mem_v, conv_prev,
                                                 (k_past, v_past), prm)

    conv_prompt = jnp.stack(conv_p)
    conv_sample = jnp.stack(conv_s)
    return (y_prompt, y_sample, conv_prompt, k_prompt, v_prompt, mem_k_prompt, mem_v_prompt,
            conv_sample, k_sample, v_sample)


_drawn_inputs = setup_inputs


def setup_inputs(seed=0):
    import zlib

    import numpy as np

    out = dict(_drawn_inputs(seed))
    spreads = {}
    factors = {'g_mem': 2.879, 'b_router': 3.179, 'g_kv': 2.91}
    for name, (base, spread) in spreads.items():
        noise = np.random.default_rng([zlib.crc32(name.encode()), seed]).standard_normal(out[name].shape)
        drawn = base * np.exp(spread * noise) if base else spread * noise
        out[name] = __import__('jax').numpy.asarray(drawn.astype(out[name].dtype))
    for name, factor in factors.items():
        out[name] = (out[name] * factor).astype(out[name].dtype)
    return out
```

```python
from contextlib import ExitStack

import concourse.bass as bass
from concourse import mybir

F32 = mybir.dt.float32
F32R = mybir.dt.float32r
I32 = mybir.dt.int32
ACT = mybir.ActivationFunctionType
ALU = mybir.AluOpType
AX = mybir.AxisListType.X

P = 128
D = 1024
KD = D // P
TP = 512
B = 8
T = TP + B
HALF = T // 2
NT = TP // P
NMEM = 256
MT = NMEM // P
HD = 64
NH = 12
FS = NH * HD // P
MH = 4
FM = MH * HD // P
CW = 31
PAST = CW - 1
PAGE = 128
NPG = 2
DFF = 2816
KF = DFF // P
E = 8
DFE = 1408
KE = DFE // P
C = 192
CB = C - P
MAXJOBS = (2 * T + E * C) // C
SLOTS = (MAXJOBS + 2) * C
EPS = 1e-6
CLAMP = 40.0

G_PRE_MIX, G_POST_MIX, G_PRE_FFN, G_POST_FFN, G_KV, G_MEM = 0, 16, 32, 48, 64, 72
G_CB, G_LNG, G_LNB, G_ROWS = 88, 94, 100, 106

U_MEM, U_IN, U_QM, U_OUTA, U_GU, U_DN, U_KV, U_Q, U_OUTB, U_END = 0, 4, 10, 11, 15, 37, 49, 55, 59, 63
M_MEM, M_IN, M_QM, M_OUTA, M_GU, M_DN, M_KV, M_Q, M_OUTB, M_END = 0, 8, 20, 22, 30, 74, 82, 94, 102, 110
T_N0, T_MIXA, T_P0, T_N1, T_P1, T_N2, T_N3, T_MIXB, T_P2 = 0, 8, 16, 24, 32, 40, 48, 56, 64
NTMP = 4
HI_AT = {t: n for n, t in enumerate([t0 + k for t0 in (T_N0, T_MIXA, T_N1, T_N2, T_N3, T_MIXB) for k in range(KD)])}
MIX_A = [6, 7, 0, 1, 2, 3, 4, 5]
S_X0, S_YA, S_XA, S_YF, S_XF, S_YB, S_XB = 0, 8, 18, 26, 36, 44, 54
TP_CTL, TP_X, TP_MEM, TP_ST, TP_UT, TP_MA, TP_KV, TP_PG, TP_MB, TP_HT, TP_XT = 0, 2, 11, 15, 18, 20, 29, 49, 73, 82, 92


def build(nc, a, o):
    (y_prompt, y_sample, conv_prompt, k_prompt, v_prompt, mem_k_prompt, mem_v_prompt,
     conv_sample, k_sample, v_sample) = o
    with ExitStack() as ctx:
        def at(name, shape, dt, offset):
            return nc.alloc_sbuf_tensor_at(name, shape, dt, offset=base0 + offset)

        def small(name, shape, dt=F32):
            return ctx.enter_context(nc.sbuf_tensor(name, shape, dt))

        def sem(name):
            return ctx.enter_context(nc.semaphore(name))

        ARENA = 190592
        base0 = -(-nc.sbuf_base // 64) * 64
        ctx.enter_context(nc.sbuf_tensor("arena", [P, ARENA // 4 + 16], F32))
        x = at("x", [P, KD, T], F32, 0)
        hh = at("hh", [P, KD, T], F32R, 16640)
        hl = at("hl", [P, KD, T], F32R, 33280)
        raw = at("raw", [P, 2, 2048], F32, 49920)
        whi = at("whi", [P, 2, 2048], F32R, 66304)
        wlo = at("wlo", [P, 2, 2048], F32R, 82688)
        A = 99072
        y_dn = at("y_dn", [P, KD, T], F32, 16640)
        xtok = at("xtok", [P, NT, D], F32, A)
        xdec = at("xdec", [P, D], F32, A + 16384)
        memtok = at("memtok", [P, MT, D], F32, A + 20480)
        mT = at("mT", [P, KD, NMEM], F32, A + 28672)
        hmh = at("hmh", [P, 2, KD, NMEM], F32R, A + 36864)
        hml = at("hml", [P, 2, KD, NMEM], F32R, A + 53248)
        mkv = at("mkv", [P, 2, 2, MT, NMEM], F32, A + 69632)
        grow = at("grow", [P, P], F32, A + 77824)
        crow = at("crow", [P, 2, P], F32, A + 78336)
        cT = at("cT", [P, FS, T], F32, A)
        udec = at("udec", [P, FS, B, CW], F32, A + 12480)
        sttok = at("sttok", [P, 2, FS * P], F32, A + 18432)
        ctmp = at("ctmp", [P, B, CW], F32, A + 24576)
        qmA = at("qmA", [P, FM, T], F32, A + 25600)
        MA = 29760
        ubuf = at("ubuf", [P, FS, PAST + T], F32, A + 72192)
        utail = at("utail", [P, FS * P], F32, A + 85408)
        y_mix = at("y_mix", [P, KD, T], F32, A + 39424)
        mean = at("mean", [P, T], F32, A + 88480)
        acth = at("acth", [P, KF, T], F32R, A)
        actl = at("actl", [P, KF, T], F32R, A + 45760)
        kT = at("kT", [P, FS, T], F32, A)
        vT = at("vT", [P, FS, T], F32, A + 12480)
        vtok = at("vtok", [P, NT, FS * P], F32, A + 24960)
        ktok = at("ktok", [P, NT, FS * P], F32, A + 37248)
        kvdec = at("kvdec", [P, 2, FS * P], F32, A + 49536)
        qT = at("qT", [P, KD, T], F32, A + 55680)
        SEG = 1280
        sp = [at(f"sp{i}", [P, SEG], F32, A + 12480 + 5120 * i) for i in range(2)]
        wt = [at(f"wt{i}", [P, SEG], F32, A + 37248 + 5120 * i) for i in range(2)]
        zc = [at("zc0", [P, SEG], F32, A + 47488), at("zc1", [P, SEG], F32, A + 72320)]
        pgs = at("pgs", [P, 2, NPG, FS * P], F32, A + 77440)
        pgT = at("pgT", [P, 2, FS, NPG * P], F32, A + 37248)
        zd = at("zd", [P, 4, 192], F32, A + 49536)
        qd2 = at("qd2", [P, B, FS, 2], F32, A + 52608)

        class Mem:
            pass

        mem = []
        for layer, off in ((0, A + MA), (1, A)):
            m = Mem()
            m.ktok = at(f"mktok{layer}", [P, MT, NMEM], F32, off)
            m.vtok = at(f"mvtok{layer}", [P, MT, NMEM], F32, off + 2048)
            m.kT = at(f"mkT{layer}", [P, FM, NMEM], F32, off + 4096)
            m.qz = at(f"mqz{layer}", [P, B * FM, 32], F32, off + 6144)
            m.pd = at(f"mpd{layer}", [32, NMEM], F32, off + 8192)
            m.pdT = at(f"mpdT{layer}", [P, MT, 32], F32, off + 9216)
            m.cache = at(f"mcache{layer}", [P, B, MT, NMEM], F32, off + 9664)
            m.cT = at(f"mcT{layer}", [P, B, FM, NMEM], F32, off + 26048)
            m.p = at(f"mp{layer}", [P, 2, NT, NMEM], F32, off + 26048)
            m.pT = at(f"mpT{layer}", [P, MT, TP], F32, off + 34240)
            mem.append(m)

        hf = at("hf", [P, KD, T], F32, 132992)
        htok = at("htok", [P, NT + 1, D], F32, 149632)
        xtk = at("xtk", [P, NT + 1, D], F32, 170112)
        ewh = at("ewh", [P, 3, 2048], F32R, 16640)
        ewl = at("ewl", [P, 3, 2048], F32R, 41216)
        eraw = at("eraw", [P, 6, 2048], F32, 65792)
        gtok = at("gtok", [P, 2, D], F32, 114944)
        ejh = at("ejh", [P, KD, C], F32R, 131328)
        ejl = at("ejl", [P, KD, C], F32R, 137472)
        eah = at("eah", [P, KE, C], F32R, 143616)
        eal = at("eal", [P, KE, C], F32R, 152064)
        ey = at("ey", [P, KD, C], F32, 160512)
        etok = at("etok", [P, 2, D], F32, 0)
        esg = at("esg", [P, 2, C], F32, 8192)
        eat = at("eat", [P, 2, C], F32, 8192 + 1536)
        yr = at("yr", [P, 2, 2, D], F32, 16640)
        fo = at("fo", [P, 2, D], F32, 33024)
        fs = at("fs", [P, 2, D], F32, 41216)
        gpost = at("gpost", [P, D], F32, 49408)

        sq = small("sq", [P, 2, T])
        rstd = small("rstd", [P, T])
        tmp = small("tmp", [P, NTMP, T])
        ident = small("ident", [P, P])
        negtri = small("negtri", [P, P])
        negone = small("negone", [P, P])
        ones = small("ones", [P, P])
        before = small("before", [P, P])
        gT = small("gT", [P, G_ROWS])
        cwT = small("cwT", [P, CW, FS])
        bias = small("bias", [P, B, NH])
        eps = small("eps", [P, 1])
        stm = small("stm", [P, 2, NT])
        sts = small("sts", [P, 2, NT])
        ms = small("ms", [P, 4])
        od = small("od", [P, FS, B])
        ptab = small("ptab", [1, B * NPG], I32)
        wr = small("wr", [P, KD, E])
        br = small("br", [P, E])
        zero = small("zero", [P, HALF])
        R = 123136
        rt = at("rt", [P, 8, NT + 1, E], F32, R)
        r5 = at("r5", [P, 12, NT + 1], F32, R + 1280)
        r8 = at("r8", [P, 6, E], F32, R + 1536)
        io8 = at("io8", [P, NT + 1, E], F32, R + 1728)
        ioj = at("ioj", [P, MAXJOBS, E], F32, R + 1888)
        ioi = at("ioi", [P, MAXJOBS, E], I32, R + 2304)
        ioe = at("ioe", [P, NT + 1, E], I32, R + 2720)
        jcmp = at("jcmp", [P, MAXJOBS, E], F32, R + 2880)
        jobf = at("jobf", [P, MAXJOBS + 1], F32, R + 3296)
        jobi = at("jobi", [P, MAXJOBS + 1], I32, R + 3360)
        sloti = at("sloti", [P, 2, NT + 1], I32, R + 3424)
        valid = at("valid", [P, NT + 1], F32, R + 3488)
        gate = at("gate", [P, 2, NT + 1], F32, R + 3520)
        frs = at("frs", [P, NT + 1, 2], F32, R + 3584)

        ps = ctx.enter_context(nc.psum_tensor("ps", [P, 8, 512], F32))
        flat = ps[:, :, :].rearrange("p b n -> p (b n)")

        xs = nc.dram_tensor("xs", (SLOTS, D), F32, kind="Internal").ap()
        ys = nc.dram_tensor("ys", (SLOTS, D), F32, kind="Internal").ap()

        x_in, mem_in, tabs_in, state_in, small_in, const_ready = map(
            sem, "x_in mem_in tabs_in state_in small_in const_ready".split())
        w_in = [sem("w_in0"), sem("w_in1")]
        w_hi, w_lo, w_used = map(sem, "w_hi w_lo w_used".split())
        tile_done = sem("tile_done")
        tile_free = [sem("tile_free0"), sem("tile_free1")]
        tmp_ready, hi_ready, tmp_used = map(sem, "tmp_ready hi_ready tmp_used".split())
        sq_ready, sq_used, stat_done, root_ready, rstd_ready = map(
            sem, "sq_ready sq_used stat_done root_ready rstd_ready".split())
        tp_done = sem("tp_done")
        tp_free = [sem("tp_free0"), sem("tp_free1")]
        mem_ss, mem_root, mem_inv, mem_sc, hm_hi, hm_lo, mkv_out = map(
            sem, "mem_ss mem_root mem_inv mem_sc hm_hi hm_lo mkv_out".split())
        u_ready, ud_new, cv, cd, cd_sum = map(sem, "u_ready ud_new cv cd cd_sum".split())
        ln_sum, ln_mean, ln_xc, ln_sq, ln_used, ln_var, ln_root, ln_rstd, ln_y = map(
            sem, "ln_sum ln_mean ln_xc ln_sq ln_used ln_var ln_root ln_rstd ln_y".split())
        outs = sem("outs")
        mk_in, mc_in, mv_in, mqz_zero, mqz_ready = map(
            sem, "mk_in mc_in mv_in mqz_zero mqz_ready".split())
        md_s, md_max, md_e, md_inv, md_p, md_t, md_pT, md_o, md_od = map(
            sem, "md_s md_max md_e md_inv md_p md_t md_pT md_o md_od".split())
        mp_s, mp_max, mp_e, mp_inv, mp_p, mp_t, mp_pT, mp_o, mp_out = map(
            sem, "mp_s mp_max mp_e mp_inv mp_p mp_t mp_pT mp_o mp_out".split())
        ga_hi, ga_lo = map(sem, "ga_hi ga_lo".split())
        kv_out = sem("kv_out")
        pg_in = [sem("pg_in0"), sem("pg_in1")]
        pg_used, pg_qk, qd_zero, qd_ready = map(
            sem, "pg_used pg_qk qd_zero qd_ready".split())
        sd_z, sd_zb, sd_zc, sd_e, sd_l, sd_sp, sd_c, sd_x, sd_w, sd_o, sd_od = map(
            sem, "sd_z sd_zb sd_zc sd_e sd_l sd_sp sd_c sd_x sd_w sd_o sd_od".split())
        sb_z, sb_zc, sb_e, sb_l, sb_s, sb_sp, sb_c, sb_w, sb_wm, sb_pv, sb_out = map(
            sem, "sb_z sb_zc sb_e sb_l sb_s sb_sp sb_c sb_w sb_wm sb_pv sb_out".split())
        hf_ready, lg_done, rr, rr_exp, rr_m1, mask_ready, cnt_done, slots_ready, io_int, io_ready = map(
            sem, "hf_ready lg_done rr rr_exp rr_m1 mask_ready cnt_done slots_ready io_int io_ready".split())
        xs_zero, ys_zero, xs_in, gt_in = map(sem, "xs_zero ys_zero xs_in gt_in".split())
        ew_in = [sem(f"ew_in{i}") for i in range(6)]
        ew_hi, ew_lo, ew_used, eg_done, es_ready, ea_tmp, ea_hi, ea_lo = map(
            sem, "ew_hi ew_lo ew_used eg_done es_ready ea_tmp ea_hi ea_lo".split())
        ed_done, ey_ready, er_done, ej_hi, ys_out, ys_ready = map(
            sem, "ed_done ey_ready er_done ej_hi ys_out ys_ready".split())
        er_free = [sem("er_free0"), sem("er_free1")]
        yr_in = [sem("yr_in0"), sem("yr_in1")]
        gp_in, f_1, f_2, f_ss, f_root, f_inv, f_n, f_y = map(
            sem, "gp_in f_1 f_2 f_ss f_root f_inv f_n f_y".split())
        y_out = [sem("y_out0"), sem("y_out1")]


        block = ctx.enter_context(nc.Block())

        def halves(ap):
            return ap.rearrange("p (h n) -> p h n", h=2)

        def pair(q):
            return ps[:, 2 * q:2 * q + 2, 0:HALF]

        def heads(ap):
            return ap.rearrange("m h d -> m (h d)")

        def row_broadcast(src, shape_ap):
            return bass.AP(tensor=src.tensor, offset=src.offset, ap=[[0, P]] + shape_ap)

        def copied_out(e, f):
            e.wait_ge(tp_free[f % 2], f // 2 + 1)

        def gain(off, k):
            return gT[:, off + k:off + k + 1]

        win, wgd, wud = a["w_in_a"][0], a["w_gate_d"][0], a["w_up_d"][0]
        xs_t = xs.rearrange("(b c) d -> b c d", c=C)
        ys_t = ys.rearrange("(b c) d -> b c d", c=C)
        DN_CUTS = [2, 2, 2, 2, 1, 1, 1]
        DN_K0 = [sum(DN_CUTS[:i]) for i in range(len(DN_CUTS))]
        seg_w = {i: TP - P * i for i in range(NT)}
        PER_JOB = KE + len(DN_CUTS)
        RAW, SPLIT = 6, 3
        assert PER_JOB % RAW == 0 and PER_JOB % SPLIT == 0 and sum(DN_CUTS) == KE
        SEG_AT = {0: 0, 1: 512, 3: 896, 2: 1024}

        @block.sync
        def _(e):
            g2 = a["g_mem"]
            n = 0
            for name in ("g_pre_mix", "g_post_mix", "g_pre_ffn", "g_post_ffn"):
                e.dma_start(grow[n:n + 16, :], a[name].rearrange("l (k p) -> (l k) p", p=P)).then_inc(tabs_in, 16)
                n += 16
            e.dma_start(grow[G_KV:G_KV + 8, :], a["g_kv"].rearrange("(k p) -> k p", p=P)).then_inc(tabs_in, 16)
            e.dma_start(grow[G_MEM:G_MEM + 16, :], g2.rearrange("l (k p) -> (l k) p", p=P)).then_inc(tabs_in, 16)
            for off, name in ((G_CB, "conv_b"), (G_LNG, "conv_ln_g"), (G_LNB, "conv_ln_b")):
                e.dma_start(grow[off:off + FS, :], a[name].rearrange("l (k p) -> (l k) p", p=P)).then_inc(tabs_in, 16)
            taps = a["conv_w"][0].rearrange("j (f p) -> (j f) p", p=P)
            for i in range(2):
                e.dma_start(crow[0:93, i, :], taps[93 * i:93 * i + 93, :]).then_inc(tabs_in, 16)
            xp = a["x_prompt"][0]
            for i in range(NT):
                e.dma_start(xtok[:, i, :], xp[i * P:(i + 1) * P, :]).then_inc(x_in, 16)
            e.dma_start(xdec[0:B, :], a["x_sample"].rearrange("b s d -> (b s) d")).then_inc(x_in, 16)
            e.dma_start(memtok[:, :, :], a["mem_prompt"][0].rearrange("(m p) d -> p m d", p=P)).then_inc(mem_in, 16)

            def rows(w, col, k0, k1, cols=2 * P):
                return w[k0 * P:k1 * P, :].rearrange("(k p) n -> p k n", p=P)[:, :, bass.ds(col, cols)]

            def load_whole(s, w, col, k0=0, k1=KD):
                v = raw[:, s, :].rearrange("p (k n) -> p k n", n=2 * P)
                h = (k0 + k1) // 2
                e.dma_start(v[:, 0:h - k0, :], rows(w, col, k0, h)).then_inc(w_in[s], 16)
                e.dma_start(v[:, h - k0:k1 - k0, :], rows(w, col, h, k1)).then_inc(w_in[s], 16)

            def load_pair(s, w1, col1, w2, col2):
                v = raw[:, s, :].rearrange("p (k j n) -> p k j n", k=KD, j=2)
                e.dma_start(v[:, :, 0, :], rows(w1, col1, 0, KD, P)).then_inc(w_in[s], 16)
                e.dma_start(v[:, :, 1, :], rows(w2, col2, 0, KD, P)).then_inc(w_in[s], 16)

            for g in range(2):
                load_whole(g, a["w_mem_kv"][0], g * NMEM)
            e.dma_start(ptab[:, :], a["page_table"].rearrange("(o b) g -> o (b g)", o=1)).then_inc(small_in, 16)
            e.dma_start(bias[:, :, :], row_broadcast(a["sb_bias"], [[0, B], [1, NH]])).then_inc(small_in, 16)
            e.dma_start(wr[:, :, :], a["w_router"][0].rearrange("(k p) e -> p k e", p=P)).then_inc(small_in, 16)
            e.dma_start(br[:, :], row_broadcast(a["b_router"], [[1, E]])).then_inc(small_in, 16)
            e.wait_ge(tp_done, TP_ST)
            st = a["state_conv"][0].rearrange("b r c -> (b r) c")
            for i in range(2):
                e.dma_start(sttok[0:4 * PAST, i, :], st[4 * PAST * i:4 * PAST * (i + 1), :]).then_inc(state_in, 16)
            for g in range(2, 4):
                e.wait_ge(w_lo, g - 1)
                load_whole(g % 2, a["w_mem_kv"][1], (g - 2) * NMEM)
            for p in range(2):
                e.wait_ge(w_lo, U_IN + p - 1)
                load_pair((U_IN + p) % 2, win, p * P, win, (FS + p) * P)
            for layer in range(2):
                for w, dst in enumerate((mem_k_prompt, mem_v_prompt)):
                    for t in range(MT):
                        e.wait_ge(tile_free[t], 2 * layer + w + 1)
                    e.dma_start(dst[layer, 0].rearrange("(m p) h d -> p m (h d)", p=P),
                                mkv[:, layer, w, :, :]).then_inc(mkv_out, 16)
            with e.Fori(1, 3) as i:
                for j in range(2):
                    e.wait_ge(w_lo, i * 2 + (U_IN + j - 1))
                    load_pair((U_IN + j) % 2, win, i * (2 * P) + j * P, win, i * (2 * P) + (FS + j) * P)
            e.wait_ge(w_lo, U_QM - 1)
            load_whole(U_QM % 2, win, 2 * FS * P)

            def mem_loads(layer):
                m = mem[layer]
                e.wait_ge(mkv_out, 64)
                e.dma_start(m.ktok[:, :, :], mem_k_prompt[layer, 0].rearrange("(m p) h d -> p m (h d)", p=P))\
                    .then_inc(mk_in, 16)
                e.dma_start(m.vtok[:, :, :], mem_v_prompt[layer, 0].rearrange("(m p) h d -> p m (h d)", p=P))\
                    .then_inc(mk_in, 16)
                for b in range(B):
                    e.dma_start(m.cache[:, b, :, :], a["cache_mem_k"][layer, b].rearrange("(m p) h d -> p m (h d)", p=P))\
                        .then_inc(mc_in, 16)
                e.wait_ge(tp_done, (TP_MA, TP_MB)[layer] + 9)
                for b in range(B):
                    e.dma_start(m.cache[:, b, :, :], a["cache_mem_v"][layer, b].rearrange("(m p) h d -> p m (h d)", p=P))\
                        .then_inc(mv_in, 16)

            for i in range(2):
                e.wait_ge(w_lo, U_OUTA + i - 1)
                load_whole((U_OUTA + i) % 2, a["w_out_a"][0], i * 2 * P)
            mem_loads(0)
            copied_out(e, TP_UT)
            copied_out(e, TP_UT + 1)
            e.dma_start(conv_prompt[0, 0], utail[0:PAST, :]).then_inc(outs, 16)
            e.dma_start(conv_sample[0, :, PAST - 1, :], utail[PAST:PAST + B, :]).then_inc(outs, 16)
            e.dma_start(conv_sample[0, :, 0:PAST - 1, :], a["state_conv"][0, :, 1:PAST, :]).then_inc(outs, 16)
            for i in range(2, 4):
                e.wait_ge(w_lo, U_OUTA + i - 1)
                load_whole((U_OUTA + i) % 2, a["w_out_a"][0], i * 2 * P)
            with e.Fori(0, KF // 2) as i:
                for j in range(2):
                    e.wait_ge(w_lo, i * 2 + (U_GU + j - 1))
                    load_pair((U_GU + j) % 2, wgd, i * (2 * P) + j * P, wud, i * (2 * P) + j * P)
            with e.Fori(0, 2) as i:
                for j in range(6):
                    e.wait_ge(w_lo, i * 6 + (U_DN + j - 1))
                    r = j % 3
                    load_whole((U_DN + j) % 2, a["w_down_d"][0], i * (4 * P) + (j // 3) * 2 * P,
                               8 * r, min(8 * r + 8, KF))
            with e.Fori(0, 3) as i:
                for j in range(2):
                    e.wait_ge(w_lo, i * 2 + (U_KV + j - 1))
                    load_whole((U_KV + j) % 2, a["w_kv"], i * (4 * P) + j * 2 * P)
            e.wait_ge(small_in, 64)
            e.wait_ge(tile_done, M_KV)
            kp = a["cache_k"].rearrange("n s h d -> n s (h d)")
            vp = a["cache_v"].rearrange("n s h d -> n s (h d)")

            def load_pages(s, src, b):
                for g in range(NPG):
                    page = e.value_load(ptab[0:1, bass.ds(b * NPG + g, 1)], min_val=0, max_val=src.shape[0] - 1)
                    e.dma_start(pgs[:, s, g:g + 1, :], src[bass.ds(page, 1)].rearrange("n s c -> s n c"))\
                        .then_inc(pg_in[s], 16)

            for b in range(2):
                load_pages(b, kp, b)
            with e.Fori(0, 2) as i:
                for j in range(2):
                    e.wait_ge(w_lo, i * 2 + (U_Q + j - 1))
                    load_whole((U_Q + j) % 2, a["w_q_b"][0], i * (4 * P) + j * 2 * P)
            for i in range(2):
                e.wait_ge(w_lo, U_OUTB + i - 1)
                load_whole((U_OUTB + i) % 2, a["w_out_b"][0], i * 2 * P)
            with e.Fori(1, B // 2) as i:
                for j in range(2):
                    e.wait_ge(pg_used, i * 2 + (j - 1))
                    load_pages(j, kp, i * 2 + j)
            with e.Fori(0, B // 2) as i:
                for j in range(2):
                    e.wait_ge(pg_used, i * 2 + (B + j - 1))
                    load_pages(j, vp, i * 2 + j)
            e.wait_ge(sb_pv, NH)
            mem_loads(1)
            for i in range(2, 4):
                e.wait_ge(w_lo, U_OUTB + i - 1)
                load_whole((U_OUTB + i) % 2, a["w_out_b"][0], i * 2 * P)

            def load_rows(blk):
                e.dma_start(gtok[:, 0:1, :], xs_t[bass.ds(blk, 1), 0:P, :].rearrange("o c d -> c o d"))\
                    .then_inc(gt_in, 16)
                e.dma_start(gtok[0:CB, 1:2, :], xs_t[bass.ds(blk, 1), P:C, :].rearrange("o c d -> c o d"))\
                    .then_inc(gt_in, 16)

            e.wait_ge(slots_ready, 1)
            nj = e.value_load(jobi[0:1, MAXJOBS:MAXJOBS + 1], min_val=E, max_val=MAXJOBS)
            e.wait_ge(tile_done, M_END)
            e.wait_ge(xs_in, 160)
            e.wait_ge(ys_zero, 16)
            load_rows(1)
            e.sem_inc(ys_out, 16)

            with e.Fori(0, nj) as j:
                ex = e.value_load(jobi[0:1, bass.ds(j, 1)], min_val=0, max_val=E - 1)
                for u in range(PER_JOB):
                    s = u % RAW
                    e.wait_ge(ew_lo, j * PER_JOB + (u + 1))
                    if u < KE:
                        v = eraw[:, s, :].rearrange("p (k j n) -> p k j n", k=KD, j=2)
                        for t, w in enumerate((a["w_gate_e"][0], a["w_up_e"][0])):
                            e.dma_start(v[:, :, t, :],
                                        w[bass.ds(ex, 1)].rearrange("o (k p) n -> p (o k) n", p=P)[:, :, u * P:(u + 1) * P])\
                                .then_inc(ew_in[s], 16)
                    else:
                        n, k0 = DN_CUTS[u - KE], DN_K0[u - KE]
                        v = eraw[:, s, 0:n * D].rearrange("p (k h n) -> p k h n", k=n, h=2)
                        src = a["w_down_e"][0][bass.ds(ex, 1)].rearrange("o (k p) n -> p (o k) n", p=P)
                        for h in range(2):
                            e.dma_start(v[:, :, h, :], src[:, k0:k0 + n, h * 512:(h + 1) * 512]).then_inc(ew_in[s], 16)
                    if u == 4:
                        e.wait_ge(er_done, j * 8 + 4)
                        load_rows(j + 2)
                    if u == 10:
                        e.wait_ge(er_free[0], j * 4 + 4)
                        e.wait_ge(er_free[1], j * 4 + 4)
                        e.dma_start(ys_t[bass.ds(j, 1), 0:P, :].rearrange("o c d -> c o d"), etok[:, 0:1, :])\
                            .then_inc(ys_out, 16)
                        e.dma_start(ys_t[bass.ds(j, 1), P:C, :].rearrange("o c d -> c o d"), etok[P - CB:P, 1:2, :])\
                            .then_inc(ys_out, 16)
            e.wait_ge(er_free[0], nj * 4 + 4)
            e.wait_ge(er_free[1], nj * 4 + 4)
            e.dma_start(ys_t[bass.ds(nj, 1), 0:P, :].rearrange("o c d -> c o d"), etok[:, 0:1, :]).then_inc(ys_out, 16)
            e.dma_start(ys_t[bass.ds(nj, 1), P:C, :].rearrange("o c d -> c o d"), etok[P - CB:P, 1:2, :]).then_inc(ys_out, 16)
            e.wait_ge(ed_done, nj + 1)
            e.wait_ge(ys_out, nj * 32 + 48)
            e.sem_inc(ys_ready, 1)
            e.dma_start(gpost[:, :], row_broadcast(a["g_post_ffn"][1], [[1, D]])).then_inc(gp_in, 16)
            for i in range(NT):
                e.wait_ge(f_y, i + 1)
                e.dma_start(y_prompt[0, i * P:(i + 1) * P, :], fo[:, i % 2, :]).then_inc(y_out[i % 2], 16)
            e.wait_ge(f_y, NT + 1)
            e.dma_start(y_sample.rearrange("b s d -> (b s) d"), fo[0:B, NT % 2, :]).then_inc(y_out[NT % 2], 16)
            e.wait_ge(y_out[0], 16 * (NT // 2 + 1))
            e.wait_ge(y_out[1], 16 * (NT // 2))
            e.wait_ge(outs, 48)
            e.wait_ge(kv_out, 64)

        @block.gpsimd
        def _(e):
            e.memset(ident[:, :], 0.0).then_inc(const_ready, 1)
            e.memset(zero[:, :], 0.0).then_inc(const_ready, 1)
            e.memset(eps[:, :], EPS).then_inc(const_ready, 1)
            e.memset(ones[:, :], 1.0).then_inc(const_ready, 1)
            e.memset(negone[:, :], -1.0).then_inc(const_ready, 1)
            e.memset(negtri[:, :], -1.0).then_inc(const_ready, 1)
            e.memset(before[:, :], 1.0).then_inc(const_ready, 1)
            e.wait_ge(const_ready, 7)
            e.affine_select(out=ident[:, :], in_=ident[:, :], compare_op=ALU.not_equal, fill=1.0, base=0,
                            pattern=[[-1, P]], channel_multiplier=1).then_inc(const_ready, 1)
            e.affine_select(out=negtri[:, :], in_=negtri[:, :], compare_op=ALU.is_ge, fill=0.0, base=0,
                            pattern=[[-1, P]], channel_multiplier=1).then_inc(const_ready, 1)
            e.affine_select(out=before[:, :], in_=before[:, :], compare_op=ALU.is_gt, fill=0.0, base=0,
                            pattern=[[1, P]], channel_multiplier=-1).then_inc(const_ready, 1)

            def lo_of(g):
                s = g % 2
                e.wait_ge(w_hi, g + 1)
                e.tensor_tensor(out=wlo[:, s, :], in0=raw[:, s, :], in1=whi[:, s, :].bitcast(F32), op=ALU.subtract).then_inc(w_lo, 1)

            def lo_of_at(c, i, n):
                s = c % 2
                e.wait_ge(w_hi, i * n + (c + 1))
                e.tensor_tensor(out=wlo[:, s, :], in0=raw[:, s, :], in1=whi[:, s, :].bitcast(F32), op=ALU.subtract).then_inc(w_lo, 1)

            def lo_tiles(t0, ks):
                for n, k in enumerate(ks):
                    t = t0 + n
                    e.wait_ge(hi_ready, HI_AT[t] + 1)
                    e.tensor_tensor(out=hl[:, k, :], in0=tmp[:, t % NTMP, :],
                                           in1=hh[:, k, :].bitcast(F32), op=ALU.subtract)\
                     .then_inc(tmp_used, 1)

            def add_tiles(t0):
                for k in range(KD):
                    t = t0 + k
                    e.wait_ge(tmp_ready, t + 1)
                    e.tensor_tensor(out=x[:, k, :], in0=tmp[:, t % NTMP, :], in1=x[:, k, :], op=ALU.add).then_inc(tmp_used, 1)

            lo_of(0)
            lo_tiles(T_N0, range(KD))
            for g in range(U_MEM, U_IN):
                lo_of(g + 1)
            e.wait_ge(mkv_out, 64)
            for i in range(2):
                e.memset(ubuf[:, 3 * i:3 * i + 3, 0:PAST], 0.0).then_inc(u_ready, 1)
            with e.Fori(0, 3) as i:
                for j in range(2):
                    lo_of_at(U_IN + j + 1, i, 2)
                    e.wait_ge(tile_free[0], i * 2 + (M_IN // 2 + j + 1))
                    e.wait_ge(tile_free[1], i * 2 + (M_IN // 2 + j + 1))
                    e.tensor_tensor(out=ubuf[:, bass.ds(i * 2 + j, 1), PAST:PAST + T],
                                           in0=tmp[:, 2 + j:3 + j, :], in1=tmp[:, j:j + 1, :], op=ALU.mult).then_inc(u_ready, 1)
            lo_of(U_OUTA)

            def mem_pool(layer):
                if layer == 0:
                    e.wait_ge(tile_done, M_IN)
                else:
                    e.wait_ge(sb_pv, NH)
                e.memset(mem[layer].qz[:, :, :], 0.0).then_inc(mqz_zero, 1)

            mem_pool(0)
            lo_tiles(T_MIXA, MIX_A)
            for g in range(U_OUTA, U_GU):
                lo_of(g + 1)
            add_tiles(T_P0)
            lo_tiles(T_N1, range(KD))

            def lo_hidden(i, j):
                e.wait_ge(ga_hi, i * 2 + (j + 1))
                e.tensor_tensor(out=actl[:, bass.ds(i * 2 + j, 1), :], in0=tmp[:, 2 + j:3 + j, :],
                                       in1=acth[:, bass.ds(i * 2 + j, 1), :].bitcast(F32), op=ALU.subtract).then_inc(ga_lo, 1)

            with e.Fori(0, KF // 2) as i:
                for j in range(2):
                    lo_of_at(U_GU + j + 1, i, 2)
                    lo_hidden(i, j)
            with e.Fori(0, 2) as i:
                for j in range(6):
                    lo_of_at(U_DN + j + 1, i, 6)
            add_tiles(T_P1)
            lo_tiles(T_N2, range(KD))
            with e.Fori(0, 3) as i:
                for j in range(2):
                    lo_of_at(U_KV + j + 1, i, 2)
            lo_tiles(T_N3, range(KD))
            with e.Fori(0, 2) as i:
                for j in range(2):
                    lo_of_at(U_Q + j + 1, i, 2)
            e.wait_ge(kv_out, 64)
            e.memset(qd2[:, :, :, :], 0.0).then_inc(qd_zero, 1)

            def keep_past(buf, ready):
                for i in range(NT):
                    blk = buf[:, SEG_AT[i]:SEG_AT[i] + P]
                    e.affine_select(out=blk, in_=blk, compare_op=ALU.is_gt, fill=0.0, base=0,
                                    pattern=[[1, P]], channel_multiplier=-1).then_inc(ready, 1)

            for h in range(NH + 1):
                if h < NH:
                    e.wait_ge(sb_s, h + 1)
                    keep_past(sp[h % 2], sb_sp)
                if h >= 1:
                    e.wait_ge(sb_w, h)
                    keep_past(wt[(h - 1) % 2], sb_wm)
                    if h % 2 == 1 and h >= 3:
                        lo_tiles(T_MIXB + (h - 3) // 2, [(h - 3) // 2])
            lo_tiles(T_MIXB + FS - 1, [FS - 1])
            mem_pool(1)
            lo_tiles(T_MIXB + FS, [6, 7])
            for g in range(U_OUTB, U_END - 1):
                lo_of(g + 1)
            add_tiles(T_P2)

            e.wait_ge(tile_done, M_END)
            e.wait_ge(tmp_used, T_P2 + KD)
            e.iota(ioe[:, :, :], pattern=[[0, NT + 1], [1, E]], base=0, channel_multiplier=0).then_inc(io_int, 1)
            e.iota(ioi[:, :, :], pattern=[[1, MAXJOBS], [0, E]], base=0, channel_multiplier=0).then_inc(io_int, 1)
            e.memset(valid[:, :], 1.0).then_inc(io_int, 1)
            e.wait_ge(io_int, 3)
            e.tensor_copy(io8[:, :, :], ioe[:, :, :]).then_inc(io_ready, 1)
            e.tensor_copy(ioj[:, :, :], ioi[:, :, :]).then_inc(io_ready, 1)
            e.affine_select(out=valid[:, NT:NT + 1], in_=valid[:, NT:NT + 1], compare_op=ALU.is_ge, fill=0.0,
                            base=B - 1, pattern=[[0, 1]], channel_multiplier=-1).then_inc(io_ready, 1)
            e.wait_ge(slots_ready, 1)
            e.wait_ge(xs_zero, 64)
            for i in range(NT + 1):
                n = P if i < NT else B
                copied_out(e, TP_HT + 2 * i)
                copied_out(e, TP_HT + 2 * i + 1)
                for s in range(2):
                    e.indirect_dma_start(out=xs, out_offset=bass.IndirectOffsetOnAxis(ap=sloti[0:n, s, i:i + 1], axis=0),
                                         in_=htok[0:n, i, :], in_offset=None).then_inc(xs_in, 16)
            nj = e.value_load(jobi[0:1, MAXJOBS:MAXJOBS + 1], min_val=E, max_val=MAXJOBS)
            e.sem_inc(ea_lo, 1)
            with e.Fori(0, nj) as j:
                for m in range(KE):
                    e.wait_ge(ea_hi, j * KE + (m + 1))
                    e.tensor_tensor(out=eal[:, m, :], in0=eat[:, m % 2, :],
                                           in1=eah[:, m, :].bitcast(F32), op=ALU.subtract)\
                     .then_inc(ea_lo, 1)
            e.wait_ge(ys_ready, 1)
            for i in range(NT + 1):
                n = P if i < NT else B
                if i >= 2:
                    e.wait_ge(f_2, i - 1)
                for s in range(2):
                    e.indirect_dma_start(out=yr[0:n, i % 2, s, :], out_offset=None, in_=ys,
                                         in_offset=bass.IndirectOffsetOnAxis(ap=sloti[0:n, s, i:i + 1], axis=0))\
                     .then_inc(yr_in[i % 2], 16)

        @block.scalar
        def _(e):
            def hi_of(g):
                s = g % 2
                e.wait_ge(w_in[s], 32 * (g // 2 + 1))
                if g >= 2:
                    e.wait_ge(w_used, g - 1)
                e.activation(whi[:, s, :], raw[:, s, :], ACT.Copy).then_inc(w_hi, 1)

            def hi_of_at(c, i, n):
                s = c % 2
                e.wait_ge(w_in[s], i * (16 * n) + 32 * (c // 2 + 1))
                e.wait_ge(w_used, i * n + (c - 1))
                e.activation(whi[:, s, :], raw[:, s, :], ACT.Copy).then_inc(w_hi, 1)

            def hi_tile(t, k):
                e.wait_ge(tmp_ready, t + 1)
                e.activation(hh[:, k, :], tmp[:, t % NTMP, :], ACT.Copy).then_inc(hi_ready, 1)

            def square(q, src):
                if q >= 2:
                    e.wait_ge(sq_used, q - 1)
                e.activation(sq[:, q % 2, :] if src is not None else halves(sq[:, q % 2, :]),
                             src if src is not None else zero[:, :].unsqueeze(1).to_broadcast([P, 2, HALF]),
                             ACT.Square).then_inc(sq_ready, 1)

            def root(n):
                e.wait_ge(stat_done, n + 1)
                e.activation(halves(rstd[:, :]), ps[:, 4:6, 0:HALF], ACT.Sqrt, scale=1.0 / D, bias=eps[:, :])\
                 .then_inc(root_ready, 1)

            e.wait_ge(const_ready, 7)
            nfill = SLOTS * D // P // 256
            xsz = xs.rearrange("s d -> (s d)").rearrange("(p a n) -> p a n", p=P, n=256)
            for i in range(4):
                lo, hi = nfill * i // 4, nfill * (i + 1) // 4
                e.dma_start(xsz[:, lo:hi, :], zero[:, 0:256].unsqueeze(1).to_broadcast([P, hi - lo, 256]))\
                 .then_inc(xs_zero, 16)
            nfill = (MAXJOBS + 1 - E) * C * D // P // 256
            ysz = ys[(E + 1) * C:SLOTS, :].rearrange("s d -> (s d)").rearrange("(p a n) -> p a n", p=P, n=256)
            e.dma_start(ysz, zero[:, 0:256].unsqueeze(1).to_broadcast([P, nfill, 256])).then_inc(ys_zero, 16)
            e.wait_ge(mem_in, 16)
            for i in range(MT):
                e.activation(mT[:, 4 * i:4 * i + 4, :].rearrange("p k n -> p (k n)"), memtok[:, i, :], ACT.Square,
                             accum_out=ms[:, i:i + 1]).then_inc(mem_ss, 1)
            e.wait_ge(mem_ss, 2)
            e.activation(ms[:, 2:4], ms[:, 0:2], ACT.Sqrt, scale=1.0 / D, bias=eps[:, :]).then_inc(mem_root, 1)
            copied_out(e, TP_X + KD - 1)
            copied_out(e, TP_X + KD)
            for k in range(KD):
                square(S_X0 + k, x[:, k, :])
            root(0)
            for layer in range(2):
                for k in range(KD):
                    copied_out(e, TP_MEM + k // 2)
                    e.activation(hmh[:, layer, k, :], mT[:, k, :], ACT.Copy, scale=gain(G_MEM + 8 * layer, k))\
                     .then_inc(hm_hi, 1)
            hi_of(0)
            for k in range(KD):
                hi_tile(T_N0 + k, k)
            for g in range(U_MEM, U_IN):
                hi_of(g + 1)
            with e.Fori(0, 3) as i:
                for j in range(2):
                    hi_of_at(U_IN + j + 1, i, 2)
                    e.wait_ge(u_ready, i * 2 + (j + 1))
                    e.wait_ge(tile_done, i * 4 + (M_IN + 2 * j + 1))
                    e.activation(halves(tmp[:, 2 + j, :]), pair(0), ACT.Copy).then_inc(tile_free[0], 1)
                    e.wait_ge(tile_done, i * 4 + (M_IN + 2 * j + 2))
                    e.activation(halves(tmp[:, j, :]), pair(1), ACT.Sigmoid).then_inc(tile_free[1], 1)
            hi_of(U_OUTA)
            for t in range(FM):
                e.wait_ge(tile_done, M_QM + t + 1)
                e.activation(halves(qmA[:, t, :]), pair(t), ACT.Copy, scale=HD ** -0.5).then_inc(tile_free[t], 1)
            for n, (lo, hi) in enumerate(((0, 4), (4, 6))):
                f = TP_UT + n
                e.wait_ge(tp_done, f + 1)
                e.activation(utail[0:PAST + B, lo * P:hi * P], ps[0:PAST + B, 6 + f % 2, 0:(hi - lo) * P], ACT.Copy)\
                 .then_inc(tp_free[f % 2], 1)

            def mem_act(layer):
                m = mem[layer]
                f = (TP_MA, TP_MB)[layer]
                e.wait_ge(tp_done, f + 1)
                e.activation(m.kT[:, :, :].rearrange("p f n -> p (f n)"), ps[:, 6 + f % 2, :], ACT.Copy)\
                 .then_inc(tp_free[f % 2], 1)
                for b in range(B):
                    e.wait_ge(tp_done, f + b + 2)
                    e.activation(m.cT[:, b, :, :].rearrange("p f n -> p (f n)"), ps[:, 6 + (f + b + 1) % 2, :], ACT.Copy)\
                     .then_inc(tp_free[(f + b + 1) % 2], 1)
                e.wait_ge(md_max, layer + 1)
                e.activation(m.pd[:, :], ps[0:32, 4, 0:NMEM], ACT.Exp, bias=stm[0:32, 0, 0:1],
                             accum_out=sts[0:32, 0, 0:1]).then_inc(md_e, 1)
                for h in range(MH + 1):
                    if h < MH:
                        s = h % 2
                        e.wait_ge(mp_max, MH * layer + h + 1)
                        for i in range(NT):
                            ins = e.activation(m.p[:, s, i, :], ps[:, 2 * s + i // 2, (i % 2) * NMEM:(i % 2 + 1) * NMEM],
                                               ACT.Exp, bias=stm[:, s, i:i + 1], accum_out=sts[:, s, i:i + 1])
                            ins.then_inc(mp_e, 1)
                    if h >= 1:
                        e.wait_ge(mp_t, MH * layer + h)
                        e.wait_ge(mp_o, MH * layer + h - 1)
                        e.activation(m.pT[:, 0, :], ps[:, 4, :], ACT.Copy).then_inc(mp_pT, 1)

            mem_act(0)
            hi_tile(T_MIXA, 6)
            hi_tile(T_MIXA + 1, 7)
            for k in range(FS):
                e.wait_ge(ln_xc, k + 1)
                if k >= 2:
                    e.wait_ge(ln_used, k - 1)
                e.activation(sq[:, k % 2, :], cT[:, k, :], ACT.Square).then_inc(ln_sq, 1)
            e.wait_ge(ln_var, 1)
            e.activation(halves(rstd[:, :]), ps[:, 4:6, 0:HALF], ACT.Sqrt, scale=1.0 / (FS * P), bias=eps[:, :])\
             .then_inc(ln_root, 1)
            for k in range(FS):
                t = T_MIXA + 2 + k
                e.wait_ge(ln_y, k + 1)
                e.wait_ge(tmp_used, t - NTMP + 1)
                e.activation(tmp[:, t % NTMP, :], cT[:, k, :], ACT.Silu, scale=gT[:, G_LNG + k:G_LNG + k + 1],
                             bias=gT[:, G_LNB + k:G_LNB + k + 1]).then_inc(tmp_ready, 1)
                hi_tile(t, k)

            def y_squares(q0, m0, y, ks):
                for k in ks:
                    e.wait_ge(tile_free[k % 2], (m0 + k) // 2 + 1)
                    square(q0 + 2 + k, y[:, k, :])

            def x_squares(q0, t0):
                for k in range(KD):
                    e.wait_ge(tmp_used, t0 + k + 1)
                    square(q0 + k, x[:, k, :])

            square(S_YA, None)
            square(S_YA + 1, None)
            for g in range(U_OUTA, U_GU):
                hi_of(g + 1)
                y_squares(S_YA, M_OUTA, y_mix, (2 * (g - U_OUTA), 2 * (g - U_OUTA) + 1))
            root(1)
            x_squares(S_XA, T_P0)
            root(2)
            for k in range(KD):
                hi_tile(T_N1 + k, k)

            def hidden(i, j, first):
                if not first:
                    e.wait_ge(tile_free[1], i * 2 + (M_GU // 2 + j - 1))
                e.wait_ge(tile_done, i * 4 + (M_GU + 2 * j + 1))
                e.activation(halves(tmp[:, j, :]), pair(0), ACT.Silu).then_inc(tile_free[0], 1)
                e.wait_ge(tile_free[1], i * 2 + (M_GU // 2 + j + 1))
                e.activation(acth[:, bass.ds(i * 2 + j, 1), :], tmp[:, 2 + j:3 + j, :], ACT.Copy).then_inc(ga_hi, 1)

            for j in range(2):
                hi_of(U_GU + j + 1)
                hidden(0, j, True)
            with e.Fori(1, KF // 2) as i:
                for j in range(2):
                    hi_of_at(U_GU + j + 1, i, 2)
                    hidden(i, j, False)
            square(S_YF, None)
            square(S_YF + 1, None)
            with e.Fori(0, 2) as i:
                for j in range(6):
                    hi_of_at(U_DN + j + 1, i, 6)
                    if j % 3 == 2:
                        for t in range(2):
                            k = 2 * (j // 3) + t
                            e.wait_ge(tile_free[t], i * 2 + ((M_DN + k) // 2 + 1))
                            e.wait_ge(sq_used, i * 4 + (S_YF + 2 + k - 1))
                            e.activation(sq[:, k % 2:k % 2 + 1, :], y_dn[:, bass.ds(i * 4 + k, 1), :], ACT.Square)\
                             .then_inc(sq_ready, 1)
            root(3)
            x_squares(S_XF, T_P1)
            root(4)
            for k in range(KD):
                hi_tile(T_N2 + k, k)
            with e.Fori(0, 3) as i:
                for j in range(2):
                    hi_of_at(U_KV + j + 1, i, 2)
            for n in range(20):
                w, i, half = n // 10, (n % 10) // 2, n % 2
                f = TP_KV + n
                rows_ = P if i < NT else B
                c0, c1 = (0, 4 * P) if half == 0 else (4 * P, FS * P)
                dst = (vtok, ktok)[w][:, i, c0:c1] if i < NT else kvdec[0:B, w, c0:c1]
                e.wait_ge(tp_done, f + 1)
                e.activation(dst, ps[0:rows_, 6 + f % 2, 0:c1 - c0], ACT.Copy).then_inc(tp_free[f % 2], 1)
                if n == 4:
                    e.wait_ge(tile_done, M_Q)
                    for k in range(KD):
                        hi_tile(T_N3 + k, k)
            copied_out(e, TP_KV + 18)
            copied_out(e, TP_KV + 19)
            e.dma_start(v_prompt[0].rearrange("(i p) h d -> p i (h d)", p=P), vtok[:, :, :]).then_inc(kv_out, 16)
            e.dma_start(k_prompt[0].rearrange("(i p) h d -> p i (h d)", p=P), ktok[:, :, :]).then_inc(kv_out, 16)
            e.dma_start(v_sample.rearrange("b s h d -> b (s h d)"), kvdec[0:B, 0, :]).then_inc(kv_out, 16)
            e.dma_start(k_sample.rearrange("b s h d -> b (s h d)"), kvdec[0:B, 1, :]).then_inc(kv_out, 16)
            with e.Fori(0, 2) as i:
                for j in range(2):
                    hi_of_at(U_Q + j + 1, i, 2)
            e.wait_ge(kv_out, 64)
            for b in range(B):
                for c in range(3):
                    f = TP_PG + 3 * b + c
                    e.wait_ge(tp_done, f + 1)
                    if b >= 2:
                        e.wait_ge(pg_qk, b - 1)
                    e.activation(pgT[:, b % 2, 2 * c:2 * c + 2, :].rearrange("p f n -> p (f n)"), ps[:, 6 + f % 2, :],
                                 ACT.Copy).then_inc(tp_free[f % 2], 1)
            e.wait_ge(sd_zc, 1)
            e.activation(zd[:, 1, :], zd[:, 1, :], ACT.Exp).then_inc(sd_e, 1)
            e.wait_ge(sd_e, 1)
            e.activation(zd[:, 1, :], zd[:, 1, :], ACT.Ln, bias=ones[:, 0:1]).then_inc(sd_l, 1)
            e.wait_ge(sd_x, 1)
            e.activation(zd[:, 3, :], zd[:, 0, :], ACT.Exp).then_inc(sd_w, 1)
            for h in range(NH + 1):
                if h < NH:
                    c = zc[h % 2]
                    e.wait_ge(sb_zc, h + 1)
                    e.activation(c[:, :], c[:, :], ACT.Exp).then_inc(sb_e, 1)
                    e.wait_ge(sb_e, h + 1)
                    e.activation(c[:, :], c[:, :], ACT.Ln, bias=ones[:, 0:1]).then_inc(sb_l, 1)
                if h >= 1:
                    e.wait_ge(sb_c, h)
                    if h >= 3:
                        e.wait_ge(sb_pv, h - 2)
                    g = h - 1
                    e.activation(wt[g % 2][:, :], flat[:, 1536 * (g % 2):1536 * (g % 2) + SEG], ACT.Exp,
                                 bias=bias[:, 0, g:g + 1]).then_inc(sb_w, 1)
                    if h % 2 == 1 and h >= 3:
                        hi_tile(T_MIXB + (h - 3) // 2, (h - 3) // 2)
            hi_tile(T_MIXB + FS - 1, FS - 1)
            mem_act(1)
            hi_tile(T_MIXB + FS, 6)
            hi_tile(T_MIXB + FS + 1, 7)
            square(S_YB, None)
            square(S_YB + 1, None)
            for g in range(U_OUTB, U_END):
                if g + 1 < U_END:
                    hi_of(g + 1)
                y_squares(S_YB, M_OUTB, y_mix, (2 * (g - U_OUTB), 2 * (g - U_OUTB) + 1))
            root(5)
            x_squares(S_XB, T_P2)
            root(6)

            e.wait_ge(rr_m1, 1)
            e.activation(rt[:, 6, :, :], rt[:, 2, :, :], ACT.Exp).then_inc(rr_exp, 1)
            for n in range(20):
                f = TP_HT + n
                dst, i = ((htok, xtk)[n // 10], (n % 10) // 2)
                rows_ = P if i < NT else B
                e.wait_ge(tp_done, f + 1)
                e.activation(dst[0:rows_, i, 512 * (n % 2):512 * (n % 2) + 512], ps[0:rows_, 6 + f % 2, :], ACT.Copy)\
                 .then_inc(tp_free[f % 2], 1)

            e.wait_ge(slots_ready, 1)
            nj = e.value_load(jobi[0:1, MAXJOBS:MAXJOBS + 1], min_val=E, max_val=MAXJOBS)

            def expert_hi(j, u):
                s = u % SPLIT
                n = 2048 if u < KE else DN_CUTS[u - KE] * D
                e.wait_ge(ew_in[u % RAW], j * (32 * PER_JOB // RAW) + 32 * (u // RAW + 1))
                e.wait_ge(ew_used, j * PER_JOB + (u + 1))
                e.activation(ewh[:, s, 0:n], eraw[:, u % RAW, 0:n], ACT.Copy).then_inc(ew_hi, 1)

            def rows_hi(c, filled):
                e.wait_ge(er_done, filled)
                e.activation(ejh[:, 2 * c:2 * c + 2, :], ps[:, 6 + c % 2, 0:2 * C].rearrange("p (k n) -> p k n", k=2),
                             ACT.Copy).then_inc(ej_hi, 1)

            for c in range(4):
                rows_hi(c, c + 1)
            with e.Fori(0, nj) as j:
                expert_hi(j, 0)
                expert_hi(j, 1)
                for u in range(PER_JOB):
                    if u + 2 < PER_JOB:
                        expert_hi(j, u + 2)
                    if u < KE:
                        if u == 0:
                            e.wait_ge(ed_done, j + 1)
                        e.wait_ge(eg_done, j * KE + (u + 1))
                        e.wait_ge(ea_tmp, j * KE + (max(u - 1, 0) + 1))
                        e.activation(esg[:, u % 2, :], ps[:, u % 2, 0:C], ACT.Silu).then_inc(es_ready, 1)
                        e.wait_ge(ea_tmp, j * KE + (u + 2))
                        e.activation(eah[:, u, :], eat[:, u % 2, :], ACT.Copy).then_inc(ea_hi, 1)
                    if u == KE - 1:
                        for c in range(4):
                            rows_hi(c, j * 8 + (8 + c + 1))
            for i in range(NT + 1):
                n = P if i < NT else B
                e.wait_ge(f_2, i + 1)
                e.activation(fs[0:n, i % 2, :], fo[0:n, i % 2, :], ACT.Square, accum_out=frs[0:n, i, 0:1]).then_inc(f_ss, 1)
                e.wait_ge(f_ss, i + 1)
                e.activation(frs[0:n, i, 1:2], frs[0:n, i, 0:1], ACT.Sqrt, scale=1.0 / D, bias=eps[0:n, :])\
                 .then_inc(f_root, 1)

        @block.vector
        def _(e):
            def copy_out(f, dst, src):
                e.wait_ge(tp_done, f + 1)
                e.tensor_copy(dst, src).then_inc(tp_free[f % 2], 1)

            def bank(f):
                return 6 + f % 2

            def inverse(n):
                e.wait_ge(root_ready, n + 1)
                e.reciprocal(rstd[:, :], rstd[:, :]).then_inc(rstd_ready, 1)
                e.wait_ge(rstd_ready, n + 1)

            def norm_tiles(t0, src, off):
                for k in range(KD):
                    t = t0 + k
                    if t >= NTMP:
                        e.wait_ge(tmp_used, t - NTMP + 1)
                    e.scalar_tensor_tensor(out=tmp[:, t % NTMP, :], in0=src[:, k, :], scalar=gain(off, k), in1=rstd[:, :],
                                           op0=ALU.mult, op1=ALU.mult).then_inc(tmp_ready, 1)

            copy_out(TP_CTL, gT[:, :], ps[:, bank(TP_CTL), 0:G_ROWS])
            copy_out(TP_CTL + 1, cwT[:, :, :].rearrange("p j f -> p (j f)"), ps[:, bank(TP_CTL + 1), 0:CW * FS])
            e.wait_ge(mem_root, 1)
            e.reciprocal(ms[:, 2:4], ms[:, 2:4]).then_inc(mem_inv, 1)
            e.wait_ge(mem_inv, 1)
            for i in range(MT):
                e.tensor_scalar(memtok[:, i, :], memtok[:, i, :], ms[:, 2 + i:3 + i], None, ALU.mult).then_inc(mem_sc, 1)
            for k in range(KD):
                copy_out(TP_X + k, x[:, k, 0:TP], ps[:, bank(TP_X + k), :])
            f = TP_X + KD
            copy_out(f, x[:, :, TP:T], ps[:, bank(f), 0:KD * B].rearrange("p (k b) -> p k b", k=KD))
            for c in range(4):
                f = TP_MEM + c
                copy_out(f, mT[:, 2 * c:2 * c + 2, :], ps[:, bank(f), :].rearrange("p (k m) -> p k m", k=2))
            for layer in range(2):
                for k in range(KD):
                    e.wait_ge(hm_hi, KD * layer + k + 1)
                    e.scalar_tensor_tensor(out=hml[:, layer, k, :], in0=mT[:, k, :], scalar=gain(G_MEM + 8 * layer, k),
                                           in1=hmh[:, layer, k, :].bitcast(F32), op0=ALU.mult, op1=ALU.subtract)\
                     .then_inc(hm_lo, 1)
            inverse(0)
            norm_tiles(T_N0, x, G_PRE_MIX)
            for n in range(8):
                e.wait_ge(tile_done, M_MEM + n + 1)
                e.tensor_copy(mkv[:, n // 4, (n // 2) % 2, n % 2, :], ps[:, 2 * (n % 2), 0:NMEM])\
                 .then_inc(tile_free[n % 2], 1)
            for c in range(3):
                f = TP_ST + c
                for h in range(2):
                    e.wait_ge(tp_done, f + 1)
                    ins = e.tensor_copy(udec[:, 2 * c + h, :, 0:PAST],
                                        ps[:, bank(f), 240 * h:240 * h + 240].rearrange("p (b r) -> p b r", b=B))
                    if h == 0:
                        ins.then_inc(cd, 1)
                ins.then_inc(tp_free[f % 2], 1)

            def conv_pair(c):
                n0 = 62 * c
                e.wait_ge(u_ready, 2 + 2 * c + 2)
                for t in range(2):
                    f = 2 * c + t
                    e.tensor_scalar(cT[:, f, 0:TP], ubuf[:, f, 0:TP], cwT[:, 0, f:f + 1], gT[:, G_CB + f:G_CB + f + 1],
                                    ALU.mult, ALU.add).then_inc(cv, 1)
                with e.Fori(1, CW) as j:
                    for t in range(2):
                        f = 2 * c + t
                        e.wait_ge(cv, j * 2 + (n0 + t - 1))
                        e.scalar_tensor_tensor(out=cT[:, f, 0:TP], in0=ubuf[:, f, bass.ds(j, TP)],
                                               scalar=cwf[:, bass.ds(j * FS + f, 1)], in1=cT[:, f, 0:TP],
                                               op0=ALU.mult, op1=ALU.add).then_inc(cv, 1)

            def conv_decode():
                for f in range(FS):
                    e.tensor_copy(udec[:, f, :, PAST:CW], ubuf[:, f, PAST + TP:PAST + T].unsqueeze(2)).then_inc(ud_new, 1)
                for f in range(FS):
                    e.wait_ge(ud_new, FS)
                    if f == 0:
                        copied_out(e, TP_ST + 2)
                    if f >= 1:
                        e.wait_ge(cd, 3 + 2 * f)
                    e.tensor_tensor(ctmp[:, :, :], udec[:, f, :, :],
                                    cwT[:, :, f].unsqueeze(1).to_broadcast([P, B, CW]), ALU.mult).then_inc(cd, 1)
                    e.wait_ge(cd, 4 + 2 * f)
                    e.tensor_reduce(cT[:, f, TP:T], ctmp[:, :, :], AX, ALU.add).then_inc(cd, 1)
                e.wait_ge(cd, 3 + 2 * FS)
                for f in range(FS):
                    e.tensor_scalar(cT[:, f, TP:T], cT[:, f, TP:T], gT[:, G_CB + f:G_CB + f + 1], None, ALU.add)\
                     .then_inc(cd_sum, 1)

            def mem_dve(layer, q, t0):
                m = mem[layer]
                e.wait_ge(mqz_zero, layer + 1)
                e.wait_ge(tile_free[0], (M_OUTA if layer == 0 else M_OUTB) // 2)
                e.wait_ge(tile_free[1], (M_OUTA if layer == 0 else M_OUTB) // 2)
                qz = m.qz[:, :, :].rearrange("p a b -> p (a b)")
                for f in range(FM):
                    for h in range(2):
                        at0 = 34 * f + h
                        e.tensor_copy(qz[64 * h:64 * h + 64, at0:at0 + 68 * (B - 1) + 1:68],
                                      q[64 * h:64 * h + 64, f, TP:T]).then_inc(mqz_ready, 1)
                e.wait_ge(md_s, layer + 1)
                e.tensor_reduce(stm[0:32, 0, 0:1], ps[0:32, 4, 0:NMEM], AX, ALU.max, negate=True).then_inc(md_max, 1)
                e.wait_ge(md_e, layer + 1)
                e.reciprocal(sts[0:32, 0, 0:1], sts[0:32, 0, 0:1]).then_inc(md_inv, 1)
                e.wait_ge(md_inv, layer + 1)
                e.tensor_scalar(m.pd[:, :], m.pd[:, :], sts[0:32, 0, 0:1], None, ALU.mult).then_inc(md_p, 1)
                e.wait_ge(md_t, layer + 1)
                e.tensor_copy(m.pdT[:, :, :], ps[:, 5, 0:64].rearrange("p (m r) -> p m r", m=MT)).then_inc(md_pT, 1)
                e.wait_ge(md_o, layer + 1)
                o_ps = ps[:, 4, 0:2 * FM * B].rearrange("p (b f h) -> p h f b", b=B, f=FM)
                for h in range(2):
                    e.tensor_copy(od[64 * h:64 * h + 64, 0:FM, :], o_ps[64 * h:64 * h + 64, h, :, :]).then_inc(md_od, 1)
                for h in range(MH + 2):
                    if h < MH:
                        s = h % 2
                        e.wait_ge(mp_s, MH * layer + h + 1)
                        e.tensor_reduce(stm[:, s, :], flat[:, 1024 * s:1024 * s + 1024].rearrange("p (i n) -> p i n", i=NT),
                                        AX, ALU.max, negate=True).then_inc(mp_max, 1)
                    if 1 <= h <= MH:
                        g = h - 1
                        s = g % 2
                        e.wait_ge(mp_e, NT * (MH * layer + g + 1))
                        e.reciprocal(sts[:, s, :], sts[:, s, :]).then_inc(mp_inv, 1)
                        e.wait_ge(mp_inv, MH * layer + g + 1)
                        for i in range(NT):
                            e.tensor_scalar(m.p[:, s, i, :], m.p[:, s, i, :], sts[:, s, i:i + 1], None, ALU.mult)\
                             .then_inc(mp_p, 1)
                        e.wait_ge(mp_t, MH * layer + g + 1)
                        e.wait_ge(mp_o, MH * layer + g)
                        e.tensor_copy(m.pT[:, 1, :], ps[:, 5, :]).then_inc(mp_pT, 1)
                    if h >= 2 and h % 2 == 1:
                        f = (h - 3) // 2
                        t = t0 + f
                        e.wait_ge(mp_o, MH * layer + h - 1)
                        e.wait_ge(md_od, 2 * layer + 2)
                        e.wait_ge(tmp_used, t - NTMP + 1)
                        e.tensor_copy(tmp[:, t % NTMP, TP:T], od[:, f, :]).then_inc(mp_out, 1)
                        e.wait_ge(mp_out, FM * layer + f + 1)
                        e.tensor_copy(tmp[:, t % NTMP, 0:TP], ps[:, 6 + f, :]).then_inc(tmp_ready, 1)

            cwf = cwT[:, :, :].rearrange("p j f -> p (j f)")
            conv_pair(0)
            conv_pair(1)
            mem_dve(0, qmA, T_MIXA)
            conv_pair(2)
            conv_decode()
            e.wait_ge(ln_sum, 1)
            e.tensor_scalar(halves(mean[:, :]), ps[:, 4:6, 0:HALF], 1.0 / (FS * P), None, ALU.mult).then_inc(ln_mean, 1)
            e.wait_ge(ln_mean, 1)
            for k in range(FS):
                e.tensor_tensor(cT[:, k, :], cT[:, k, :], mean[:, :], ALU.subtract).then_inc(ln_xc, 1)
            e.wait_ge(ln_root, 1)
            e.reciprocal(rstd[:, :], rstd[:, :]).then_inc(ln_rstd, 1)
            e.wait_ge(ln_rstd, 1)
            e.wait_ge(ln_sq, FS)
            for k in range(FS):
                e.tensor_tensor(cT[:, k, :], cT[:, k, :], rstd[:, :], ALU.mult).then_inc(ln_y, 1)

            def out_tiles(m0, y, n=KD):
                for k in range(n):
                    e.wait_ge(tile_done, m0 + k + 1)
                    e.tensor_copy(halves(y[:, k, :]), pair(k % 2)).then_inc(tile_free[k % 2], 1)

            out_tiles(M_OUTA, y_mix)
            inverse(1)
            norm_tiles(T_P0, y_mix, G_POST_MIX)
            inverse(2)
            norm_tiles(T_N1, x, G_PRE_FFN)

            def hidden(i, j, first):
                if not first:
                    e.wait_ge(ga_lo, i * 2 + (j - 1))
                e.wait_ge(tile_free[0], i * 2 + (M_GU // 2 + j + 1))
                e.wait_ge(tile_done, i * 4 + (M_GU + 2 * j + 2))
                e.tensor_tensor(halves(tmp[:, 2 + j, :]), pair(1), halves(tmp[:, j, :]), ALU.mult).then_inc(tile_free[1], 1)

            for j in range(2):
                hidden(0, j, True)
            with e.Fori(1, KF // 2) as i:
                for j in range(2):
                    hidden(i, j, False)
            with e.Fori(0, 2) as i:
                for k in range(4):
                    e.wait_ge(tile_done, i * 4 + (M_DN + k + 1))
                    e.tensor_copy(y_dn[:, bass.ds(i * 4 + k, 1), :].rearrange("p o (h n) -> p (o h) n", h=2), pair(k % 2))\
                     .then_inc(tile_free[k % 2], 1)
            inverse(3)
            norm_tiles(T_P1, y_dn, G_POST_FFN)
            inverse(4)
            norm_tiles(T_N2, x, G_KV)
            for m in range(2 * FS):
                e.wait_ge(tile_done, M_KV + m + 1)
                e.tensor_copy(halves((kT, vT)[m // FS][:, m % FS, :]), pair(m % 2)).then_inc(tile_free[m % 2], 1)
            norm_tiles(T_N3, x, G_PRE_MIX + 8)
            for m in range(KD):
                e.wait_ge(tile_done, M_Q + m + 1)
                e.tensor_scalar(halves(qT[:, m, :]), pair(m % 2), HD ** -0.5, None, ALU.mult)\
                 .then_inc(tile_free[m % 2], 1)

            e.wait_ge(qd_zero, 1)
            e.wait_ge(tile_free[0], M_OUTB // 2)
            e.wait_ge(tile_free[1], M_OUTB // 2)
            for h in range(2):
                e.tensor_copy(qd2[64 * h:64 * h + 64, :, :, h],
                              qT[64 * h:64 * h + 64, 0:FS, TP:T].rearrange("p f b -> p b f")).then_inc(qd_ready, 1)
            bias2 = bias[:, :, :].rearrange("p b h -> p (b h)").unsqueeze(1).to_broadcast([P, NPG, B * NH])

            def pages(ap):
                return ap.rearrange("p (g r) -> p g r", g=NPG)

            e.wait_ge(small_in, 64)
            e.wait_ge(sd_z, 1)
            e.tensor_tensor(pages(zd[:, 0, :]), pages(ps[:, 0, 0:192]), bias2, ALU.add).then_inc(sd_zb, 1)
            e.wait_ge(sd_zb, 1)
            e.tensor_scalar(zd[:, 1, :], zd[:, 0, :], CLAMP, None, ALU.min).then_inc(sd_zc, 1)
            e.wait_ge(sd_l, 1)
            e.tensor_tensor(zd[:, 2, :], zd[:, 0, :], zd[:, 1, :], ALU.max).then_inc(sd_sp, 1)
            e.wait_ge(sd_c, 1)
            e.wait_ge(sd_sp, 1)
            e.tensor_tensor(pages(zd[:, 0, :]), pages(ps[:, 0, 0:192]), bias2, ALU.add).then_inc(sd_x, 1)
            e.wait_ge(sd_o, 1)
            o_ps = ps[:, 1, 0:2 * FS * B].rearrange("p (b f h) -> p h f b", b=B, f=FS)
            for h in range(2):
                e.tensor_copy(od[64 * h:64 * h + 64, :, :], o_ps[64 * h:64 * h + 64, h, :, :]).then_inc(sd_od, 1)
            for h in range(NH + 2):
                if h < NH:
                    z = flat[:, 1536 * (h % 2):1536 * (h % 2) + SEG]
                    e.wait_ge(sb_z, h + 1)
                    if h >= 2:
                        e.wait_ge(sb_s, h - 1)
                    e.tensor_scalar(zc[h % 2][:, :], z, bias[:, 0, h:h + 1], CLAMP, ALU.add, ALU.min).then_inc(sb_zc, 1)
                    e.wait_ge(sb_l, h + 1)
                    if h >= 2:
                        e.wait_ge(sb_c, h - 1)
                    e.scalar_tensor_tensor(out=sp[h % 2][:, :], in0=z, scalar=bias[:, 0, h:h + 1], in1=zc[h % 2][:, :],
                                           op0=ALU.add, op1=ALU.max).then_inc(sb_s, 1)
                if h % 2 == 1 and h >= 3:
                    f = (h - 3) // 2
                    t = T_MIXB + f
                    e.wait_ge(sb_pv, h - 1)
                    e.wait_ge(sd_od, 2)
                    e.wait_ge(tmp_used, t - NTMP + 1)
                    e.tensor_copy(tmp[:, t % NTMP, TP:T], od[:, f, :]).then_inc(sb_out, 1)
                    e.wait_ge(sb_out, f + 1)
                    e.tensor_copy(tmp[:, t % NTMP, 0:TP], ps[:, 6 + f % 2, :]).then_inc(tmp_ready, 1)
            mem_dve(1, qT[:, FS:KD, :], T_MIXB + FS)
            out_tiles(M_OUTB, y_mix)
            inverse(5)
            norm_tiles(T_P2, y_mix, G_POST_MIX + 8)
            inverse(6)
            for k in range(KD):
                e.scalar_tensor_tensor(out=hf[:, k, :], in0=x[:, k, :], scalar=gain(G_PRE_FFN + 8, k), in1=rstd[:, :],
                                       op0=ALU.mult, op1=ALU.mult).then_inc(hf_ready, 1)

            lg, eq, dl, oh1, oh2, msk, pr, sl = (rt[:, n, :, :] for n in range(8))
            m1, i1, m2, i2, zs, p1, p2, pp = (r5[:, n, :] for n in range(8))
            links = [0]

            def link(ins):
                links[0] += 1
                ins.then_inc(rr, 1)
                e.wait_ge(rr, links[0])

            def over_e(v):
                return v.unsqueeze(2).to_broadcast([P, NT + 1, E])

            e.wait_ge(io_ready, 3)
            link(e.memset(lg, 0.0))
            e.wait_ge(lg_done, 1)
            link(e.tensor_tensor(lg[:, 0:NT, :], ps[:, 4, 0:NT * E].rearrange("p (i e) -> p i e", e=E),
                                 br[:, :].unsqueeze(1).to_broadcast([P, NT, E]), ALU.add))
            link(e.tensor_tensor(lg[0:B, NT, :], ps[0:B, 4, NT * E:(NT + 1) * E], br[0:B, :], ALU.add))

            def first_max(vals, mx, idx, onehot):
                link(e.tensor_reduce(mx, vals, AX, ALU.max))
                link(e.tensor_tensor(eq, vals, over_e(mx), ALU.is_ge))
                link(e.scalar_tensor_tensor(out=eq, in0=eq, scalar=-float(E), in1=io8[:, :, :], op0=ALU.mult, op1=ALU.add))
                link(e.tensor_reduce(idx, eq, AX, ALU.min))
                link(e.tensor_scalar(idx, idx, float(E), None, ALU.add))
                link(e.tensor_tensor(onehot, io8[:, :, :], over_e(idx), ALU.is_equal))

            first_max(lg, m1, i1, oh1)
            e.tensor_tensor(dl, lg, over_e(m1), ALU.subtract).then_inc(rr_m1, 1)
            link(e.scalar_tensor_tensor(out=sl, in0=oh1, scalar=-1e30, in1=lg, op0=ALU.mult, op1=ALU.add))
            first_max(sl, m2, i2, oh2)
            link(e.tensor_tensor(msk, oh1, oh2, ALU.add))
            e.tensor_tensor(msk, msk, over_e(valid[:, :]), ALU.mult).then_inc(mask_ready, 1)
            e.wait_ge(rr_exp, 1)
            link(e.tensor_reduce(zs, pr, AX, ALU.add))
            link(e.reciprocal(zs, zs))
            link(e.tensor_tensor(pr, pr, over_e(zs), ALU.mult))
            link(e.tensor_tensor(dl, pr, oh1, ALU.mult))
            link(e.tensor_reduce(p1, dl, AX, ALU.add))
            link(e.tensor_tensor(dl, pr, oh2, ALU.mult))
            link(e.tensor_reduce(p2, dl, AX, ALU.add))
            link(e.tensor_tensor(pp, p1, p2, ALU.add))
            link(e.reciprocal(pp, pp))
            link(e.tensor_tensor(gate[:, 0, :], p1, pp, ALU.mult))
            link(e.tensor_tensor(gate[:, 1, :], p2, pp, ALU.mult))
            cnt, nb, je, jb = (r8[:, n, :] for n in range(4))
            e.wait_ge(cnt_done, 1)
            link(e.tensor_copy(cnt, ps[:, 5, (NT + 1) * E:(NT + 2) * E]))
            link(e.tensor_scalar(nb, cnt, float(C), 1.0, ALU.is_gt, ALU.add))
            for n in range(2, (T + C - 1) // C):
                link(e.scalar_tensor_tensor(out=nb, in0=cnt, scalar=float(n * C), in1=nb, op0=ALU.is_gt, op1=ALU.add))
            link(e.tensor_copy(je, nb))
            for n in range(1, E):
                link(e.tensor_tensor(je[:, n:n + 1], je[:, n - 1:n], nb[:, n:n + 1], ALU.add))
            link(e.tensor_tensor(jb, je, nb, ALU.subtract))
            link(e.tensor_scalar(jb, jb, 1.0, float(C), ALU.add, ALU.mult))
            link(e.tensor_tensor(sl, ps[:, 5, 0:(NT + 1) * E].rearrange("p (i e) -> p i e", e=E),
                                 jb.unsqueeze(1).to_broadcast([P, NT + 1, E]), ALU.add))
            for s, oh in enumerate((oh1, oh2)):
                link(e.tensor_tensor(dl, sl, oh, ALU.mult))
                link(e.tensor_reduce(m1 if s == 0 else m2, dl, AX, ALU.add))
                link(e.tensor_copy(sloti[:, s, :], m1 if s == 0 else m2))
            link(e.tensor_tensor(jcmp[:, :, :], ioj[:, :, :], je.unsqueeze(1).to_broadcast([P, MAXJOBS, E]), ALU.is_ge))
            link(e.tensor_reduce(jobf[:, 0:MAXJOBS], jcmp[:, :, :], AX, ALU.add))
            link(e.tensor_scalar(jobf[:, 0:MAXJOBS], jobf[:, 0:MAXJOBS], float(E - 1), None, ALU.min))
            link(e.tensor_copy(jobf[:, MAXJOBS:MAXJOBS + 1], je[:, E - 1:E]))
            e.tensor_copy(jobi[:, :], jobf[:, :]).then_inc(slots_ready, 1)
            e.wait_ge(slots_ready, 1)

            nj = e.value_load(jobi[0:1, MAXJOBS:MAXJOBS + 1], min_val=E, max_val=MAXJOBS)
            e.wait_ge(tile_done, M_END)
            e.sem_inc(ew_lo, RAW)
            e.sem_inc(ea_tmp, 1)

            def expert_lo(j, u):
                n = 2048 if u < KE else DN_CUTS[u - KE] * D
                s = u % SPLIT
                e.wait_ge(ew_hi, j * PER_JOB + (u + 1))
                e.tensor_tensor(ewl[:, s, 0:n], eraw[:, u % RAW, 0:n], ewh[:, s, 0:n].bitcast(F32), ALU.subtract)\
                 .then_inc(ew_lo, 1)

            def rows_lo(c, his):
                e.wait_ge(ej_hi, his)
                e.tensor_tensor(ejl[:, 2 * c:2 * c + 2, :], ps[:, 6 + c % 2, 0:2 * C].rearrange("p (k n) -> p k n", k=2),
                                ejh[:, 2 * c:2 * c + 2, :].bitcast(F32), ALU.subtract).then_inc(er_free[c % 2], 1)


            def result_tiles(done):
                e.wait_ge(ed_done, done)
                for c in range(4):
                    e.tensor_copy(ey[:, 2 * c:2 * c + 2, :], ps[:, 2 + c, 0:2 * C].rearrange("p (k n) -> p k n", k=2))\
                     .then_inc(ey_ready, 1)

            def result_rows(fills, stored):
                e.wait_ge(ys_out, stored)
                for n in range(4):
                    own = slice(0, P) if n < 2 else slice(P - CB, P)
                    e.wait_ge(er_done, fills + (n + 1))
                    e.tensor_copy(etok[own, n // 2, 512 * (n % 2):512 * (n % 2) + 512], ps[own, 6 + n % 2, :])\
                     .then_inc(er_free[n % 2], 1)

            for c in range(4):
                rows_lo(c, c + 1)
            with e.Fori(0, nj) as j:
                expert_lo(j, 0)
                result_tiles(j + 1)
                expert_lo(j, 1)
                for u in range(PER_JOB):
                    if u + 2 < PER_JOB:
                        expert_lo(j, u + 2)
                    if u < KE:
                        e.wait_ge(es_ready, j * KE + (u + 1))
                        e.wait_ge(ea_lo, j * KE + (max(u - 1, 0) + 1))
                        e.tensor_tensor(eat[:, u % 2, :], ps[:, u % 2, C:2 * C], esg[:, u % 2, :], ALU.mult)\
                         .then_inc(ea_tmp, 1)
                    if u == 0:
                        result_rows(j * 8 + 4, j * 32 + 16)
                    if u == KE - 1:
                        for c in range(4):
                            rows_lo(c, j * 4 + (4 + c + 1))
            result_tiles(nj + 1)
            result_rows(nj * 8 + 4, nj * 32 + 16)

            e.wait_ge(gp_in, 16)
            for i in range(NT + 1):
                n = P if i < NT else B
                s = i % 2
                e.wait_ge(yr_in[s], 32 * (i // 2 + 1))
                if i >= 2:
                    e.wait_ge(y_out[s], 16 * (i // 2))
                    e.wait_ge(f_y, i - 1)
                e.tensor_scalar(fo[0:n, s, :], yr[0:n, s, 0, :], gate[0:n, 0, i:i + 1], None, ALU.mult).then_inc(f_1, 1)
                e.wait_ge(f_1, i + 1)
                e.scalar_tensor_tensor(out=fo[0:n, s, :], in0=yr[0:n, s, 1, :], scalar=gate[0:n, 1, i:i + 1],
                                       in1=fo[0:n, s, :], op0=ALU.mult, op1=ALU.add).then_inc(f_2, 1)
                e.wait_ge(f_root, i + 1)
                e.reciprocal(frs[0:n, i, 1:2], frs[0:n, i, 1:2]).then_inc(f_inv, 1)
                e.wait_ge(f_inv, i + 1)
                e.scalar_tensor_tensor(out=fo[0:n, s, :], in0=fo[0:n, s, :], scalar=frs[0:n, i, 1:2], in1=gpost[0:n, :],
                                       op0=ALU.mult, op1=ALU.mult).then_inc(f_n, 1)
                e.wait_ge(f_n, i + 1)
                e.tensor_tensor(fo[0:n, s, :], fo[0:n, s, :], xtk[0:n, i, :], ALU.add).then_inc(f_y, 1)

        @block.tensor
        def _(e):
            def fill(f, parts):
                if f >= 2:
                    e.wait_ge(tp_free[f % 2], f // 2)
                for dst, src in parts:
                    n = src.shape[0]
                    ins = e.transpose(dst, src, ident[0:n, 0:n])
                ins.then_inc(tp_done, 1)

            def bank(f):
                return ps[:, 6 + f % 2, :]

            def sum_squares(q, first, last):
                e.wait_ge(sq_ready, q + 1)
                for h in range(2):
                    ins = e.matmul(ps[:, 4 + h, 0:HALF], ones[:, :], sq[:, q % 2, h * HALF:(h + 1) * HALF],
                                   start=first, stop=last, skip_group_check=True)
                ins.then_inc(sq_used, 1)
                return ins

            def sum_all(q0, n, inst):
                if inst:
                    e.wait_ge(root_ready, inst)
                for k in range(n):
                    sum_squares(q0 + k, k == 0, k == n - 1)
                e.wait_ge(sq_used, q0 + n)
                e.sem_inc(stat_done, 1)

            def open_sums(inst):
                e.wait_ge(root_ready, inst)
                for h in range(2):
                    e.matmul(ps[:, 4 + h, 0:HALF], ones[:, :], zero[:, :], start=True, stop=False,
                             skip_group_check=True)

            def close_sums(q):
                sum_squares(q, False, False)
                sum_squares(q + 1, False, True)
                e.wait_ge(sq_used, q + 2)
                e.sem_inc(stat_done, 1)

            def three(dst, w_hi_, w_lo_, x_hi, x_lo, first, last, check=False):
                e.matmul(dst, w_hi_, x_hi, start=first, stop=False, skip_group_check=check)
                e.matmul(dst, w_hi_, x_lo, start=False, stop=False, skip_group_check=check)
                return e.matmul(dst, w_lo_, x_hi, start=False, stop=last, skip_group_check=check)

            def tile(q, s, col, ks, first=True, last=True, xh=hh, xl=hl, k0=0, ready=None):
                for h in range(2):
                    c = slice(h * HALF, (h + 1) * HALF)
                    for n, k in enumerate(ks):
                        if ready and h == 0:
                            e.wait_ge(*ready[n])
                        o = (k - k0) * 2 * P + col
                        ins = three(ps[:, 2 * q + h, 0:HALF], whi[:, s, o:o + P], wlo[:, s, o:o + P],
                                    xh[:, k, c], xl[:, k, c], first and n == 0, last and n == len(ks) - 1)
                return ins

            def inputs(t0, ks=range(KD)):
                return [(tmp_used, t0 + n + 1) for n, _ in enumerate(ks)]

            def chunk_tiles(g, m, i, gi, mi, ks=range(KD), ready=None):
                s = g % 2
                e.wait_ge(w_lo, i * gi + (g + 1))
                for t in range(2):
                    e.wait_ge(tile_free[t], i * (mi // 2) + m // 2)
                    ins = tile(t, s, t * P, ks, ready=ready if t == 0 else None)
                    ins.then_inc(tile_done, 1)
                    if t == 1:
                        e.wait_ge(tile_done, i * mi + (m + 2))
                        e.sem_inc(w_used, 1)

            e.wait_ge(const_ready, 10)
            e.wait_ge(tabs_in, 176)
            fill(TP_CTL, [(bank(TP_CTL)[:, 0:G_ROWS], grow[0:G_ROWS, :])])
            fill(TP_CTL + 1, [(bank(TP_CTL + 1)[:, 93 * i:93 * i + 93], crow[0:93, i, :]) for i in range(2)])
            e.wait_ge(x_in, 80)
            for k in range(KD):
                f = TP_X + k
                fill(f, [(bank(f)[:, i * P:(i + 1) * P], xtok[:, i, k * P:(k + 1) * P]) for i in range(NT)])
            f = TP_X + KD
            fill(f, [(bank(f)[:, k * B:(k + 1) * B], xdec[0:B, k * P:(k + 1) * P]) for k in range(KD)])
            e.wait_ge(mem_sc, 2)
            for c in range(4):
                f = TP_MEM + c
                fill(f, [(bank(f)[:, (2 * k + i) * P:(2 * k + i + 1) * P], memtok[:, i, (2 * c + k) * P:(2 * c + k + 1) * P])
                         for k in range(2) for i in range(MT)])
            sum_all(S_X0, KD, 0)
            for g in range(4):
                e.wait_ge(w_lo, g + 1)
                e.wait_ge(hm_lo, KD * (g // 2 + 1))
                for t in range(MT):
                    m = 2 * g + t
                    if m >= 2:
                        e.wait_ge(tile_free[t], m // 2)
                    for k in range(KD):
                        c = slice(t * P, (t + 1) * P)
                        wv = slice(k * 2 * P, (k + 1) * 2 * P)
                        ins = three(ps[:, 2 * t, 0:NMEM], hmh[:, g // 2, k, c], hml[:, g // 2, k, c],
                                    whi[:, g % 2, wv], wlo[:, g % 2, wv], k == 0, k == KD - 1)
                    ins.then_inc(tile_done, 1)
                e.wait_ge(tile_done, 2 * g + 2)
                e.sem_inc(w_used, 1)
            e.wait_ge(state_in, 32)
            for c in range(3):
                f = TP_ST + c
                fill(f, [(bank(f)[:, 240 * h + 120 * i:240 * h + 120 * i + 120],
                          sttok[0:4 * PAST, i, (2 * c + h) * P:(2 * c + h + 1) * P]) for h in range(2) for i in range(2)])
            with e.Fori(0, 3) as i:
                for j in range(2):
                    chunk_tiles(U_IN + j, M_IN + 2 * j, i, 2, 4, ready=inputs(T_N0) if j == 0 else None)
            chunk_tiles(U_QM, M_QM, 0, 0, 0)
            e.wait_ge(u_ready, 2 + FS)
            for n, (lo, hi) in enumerate(((0, 4), (4, 6))):
                f = TP_UT + n
                fill(f, [(bank(f)[0:PAST + B, (c - lo) * P:(c - lo + 1) * P], ubuf[:, c, TP:PAST + T]) for c in range(lo, hi)])

            def mem_pe(layer, q):
                m = mem[layer]
                f = (TP_MA, TP_MB)[layer]
                e.wait_ge(mk_in, 32 * (layer + 1))
                fill(f, [(bank(f)[:, (2 * c + i) * P:(2 * c + i + 1) * P], m.ktok[:, i, c * P:(c + 1) * P])
                         for c in range(FM) for i in range(MT)])
                e.wait_ge(mc_in, 16 * B * (layer + 1))
                for b in range(B):
                    g = f + 1 + b
                    fill(g, [(bank(g)[:, (2 * c + i) * P:(2 * c + i + 1) * P], m.cache[:, b, i, c * P:(c + 1) * P])
                             for c in range(FM) for i in range(MT)])
                e.wait_ge(mqz_ready, 4 * (layer + 1))
                copied_out(e, f + 7)
                copied_out(e, f + 8)
                for b in range(B):
                    for c in range(FM):
                        ins = e.matmul(ps[0:32, 4, 0:NMEM], m.qz[:, FM * b + c, :], m.cT[:, b, c, :],
                                       start=(b == 0 and c == 0), stop=(b == B - 1 and c == FM - 1))
                ins.then_inc(md_s, 1)
                e.wait_ge(md_p, layer + 1)
                for i in range(MT):
                    ins = e.transpose(ps[:, 5, 32 * i:32 * i + 32], m.pd[:, i * P:(i + 1) * P], ident[0:32, 0:32])
                ins.then_inc(md_t, 1)
                e.wait_ge(md_pT, layer + 1)
                e.wait_ge(mv_in, 16 * B * (layer + 1))
                for b in range(B):
                    for c in range(FM):
                        o = 2 * (FM * b + c)
                        for i in range(MT):
                            ins = e.matmul(ps[:, 4, o:o + 2], m.cache[:, b, i, c * P:(c + 1) * P],
                                           m.pdT[:, i, 4 * b + 2 * c:4 * b + 2 * c + 2],
                                           start=(o == 0 and i == 0), stop=(i == MT - 1), skip_group_check=True)
                ins.then_inc(md_o, 1)

                def scores(h):
                    c, r = h // 2, slice(64 * (h % 2), 64 * (h % 2) + 64)
                    s = h % 2
                    if h >= 2:
                        e.wait_ge(mp_e, NT * (MH * layer + h - 1))
                    for i in range(NT):
                        ins = e.matmul(ps[:, 2 * s + i // 2, (i % 2) * NMEM:(i % 2 + 1) * NMEM],
                                       q[r, c, i * P:(i + 1) * P], m.kT[r, c, :], start=True, stop=True)
                    ins.then_inc(mp_s, 1)

                scores(0)
                for h in range(MH):
                    if h + 1 < MH:
                        scores(h + 1)
                    s = h % 2
                    e.wait_ge(mp_p, NT * (MH * layer + h + 1))
                    if h >= 1:
                        e.wait_ge(mp_pT, 2 * (MH * layer + h))
                    e.wait_ge(md_od, 2 * (layer + 1))
                    for i in range(MT):
                        for t in range(NT):
                            ins = e.transpose(ps[:, 4 + i, t * P:(t + 1) * P], m.p[:, s, t, i * P:(i + 1) * P], ident[:, :])
                    ins.then_inc(mp_t, 1)
                    e.wait_ge(mp_pT, 2 * (MH * layer + h + 1))
                    for i in range(MT):
                        ins = e.matmul(ps[64 * s:64 * s + 64, 6 + h // 2, :], m.vtok[:, i, h * HD:(h + 1) * HD],
                                       m.pT[:, i, :], start=(i == 0), stop=(i == MT - 1))
                    ins.then_inc(mp_o, 1)

            mem_pe(0, qmA)
            e.wait_ge(cv, 2 * CW * 3)
            e.wait_ge(cd_sum, FS)
            e.wait_ge(mp_pT, 2 * MH)
            for k in range(FS):
                for h in range(2):
                    ins = e.matmul(ps[:, 4 + h, 0:HALF], ones[:, :], cT[:, k, h * HALF:(h + 1) * HALF],
                                   start=(k == 0), stop=(k == FS - 1), skip_group_check=True)
            ins.then_inc(ln_sum, 1)
            e.wait_ge(ln_mean, 1)
            for k in range(FS):
                e.wait_ge(ln_sq, k + 1)
                for h in range(2):
                    ins = e.matmul(ps[:, 4 + h, 0:HALF], ones[:, :], sq[:, k % 2, h * HALF:(h + 1) * HALF],
                                   start=(k == 0), stop=(k == FS - 1), skip_group_check=True)
                ins.then_inc(ln_used, 1)
            e.wait_ge(ln_used, FS)
            e.sem_inc(ln_var, 1)

            def out_projection(u0, m0, t0, q0, ks, inst):
                e.wait_ge(tmp_used, t0 + 1)
                open_sums(inst)
                for g in range(4):
                    chunk_tiles(u0 + g, m0 + 2 * g, 0, 0, 0, ks, inputs(t0) if g == 0 else None)
                    for t in range(2):
                        sum_squares(q0 + 2 * g + t, False, False)
                close_sums(q0 + 8)

            e.wait_ge(ln_root, 1)
            out_projection(U_OUTA, M_OUTA, T_MIXA, S_YA, MIX_A, 1)
            sum_all(S_XA, KD, 2)
            with e.Fori(0, KF // 2) as i:
                for j in range(2):
                    chunk_tiles(U_GU + j, M_GU + 2 * j, i, 2, 4, ready=inputs(T_N1) if j == 0 else None)
            open_sums(3)
            e.wait_ge(ga_lo, KF)
            with e.Fori(0, 2) as i:
                for c in range(2):
                    for r in range(3):
                        g = U_DN + 3 * c + r
                        ks = range(8 * r, min(8 * r + 8, KF))
                        e.wait_ge(w_lo, i * 6 + (g + 1))
                        for t in range(2):
                            if r == 0:
                                e.wait_ge(tile_free[t], i * 2 + (M_DN // 2 + c))
                            ins = tile(t, g % 2, t * P, ks, r == 0, r == 2, acth, actl, 8 * r)
                            if r == 2:
                                ins.then_inc(tile_done, 1)
                            elif t == 1:
                                ins.then_inc(w_used, 1)
                        if r == 2:
                            e.wait_ge(tile_done, i * 4 + (M_DN + 2 * c + 2))
                            e.sem_inc(w_used, 1)
                        if r == 0:
                            for t in range(2):
                                e.wait_ge(sq_ready, i * 4 + (S_YF + 2 * c + t + 1))
                                for h in range(2):
                                    ins = e.matmul(ps[:, 4 + h, 0:HALF], ones[:, :], sq[:, t, h * HALF:(h + 1) * HALF],
                                                   start=False, stop=False, skip_group_check=True)
                                ins.then_inc(sq_used, 1)
            close_sums(S_YF + 8)
            sum_all(S_XF, KD, 4)
            with e.Fori(0, 3) as i:
                for j in range(2):
                    chunk_tiles(U_KV + j, M_KV + 2 * j, i, 2, 4, ready=inputs(T_N2) if j == 0 else None)
            e.wait_ge(tile_free[0], M_Q // 2)
            e.wait_ge(tile_free[1], M_Q // 2)
            for n in range(20):
                w, i, half = n // 10, (n % 10) // 2, n % 2
                f = TP_KV + n
                c0, c1 = (0, 4) if half == 0 else (4, 6)
                src, lo, hi = ((vT, kT)[w], i * P, i * P + P) if i < NT else ((vT, kT)[w], TP, T)
                fill(f, [(bank(f)[0:hi - lo, (c - c0) * P:(c - c0 + 1) * P], src[:, c, lo:hi]) for c in range(c0, c1)])
            with e.Fori(0, 2) as i:
                for j in range(2):
                    chunk_tiles(U_Q + j, M_Q + 2 * j, i, 2, 4, ready=inputs(T_N3) if j == 0 else None)

            e.wait_ge(qd_ready, 2)
            for b in range(B + 1):
                if b < B:
                    e.wait_ge(pg_in[b % 2], 32 * (b // 2 + 1))
                    for c in range(3):
                        f = TP_PG + 3 * b + c
                        parts = [(bank(f)[:, (2 * n + g) * P:(2 * n + g + 1) * P],
                                  pgs[:, b % 2, g, (2 * c + n) * P:(2 * c + n + 1) * P]) for n in range(2) for g in range(NPG)]
                        fill(f, parts)
                    e.wait_ge(tp_done, TP_PG + 3 * b + 3)
                    e.sem_inc(pg_used, 1)
                if b >= 1:
                    d = b - 1
                    for c in range(3):
                        copied_out(e, TP_PG + 3 * d + c)
                    for c in range(FS):
                        for g in range(NPG):
                            o = 96 * g + NH * d + 2 * c
                            ins = e.matmul(ps[:, 0, o:o + 2], pgT[:, d % 2, c, g * P:(g + 1) * P], qd2[:, d, c, :],
                                           start=(d == 0 and c == 0 and g == 0), stop=False, skip_group_check=True)
                    ins.then_inc(pg_qk, 1)
            e.wait_ge(pg_qk, B)
            e.sem_inc(sd_z, 1)
            e.wait_ge(sd_sp, 1)
            e.matmul(ps[:, 0, 0:96], negtri[:, :], zd[:, 2, 0:96], start=False, stop=False, skip_group_check=True)
            e.matmul(ps[:, 0, 0:96], negone[:, :], zd[:, 2, 96:192], start=False, stop=False, skip_group_check=True)
            e.matmul(ps[:, 0, 96:192], negtri[:, :], zd[:, 2, 96:192], start=False, stop=True, skip_group_check=True)\
             .then_inc(sd_c, 1)
            e.wait_ge(sd_w, 1)
            for b in range(B):
                e.wait_ge(pg_in[b % 2], 32 * (B // 2 + b // 2 + 1))
                for c in range(FS):
                    o = 2 * (FS * b + c)
                    for g in range(NPG):
                        p0 = 96 * g + NH * b + 2 * c
                        ins = e.matmul(ps[:, 1, o:o + 2], pgs[:, b % 2, g, c * P:(c + 1) * P], zd[:, 3, p0:p0 + 2],
                                       start=(o == 0 and g == 0), stop=(g == NPG - 1), skip_group_check=True)
                ins.then_inc(pg_used, 1)
            e.wait_ge(pg_used, 2 * B)
            e.sem_inc(sd_o, 1)
            e.wait_ge(sd_od, 2)

            def segment(buf, i, c0=0):
                return buf[:, SEG_AT[i] + c0:SEG_AT[i] + seg_w[i]]

            for h in range(NH + 2):
                if h < NH:
                    c, r = h // 2, slice(64 * (h % 2), 64 * (h % 2) + 64)
                    z = flat[:, 1536 * (h % 2):1536 * (h % 2) + SEG]
                    if h >= 2:
                        e.wait_ge(sb_w, h - 1)
                    for i in (0, 1, 3, 2):
                        ins = e.matmul(segment(z, i), kT[r, c, i * P:(i + 1) * P], qT[r, c, i * P:TP],
                                       start=(i != 3), stop=False, skip_group_check=True)
                    ins.then_inc(sb_z, 1)
                if 1 <= h <= NH:
                    g = h - 1
                    z = flat[:, 1536 * (g % 2):1536 * (g % 2) + SEG]
                    e.wait_ge(sb_sp, NT * (g + 1))
                    for i in (0, 1, 3, 2):
                        ins = e.matmul(segment(z, i), negtri[:, :], segment(sp[g % 2], i), start=False, stop=False,
                                       skip_group_check=True)
                        for n in range(i + 1, NT):
                            ins = e.matmul(segment(z, i, (n - i) * P), negone[:, :], segment(sp[g % 2], n),
                                           start=False, stop=False, skip_group_check=True)
                    ins.then_inc(sb_c, 1)
                if h >= 2:
                    g = h - 2
                    c, r = g // 2, slice(64 * (g % 2), 64 * (g % 2) + 64)
                    e.wait_ge(sb_wm, NT * (g + 1))
                    if c >= 2:
                        e.wait_ge(tmp_ready, T_MIXB + c - 1)
                    for i in range(NT):
                        ins = e.matmul(ps[r, 6 + c % 2, i * P:TP], vtok[:, i, g * HD:(g + 1) * HD], segment(wt[g % 2], i),
                                       start=(i == 0), stop=(i == NT - 1), skip_group_check=True)
                    ins.then_inc(sb_pv, 1)
            e.wait_ge(tmp_ready, T_MIXB + FS)
            mem_pe(1, qT[:, FS:KD, :])
            out_projection(U_OUTB, M_OUTB, T_MIXB, S_YB, range(KD), 5)
            sum_all(S_XB, KD, 6)

            e.wait_ge(hf_ready, KD)
            e.wait_ge(root_ready, 7)
            for i in range(NT + 1):
                n = P if i < NT else B
                for k in range(KD):
                    ins = e.matmul(ps[0:n, 4, i * E:(i + 1) * E], hf[:, k, i * P:i * P + n], wr[:, k, :],
                                   start=(i == 0 and k == 0), stop=(k == KD - 1), skip_group_check=True)
            ins.then_inc(lg_done, 1)
            for n in range(10):
                f, i = TP_HT + n, n // 2
                w = P if i < NT else B
                fill(f, [(bank(f)[0:w, k * P:(k + 1) * P], hf[:, 4 * (n % 2) + k, i * P:i * P + w]) for k in range(4)])
            e.wait_ge(mask_ready, 1)
            msk = rt[:, 5, :, :]
            for i in range(NT + 1):
                ins = e.matmul(ps[:, 5, i * E:(i + 1) * E], before[:, :], msk[:, i, :], start=(i == 0), stop=False,
                               skip_group_check=True)
                for n in range(i):
                    e.matmul(ps[:, 5, i * E:(i + 1) * E], ones[:, :], msk[:, n, :], start=False, stop=False,
                             skip_group_check=True)
            for n in range(NT + 1):
                ins = e.matmul(ps[:, 5, (NT + 1) * E:(NT + 2) * E], ones[:, :], msk[:, n, :], start=False,
                               stop=(n == NT), skip_group_check=True)
            ins.then_inc(cnt_done, 1)
            for n in range(10):
                f, i = TP_XT + n, n // 2
                w = P if i < NT else B
                fill(f, [(bank(f)[0:w, k * P:(k + 1) * P], x[:, 4 * (n % 2) + k, i * P:i * P + w]) for k in range(4)])

            e.wait_ge(slots_ready, 1)
            nj = e.value_load(jobi[0:1, MAXJOBS:MAXJOBS + 1], min_val=E, max_val=MAXJOBS)
            e.sem_inc(ew_used, SPLIT)
            copied_out(e, TP_XT + 8)
            copied_out(e, TP_XT + 9)

            def rows_in(landed, base, prologue=False):
                e.wait_ge(gt_in, landed)
                for c in range(4):
                    if not (prologue and c < 2):
                        e.wait_ge(er_free[c % 2], base + c // 2)
                    for k in range(2):
                        kk = 2 * c + k
                        e.transpose(ps[:, 6 + c % 2, k * C:k * C + P], gtok[:, 0, kk * P:(kk + 1) * P], ident[:, :])
                        ins = e.transpose(ps[:, 6 + c % 2, k * C + P:(k + 1) * C], gtok[0:CB, 1, kk * P:(kk + 1) * P],
                                          ident[0:CB, 0:CB])
                    ins.then_inc(er_done, 1)

            def rows_out(ready, base):
                e.wait_ge(ey_ready, ready)
                for n in range(4):
                    lo = 0 if n < 2 else CB
                    e.wait_ge(er_free[n % 2], base + n // 2)
                    for k in range(4):
                        ins = e.transpose(ps[:, 6 + n % 2, k * P:(k + 1) * P], ey[:, 4 * (n % 2) + k, lo:lo + P],
                                          ident[:, :])
                    ins.then_inc(er_done, 1)

            rows_in(32, 0, True)
            for c in range(4):
                for h in range(2):
                    ins = e.matmul(ps[:, 2 + c, h * C:(h + 1) * C], ones[:, :], zero[:, 0:C], start=True, stop=True)
            ins.then_inc(ed_done, 1)
            with e.Fori(0, nj) as j:
                for u in range(PER_JOB):
                    s = u % SPLIT
                    e.wait_ge(ew_lo, j * PER_JOB + (RAW + u + 1))
                    if u < KE:
                        if u == 0:
                            e.wait_ge(ej_hi, j * 4 + 4)
                            e.wait_ge(er_free[0], j * 4 + 2)
                            e.wait_ge(er_free[1], j * 4 + 2)
                        e.wait_ge(ea_tmp, j * KE + (max(u - 1, 0) + 1))
                        for t in range(2):
                            for k in range(KD):
                                o = k * 2 * P + t * P
                                ins = three(ps[:, u % 2, t * C:(t + 1) * C], ewh[:, s, o:o + P], ewl[:, s, o:o + P],
                                            ejh[:, k, :], ejl[:, k, :], k == 0, k == KD - 1)
                        ins.then_inc(eg_done, 1)
                        e.wait_ge(eg_done, j * KE + (u + 1))
                        e.sem_inc(ew_used, 1)
                        if u == 0:
                            rows_out(j * 4 + 4, j * 4 + 2)
                        if u == KE - 1:
                            rows_in(j * 32 + 64, j * 4 + 4)
                    else:
                        n, k0 = DN_CUTS[u - KE], DN_K0[u - KE]
                        if u == KE:
                            e.wait_ge(ea_lo, j * KE + (KE + 1))
                            e.wait_ge(ey_ready, j * 4 + 4)
                        for i in range(n):
                            k = k0 + i
                            for m in range(KD):
                                o = i * D + m * P
                                ins = three(ps[:, 2 + m // 2, (m % 2) * C:(m % 2 + 1) * C], ewh[:, s, o:o + P],
                                            ewl[:, s, o:o + P], eah[:, k, :], eal[:, k, :],
                                            k == 0 and m % 2 == 0, k == KE - 1, True)
                        if u < PER_JOB - 1:
                            ins.then_inc(ew_used, 1)
                        else:
                            ins.then_inc(ed_done, 1)
                            e.wait_ge(ed_done, j + 2)
                            e.sem_inc(ew_used, 1)
            rows_out(nj * 4 + 4, nj * 4 + 2)


_OUTS = [(1, TP, D), (B, 1, D), (1, 1, PAST, FS * P), (1, TP, NH, HD), (1, TP, NH, HD), (2, 1, NMEM, MH, HD),
         (2, 1, NMEM, MH, HD), (1, B, PAST, FS * P), (B, 1, NH, HD), (B, 1, NH, HD)]


def kernel(**inputs):
    import numpy as _np
    import concourse.bacc as _bacc
    from concourse.bass_utils import run_bass_kernel_spmd as _run

    nc = _bacc.Bacc("TRN2", target_bir_lowering=False, num_devices=1)
    arrays, args = {}, {}
    for name, value in inputs.items():
        v = _np.ascontiguousarray(value)
        arrays[f"in_{name}"] = v
        args[name] = nc.dram_tensor(f"in_{name}", v.shape, mybir.dt.from_np(v.dtype), kind="ExternalInput").ap()
    outs = [nc.dram_tensor(f"out_{i}", shape, F32, kind="ExternalOutput").ap() for i, shape in enumerate(_OUTS)]
    build(nc, args, outs)
    r = _run(nc, [arrays], core_ids=[0])
    return tuple(r.results[0][f"out_{i}"] for i in range(len(_OUTS)))
```

```python
from contextlib import ExitStack

import concourse.bass as bass
from concourse import mybir

F32 = mybir.dt.float32
F32R = mybir.dt.float32r
I32 = mybir.dt.int32
ACT = mybir.ActivationFunctionType
ALU = mybir.AluOpType
AX = mybir.AxisListType.X

P = 128
D = 1024
KD = D // P
TP = 512
B = 8
T = TP + B
HALF = T // 2
NT = TP // P
NMEM = 256
MT = NMEM // P
HD = 64
NH = 12
FS = NH * HD // P
MH = 4
FM = MH * HD // P
CW = 31
PAST = CW - 1
PAGE = 128
NPG = 2
DFF = 2816
KF = DFF // P
E = 8
DFE = 1408
KE = DFE // P
C = 192
CB = C - P
MAXJOBS = (2 * T + E * C) // C
SLOTS = (MAXJOBS + 2) * C
EPS = 1e-6
CLAMP = 40.0

G_PRE_MIX, G_POST_MIX, G_PRE_FFN, G_POST_FFN, G_KV, G_MEM = 0, 16, 32, 48, 64, 72
G_CB, G_LNG, G_LNB, G_ROWS = 88, 94, 100, 106

U_MEM, U_IN, U_QM, U_OUTA, U_GU, U_DN, U_KV, U_Q, U_OUTB, U_END = 0, 4, 10, 11, 15, 37, 49, 55, 59, 63
M_MEM, M_IN, M_QM, M_OUTA, M_GU, M_DN, M_KV, M_Q, M_OUTB, M_END = 0, 8, 20, 22, 30, 74, 82, 94, 102, 110
T_N0, T_MIXA, T_P0, T_N1, T_P1, T_N2, T_N3, T_MIXB, T_P2 = 0, 8, 16, 24, 32, 40, 48, 56, 64
NTMP = 4
HI_AT = {t: n for n, t in enumerate([t0 + k for t0 in (T_N0, T_MIXA, T_N1, T_N2, T_N3, T_MIXB) for k in range(KD)])}
MIX_A = [6, 7, 0, 1, 2, 3, 4, 5]
S_X0, S_YA, S_XA, S_YF, S_XF, S_YB, S_XB = 0, 8, 18, 26, 36, 44, 54
SUM_END = [S_YA, S_XA, S_YF, S_XF, S_YB, S_XB, S_XB + KD]
TP_CTL, TP_X, TP_MEM, TP_ST, TP_UT, TP_MA, TP_KV, TP_PG, TP_MB, TP_HT, TP_XT = 0, 2, 11, 15, 18, 20, 29, 49, 73, 82, 92


def build(nc, a, o):
    (y_prompt, y_sample, conv_prompt, k_prompt, v_prompt, mem_k_prompt, mem_v_prompt,
     conv_sample, k_sample, v_sample) = o
    with ExitStack() as ctx:
        def at(name, shape, dt, offset):
            return nc.alloc_sbuf_tensor_at(name, shape, dt, offset=base0 + offset)

        def small(name, shape, dt=F32):
            return ctx.enter_context(nc.sbuf_tensor(name, shape, dt))

        def sem(name):
            return ctx.enter_context(nc.semaphore(name))

        ARENA = 190592
        base0 = -(-nc.sbuf_base // 64) * 64
        ctx.enter_context(nc.sbuf_tensor("arena", [P, ARENA // 4 + 16], F32))
        x = at("x", [P, KD, T], F32, 0)
        hh = at("hh", [P, KD, T], F32R, 16640)
        hl = at("hl", [P, KD, T], F32R, 33280)
        raw = at("raw", [P, 2, 2048], F32, 49920)
        whi = at("whi", [P, 2, 2048], F32R, 66304)
        wlo = at("wlo", [P, 2, 2048], F32R, 82688)
        A = 99072
        y_dn = at("y_dn", [P, KD, T], F32, 16640)
        xtok = at("xtok", [P, NT, D], F32, A)
        xdec = at("xdec", [P, D], F32, A + 16384)
        memtok = at("memtok", [P, MT, D], F32, A + 20480)
        mT = at("mT", [P, KD, NMEM], F32, A + 28672)
        hmh = at("hmh", [P, 2, KD, NMEM], F32R, A + 36864)
        hml = at("hml", [P, 2, KD, NMEM], F32R, A + 53248)
        mkv = at("mkv", [P, 2, 2, MT, NMEM], F32, A + 69632)
        grow = at("grow", [P, P], F32, A + 77824)
        crow = at("crow", [P, 2, P], F32, A + 78336)
        cT = at("cT", [P, FS, T], F32, A)
        udec = at("udec", [P, FS, B, CW], F32, A + 12480)
        sttok = at("sttok", [P, 2, FS * P], F32, A + 18432)
        cprod = at("cprod", [P, TP], F32, A + 18432)
        ctmp = at("ctmp", [P, B, CW], F32, A + 24576)
        qmA = at("qmA", [P, FM, T], F32, A + 25600)
        MA = 29760
        ubuf = at("ubuf", [P, FS, PAST + T], F32, A + 72192)
        utail = at("utail", [P, FS * P], F32, A + 85408)
        y_mix = at("y_mix", [P, KD, T], F32, A + 39424)
        mean = at("mean", [P, T], F32, A + 88480)
        acth = at("acth", [P, KF, T], F32R, A)
        actl = at("actl", [P, KF, T], F32R, A + 45760)
        kT = at("kT", [P, FS, T], F32, A)
        vT = at("vT", [P, FS, T], F32, A + 12480)
        vtok = at("vtok", [P, NT, FS * P], F32, A + 24960)
        ktok = at("ktok", [P, NT, FS * P], F32, A + 37248)
        kvdec = at("kvdec", [P, 2, FS * P], F32, A + 49536)
        qT = at("qT", [P, KD, T], F32, A + 55680)
        SEG = 1280
        sp = [at(f"sp{i}", [P, SEG], F32, A + 12480 + 5120 * i) for i in range(2)]
        wt = [at(f"wt{i}", [P, SEG], F32, A + 37248 + 5120 * i) for i in range(2)]
        zc = [at("zc0", [P, SEG], F32, A + 47488), at("zc1", [P, SEG], F32, A + 72320)]
        pgs = at("pgs", [P, 2, NPG, FS * P], F32, A + 77440)
        pgT = at("pgT", [P, 2, FS, NPG * P], F32, A + 37248)
        zd = at("zd", [P, 4, 192], F32, A + 49536)
        qd2 = at("qd2", [P, B, FS, 2], F32, A + 52608)

        class Mem:
            pass

        mem = []
        for layer, off in ((0, A + MA), (1, A)):
            m = Mem()
            m.ktok = at(f"mktok{layer}", [P, MT, NMEM], F32, off)
            m.vtok = at(f"mvtok{layer}", [P, MT, NMEM], F32, off + 2048)
            m.kT = at(f"mkT{layer}", [P, FM, NMEM], F32, off + 4096)
            m.qz = at(f"mqz{layer}", [P, B * FM, 32], F32, off + 6144)
            m.pd = at(f"mpd{layer}", [32, NMEM], F32, off + 8192)
            m.pdT = at(f"mpdT{layer}", [P, MT, 32], F32, off + 9216)
            m.cache = at(f"mcache{layer}", [P, B, MT, NMEM], F32, off + 9664)
            m.cT = at(f"mcT{layer}", [P, B, FM, NMEM], F32, off + 26048)
            m.p = at(f"mp{layer}", [P, 2, NT, NMEM], F32, off + 26048)
            m.pT = at(f"mpT{layer}", [P, MT, TP], F32, off + 34240)
            mem.append(m)

        hf = at("hf", [P, KD, T], F32, 132992)
        htok = at("htok", [P, NT + 1, D], F32, 149632)
        xtk = at("xtk", [P, NT + 1, D], F32, 170112)
        ewh = at("ewh", [P, 3, 2048], F32R, 16640)
        ewl = at("ewl", [P, 3, 2048], F32R, 41216)
        eraw = at("eraw", [P, 6, 2048], F32, 65792)
        gtok = at("gtok", [P, 2, D], F32, 114944)
        ejx = at("ejx", [P, KD, 2, C], F32R, 131328)
        eah = at("eah", [P, KE, C], F32R, 143616)
        eal = at("eal", [P, KE, C], F32R, 152064)
        etok = at("etok", [P, 2, D], F32, 0)
        esg = at("esg", [P, 2, C], F32, 8192)
        eup = at("eup", [P, 2, C], F32, 8192 + 1536)
        eat = at("eat", [P, 2, C], F32, 8192 + 3072)
        yr = at("yr", [P, NT + 1, 2, D], F32, 16640)
        fo = at("fo", [P, NT + 1, D], F32, 57600)
        fs = at("fs", [P, 2, D], F32, 78080)
        gpost = at("gpost", [P, D], F32, 86272)

        sq = small("sq", [P, 2, T])
        rstd = small("rstd", [P, T])
        tmp = small("tmp", [P, NTMP, T])
        ident = small("ident", [P, P])
        negtri = small("negtri", [P, P])
        negone = small("negone", [P, P])
        ones = small("ones", [P, P])
        before = small("before", [P, P])
        gT = small("gT", [P, G_ROWS])
        cwT = small("cwT", [P, CW, FS])
        bias = small("bias", [P, B, NH])
        eps = small("eps", [P, 1])
        stm = small("stm", [P, 2, NT])
        sts = small("sts", [P, 2, NT])
        ms = small("ms", [P, 4])
        od = small("od", [P, FS, B])
        ptab = small("ptab", [1, B * NPG], I32)
        wr = small("wr", [P, KD, E])
        br = small("br", [P, E])
        zero = small("zero", [P, HALF])
        R = 123136
        rt = at("rt", [P, 8, NT + 1, E], F32, R)
        r5 = at("r5", [P, 12, NT + 1], F32, R + 1280)
        r8 = at("r8", [P, 6, E], F32, R + 1536)
        io8 = at("io8", [P, NT + 1, E], F32, R + 1728)
        ioj = at("ioj", [P, MAXJOBS, E], F32, R + 1888)
        ioi = at("ioi", [P, MAXJOBS, E], I32, R + 2304)
        ioe = at("ioe", [P, NT + 1, E], I32, R + 2720)
        jcmp = at("jcmp", [P, MAXJOBS, E], F32, R + 2880)
        jobf = at("jobf", [P, MAXJOBS + 1], F32, R + 3296)
        jobi = at("jobi", [P, MAXJOBS + 1], I32, R + 3360)
        sloti = at("sloti", [P, 2, NT + 1], I32, R + 3424)
        valid = at("valid", [P, NT + 1], F32, R + 3488)
        gate = at("gate", [P, 2, NT + 1], F32, R + 3520)
        frs = at("frs", [P, NT + 1, 2], F32, R + 3584)

        ps = ctx.enter_context(nc.psum_tensor("ps", [P, 8, 512], F32))
        flat = ps[:, :, :].rearrange("p b n -> p (b n)")

        xs = nc.dram_tensor("xs", (SLOTS, D), F32, kind="Internal").ap()
        ys = nc.dram_tensor("ys", (SLOTS, D), F32, kind="Internal").ap()

        x_in, mem_in, tabs_in, state_in, small_in, const_ready = map(
            sem, "x_in mem_in tabs_in state_in small_in const_ready".split())
        w_in = [sem("w_in0"), sem("w_in1")]
        w_hi, w_lo, w_used = map(sem, "w_hi w_lo w_used".split())
        tile_done = sem("tile_done")
        tile_free = [sem("tile_free0"), sem("tile_free1")]
        tmp_ready, hi_ready, tmp_used = map(sem, "tmp_ready hi_ready tmp_used".split())
        sq_ready, sq_used, root_ready, rstd_ready = map(sem, "sq_ready sq_used root_ready rstd_ready".split())
        tp_done = sem("tp_done")
        tp_free = [sem("tp_free0"), sem("tp_free1")]
        mem_ss, mem_root, mem_inv, mem_sc, hm_hi, hm_lo, mkv_out = map(
            sem, "mem_ss mem_root mem_inv mem_sc hm_hi hm_lo mkv_out".split())
        u_ready, ud_new, cv, cvp, cd, cd_sum = map(sem, "u_ready ud_new cv cvp cd cd_sum".split())
        ln_sum, ln_mean, ln_xc, ln_sq, ln_used, ln_root, ln_rstd, ln_y = map(
            sem, "ln_sum ln_mean ln_xc ln_sq ln_used ln_root ln_rstd ln_y".split())
        outs = sem("outs")
        mk_in, mc_in, mv_in, mqz_zero, mqz_ready = map(
            sem, "mk_in mc_in mv_in mqz_zero mqz_ready".split())
        md_s, md_max, md_e, md_inv, md_p, md_t, md_pT, md_o, md_od = map(
            sem, "md_s md_max md_e md_inv md_p md_t md_pT md_o md_od".split())
        mp_s, mp_max, mp_e, mp_inv, mp_p, mp_t, mp_pT, mp_o, mp_out = map(
            sem, "mp_s mp_max mp_e mp_inv mp_p mp_t mp_pT mp_o mp_out".split())
        ga_hi, ga_lo = map(sem, "ga_hi ga_lo".split())
        kv_out = sem("kv_out")
        pg_in = [sem("pg_in0"), sem("pg_in1")]
        pg_used, pg_qk, qd_zero, qd_ready = map(
            sem, "pg_used pg_qk qd_zero qd_ready".split())
        sd_zb, sd_zc, sd_e, sd_l, sd_sp, sd_c, sd_x, sd_w, sd_od = map(
            sem, "sd_zb sd_zc sd_e sd_l sd_sp sd_c sd_x sd_w sd_od".split())
        sb_z, sb_zc, sb_e, sb_l, sb_s, sb_sp, sb_c, sb_w, sb_wm, sb_pv, sb_out = map(
            sem, "sb_z sb_zc sb_e sb_l sb_s sb_sp sb_c sb_w sb_wm sb_pv sb_out".split())
        hf_ready, lg_done, rr, rr_exp, rr_m1, mask_ready, cnt_done, slots_ready, io_int, io_ready = map(
            sem, "hf_ready lg_done rr rr_exp rr_m1 mask_ready cnt_done slots_ready io_int io_ready".split())
        xs_zero, ys_zero, xs_in, g0_in, gt_in = map(sem, "xs_zero ys_zero xs_in g0_in gt_in".split())
        ew_in = [sem(f"ew_in{i}") for i in range(6)]
        ew_hi, ew_lo, ew_used, eg_done, eg_silu, ea_tmp, ea_hi, ea_lo = map(
            sem, "ew_hi ew_lo ew_used eg_done eg_silu ea_tmp ea_hi ea_lo".split())
        ed_done, ey_ready, er_done, ej_hi, ys_out, ys_ready = map(
            sem, "ed_done ey_ready er_done ej_hi ys_out ys_ready".split())
        eb_free = [sem(f"eb_free{i}") for i in range(4)]
        yr_in = [sem(f"yr_in{i}") for i in range(NT + 1)]
        gp_in, f_1, f_2, f_ss, f_root, f_inv, f_n, f_y = map(
            sem, "gp_in f_1 f_2 f_ss f_root f_inv f_n f_y".split())
        y_out = sem("y_out")


        block = ctx.enter_context(nc.Block())

        def halves(ap):
            return ap.rearrange("p (h n) -> p h n", h=2)

        def pair(q):
            return ps[:, 2 * q:2 * q + 2, 0:HALF]

        def heads(ap):
            return ap.rearrange("m h d -> m (h d)")

        def row_broadcast(src, shape_ap):
            return bass.AP(tensor=src.tensor, offset=src.offset, ap=[[0, P]] + shape_ap)

        def copied_out(e, f):
            e.wait_ge(tp_free[f % 2], f // 2 + 1)

        def gain(off, k):
            return gT[:, off + k:off + k + 1]

        win, wgd, wud = a["w_in_a"][0], a["w_gate_d"][0], a["w_up_d"][0]
        xs_t = xs.rearrange("(b c) d -> b c d", c=C)
        ys_t = ys.rearrange("(b c) d -> b c d", c=C)
        DN_CUTS = [2, 2, 2, 2, 1, 1, 1]
        DN_K0 = [sum(DN_CUTS[:i]) for i in range(len(DN_CUTS))]
        seg_w = {i: TP - P * i for i in range(NT)}
        PER_JOB = KE + len(DN_CUTS)
        RAW, SPLIT = 6, 3
        assert PER_JOB % RAW == 0 and PER_JOB % SPLIT == 0 and sum(DN_CUTS) == KE
        EB = [0, 1, 6, 7]
        EB_USES = [7, 7, 6, 6]

        def eb_at(n):
            return n % 4, n // 4

        SEG_AT = {0: 0, 1: 512, 3: 896, 2: 1024}

        def kv_fill(n):
            w, i, half = n // 10, (n % 10) // 2, n % 2
            f = TP_KV + n
            rows_ = P if i < NT else B
            c0, c1 = (0, 4 * P) if half == 0 else (4 * P, FS * P)
            dst = (vtok, ktok)[w][:, i, c0:c1] if i < NT else kvdec[0:B, w, c0:c1]
            return f, dst, ps[0:rows_, 6 + f % 2, 0:c1 - c0]

        @block.sync
        def _(e):
            g2 = a["g_mem"]
            n = 0
            for name in ("g_pre_mix", "g_post_mix", "g_pre_ffn", "g_post_ffn"):
                e.dma_start(grow[n:n + 16, :], a[name].rearrange("l (k p) -> (l k) p", p=P)).then_inc(tabs_in, 16)
                n += 16
            e.dma_start(grow[G_KV:G_KV + 8, :], a["g_kv"].rearrange("(k p) -> k p", p=P)).then_inc(tabs_in, 16)
            e.dma_start(grow[G_MEM:G_MEM + 16, :], g2.rearrange("l (k p) -> (l k) p", p=P)).then_inc(tabs_in, 16)
            for off, name in ((G_CB, "conv_b"), (G_LNG, "conv_ln_g"), (G_LNB, "conv_ln_b")):
                e.dma_start(grow[off:off + FS, :], a[name].rearrange("l (k p) -> (l k) p", p=P)).then_inc(tabs_in, 16)
            taps = a["conv_w"][0].rearrange("j (f p) -> (j f) p", p=P)
            for i in range(2):
                e.dma_start(crow[0:93, i, :], taps[93 * i:93 * i + 93, :]).then_inc(tabs_in, 16)
            xp = a["x_prompt"][0]
            for i in range(NT):
                e.dma_start(xtok[:, i, :], xp[i * P:(i + 1) * P, :]).then_inc(x_in, 16)
            e.dma_start(xdec[0:B, :], a["x_sample"].rearrange("b s d -> (b s) d")).then_inc(x_in, 16)
            e.dma_start(memtok[:, :, :], a["mem_prompt"][0].rearrange("(m p) d -> p m d", p=P)).then_inc(mem_in, 16)

            def rows(w, col, k0, k1, cols=2 * P):
                return w[k0 * P:k1 * P, :].rearrange("(k p) n -> p k n", p=P)[:, :, bass.ds(col, cols)]

            def load_whole(s, w, col, k0=0, k1=KD):
                v = raw[:, s, :].rearrange("p (k n) -> p k n", n=2 * P)
                h = (k0 + k1) // 2
                e.dma_start(v[:, 0:h - k0, :], rows(w, col, k0, h)).then_inc(w_in[s], 16)
                e.dma_start(v[:, h - k0:k1 - k0, :], rows(w, col, h, k1)).then_inc(w_in[s], 16)

            def load_pair(s, w1, col1, w2, col2):
                v = raw[:, s, :].rearrange("p (k j n) -> p k j n", k=KD, j=2)
                e.dma_start(v[:, :, 0, :], rows(w1, col1, 0, KD, P)).then_inc(w_in[s], 16)
                e.dma_start(v[:, :, 1, :], rows(w2, col2, 0, KD, P)).then_inc(w_in[s], 16)

            for g in range(2):
                load_whole(g, a["w_mem_kv"][0], g * NMEM)
            e.dma_start(ptab[:, :], a["page_table"].rearrange("(o b) g -> o (b g)", o=1)).then_inc(small_in, 16)
            e.dma_start(bias[:, :, :], row_broadcast(a["sb_bias"], [[0, B], [1, NH]])).then_inc(small_in, 16)
            e.dma_start(wr[:, :, :], a["w_router"][0].rearrange("(k p) e -> p k e", p=P)).then_inc(small_in, 16)
            e.dma_start(br[:, :], row_broadcast(a["b_router"], [[1, E]])).then_inc(small_in, 16)
            e.wait_ge(tp_done, TP_ST)
            st = a["state_conv"][0].rearrange("b r c -> (b r) c")
            for i in range(2):
                e.dma_start(sttok[0:4 * PAST, i, :], st[4 * PAST * i:4 * PAST * (i + 1), :]).then_inc(state_in, 16)
            for g in range(2, 4):
                e.wait_ge(w_lo, g - 1)
                load_whole(g % 2, a["w_mem_kv"][1], (g - 2) * NMEM)
            for p in range(2):
                e.wait_ge(w_lo, U_IN + p - 1)
                load_pair((U_IN + p) % 2, win, p * P, win, (FS + p) * P)
            for layer in range(2):
                for w, dst in enumerate((mem_k_prompt, mem_v_prompt)):
                    for t in range(MT):
                        e.wait_ge(tile_free[t], 2 * layer + w + 1)
                    e.dma_start(dst[layer, 0].rearrange("(m p) h d -> p m (h d)", p=P),
                                mkv[:, layer, w, :, :]).then_inc(mkv_out, 16)
            with e.Fori(1, 3) as i:
                for j in range(2):
                    e.wait_ge(w_lo, i * 2 + (U_IN + j - 1))
                    load_pair((U_IN + j) % 2, win, i * (2 * P) + j * P, win, i * (2 * P) + (FS + j) * P)
            e.wait_ge(w_lo, U_QM - 1)
            load_whole(U_QM % 2, win, 2 * FS * P)

            def mem_loads(layer):
                m = mem[layer]
                e.wait_ge(mkv_out, 64)
                e.dma_start(m.ktok[:, :, :], mem_k_prompt[layer, 0].rearrange("(m p) h d -> p m (h d)", p=P))\
                    .then_inc(mk_in, 16)
                e.dma_start(m.vtok[:, :, :], mem_v_prompt[layer, 0].rearrange("(m p) h d -> p m (h d)", p=P))\
                    .then_inc(mk_in, 16)
                for b in range(B):
                    e.dma_start(m.cache[:, b, :, :], a["cache_mem_k"][layer, b].rearrange("(m p) h d -> p m (h d)", p=P))\
                        .then_inc(mc_in, 16)
                e.wait_ge(tp_done, (TP_MA, TP_MB)[layer] + 9)
                for b in range(B):
                    e.dma_start(m.cache[:, b, :, :], a["cache_mem_v"][layer, b].rearrange("(m p) h d -> p m (h d)", p=P))\
                        .then_inc(mv_in, 16)

            for i in range(2):
                e.wait_ge(w_lo, U_OUTA + i - 1)
                load_whole((U_OUTA + i) % 2, a["w_out_a"][0], i * 2 * P)
            mem_loads(0)
            copied_out(e, TP_UT)
            copied_out(e, TP_UT + 1)
            e.dma_start(conv_prompt[0, 0], utail[0:PAST, :]).then_inc(outs, 16)
            e.dma_start(conv_sample[0, :, PAST - 1, :], utail[PAST:PAST + B, :]).then_inc(outs, 16)
            e.dma_start(conv_sample[0, :, 0:PAST - 1, :], a["state_conv"][0, :, 1:PAST, :]).then_inc(outs, 16)
            for i in range(2, 4):
                e.wait_ge(w_lo, U_OUTA + i - 1)
                load_whole((U_OUTA + i) % 2, a["w_out_a"][0], i * 2 * P)
            with e.Fori(0, KF // 2) as i:
                for j in range(2):
                    e.wait_ge(w_lo, i * 2 + (U_GU + j - 1))
                    load_pair((U_GU + j) % 2, wgd, i * (2 * P) + j * P, wud, i * (2 * P) + j * P)
            with e.Fori(0, 2) as i:
                for j in range(6):
                    e.wait_ge(w_lo, i * 6 + (U_DN + j - 1))
                    r = j % 3
                    load_whole((U_DN + j) % 2, a["w_down_d"][0], i * (4 * P) + (j // 3) * 2 * P,
                               8 * r, min(8 * r + 8, KF))
            with e.Fori(0, 3) as i:
                for j in range(2):
                    e.wait_ge(w_lo, i * 2 + (U_KV + j - 1))
                    load_whole((U_KV + j) % 2, a["w_kv"], i * (4 * P) + j * 2 * P)
            e.wait_ge(small_in, 64)
            e.wait_ge(tile_done, M_KV)
            kp = a["cache_k"].rearrange("n s h d -> n s (h d)")
            vp = a["cache_v"].rearrange("n s h d -> n s (h d)")

            def load_pages(s, src, b):
                for g in range(NPG):
                    page = e.value_load(ptab[0:1, bass.ds(b * NPG + g, 1)], min_val=0, max_val=src.shape[0] - 1)
                    e.dma_start(pgs[:, s, g:g + 1, :], src[bass.ds(page, 1)].rearrange("n s c -> s n c"))\
                        .then_inc(pg_in[s], 16)

            for b in range(2):
                load_pages(b, kp, b)
            with e.Fori(0, 2) as i:
                for j in range(2):
                    e.wait_ge(w_lo, i * 2 + (U_Q + j - 1))
                    load_whole((U_Q + j) % 2, a["w_q_b"][0], i * (4 * P) + j * 2 * P)
            for i in range(2):
                e.wait_ge(w_lo, U_OUTB + i - 1)
                load_whole((U_OUTB + i) % 2, a["w_out_b"][0], i * 2 * P)
            with e.Fori(1, B // 2) as i:
                for j in range(2):
                    e.wait_ge(tp_done, i * 6 + (TP_PG + 3 * j - 3))
                    load_pages(j, kp, i * 2 + j)
            for j in range(2):
                e.wait_ge(tp_done, TP_PG + 3 * (B - 2 + j) + 3)
                load_pages(j, vp, j)
            with e.Fori(1, B // 2) as i:
                for j in range(2):
                    e.wait_ge(pg_used, i * 2 + (j - 1))
                    load_pages(j, vp, i * 2 + j)
            e.wait_ge(sb_pv, NH)
            mem_loads(1)
            for i in range(2, 4):
                e.wait_ge(w_lo, U_OUTB + i - 1)
                load_whole((U_OUTB + i) % 2, a["w_out_b"][0], i * 2 * P)

            def load_rows(blk):
                e.dma_start(gtok[:, 0:1, :], xs_t[bass.ds(blk, 1), 0:P, :].rearrange("o c d -> c o d"))\
                    .then_inc(gt_in, 16)
                e.dma_start(gtok[0:CB, 1:2, :], xs_t[bass.ds(blk, 1), P:C, :].rearrange("o c d -> c o d"))\
                    .then_inc(gt_in, 16)

            e.wait_ge(slots_ready, 1)
            nj = e.value_load(jobi[0:1, MAXJOBS:MAXJOBS + 1], min_val=E, max_val=MAXJOBS)
            e.wait_ge(tile_done, M_END)
            e.wait_ge(ys_zero, 16)
            e.wait_ge(xs_in, 160)
            e.sem_inc(ys_out, 16)

            with e.Fori(0, nj) as j:
                ex = e.value_load(jobi[0:1, bass.ds(j, 1)], min_val=0, max_val=E - 1)
                for u in range(PER_JOB):
                    s = u % RAW
                    e.wait_ge(ew_lo, j * PER_JOB + (u + 1))
                    if u < KE:
                        v = eraw[:, s, :].rearrange("p (k j n) -> p k j n", k=KD, j=2)
                        for t, w in enumerate((a["w_gate_e"][0], a["w_up_e"][0])):
                            e.dma_start(v[:, :, t, :],
                                        w[bass.ds(ex, 1)].rearrange("o (k p) n -> p (o k) n", p=P)[:, :, u * P:(u + 1) * P])\
                                .then_inc(ew_in[s], 16)
                    else:
                        n, k0 = DN_CUTS[u - KE], DN_K0[u - KE]
                        v = eraw[:, s, 0:n * D].rearrange("p (k h n) -> p k h n", k=n, h=2)
                        src = a["w_down_e"][0][bass.ds(ex, 1)].rearrange("o (k p) n -> p (o k) n", p=P)
                        for h in range(2):
                            e.dma_start(v[:, :, h, :], src[:, k0:k0 + n, h * 512:(h + 1) * 512]).then_inc(ew_in[s], 16)
                    if u == 4:
                        e.wait_ge(er_done, j * 4 + 4)
                        load_rows(j + 2)
                    if u == 10:
                        e.wait_ge(ey_ready, j * 4 + 4)
                        e.dma_start(ys_t[bass.ds(j, 1), 0:P, :].rearrange("o c d -> c o d"), etok[:, 0:1, :])\
                            .then_inc(ys_out, 16)
                        e.dma_start(ys_t[bass.ds(j, 1), P:C, :].rearrange("o c d -> c o d"), etok[P - CB:P, 1:2, :])\
                            .then_inc(ys_out, 16)
            e.wait_ge(ey_ready, nj * 4 + 4)
            e.dma_start(ys_t[bass.ds(nj, 1), 0:P, :].rearrange("o c d -> c o d"), etok[:, 0:1, :]).then_inc(ys_out, 16)
            e.dma_start(ys_t[bass.ds(nj, 1), P:C, :].rearrange("o c d -> c o d"), etok[P - CB:P, 1:2, :]).then_inc(ys_out, 16)
            e.wait_ge(ed_done, nj + 1)
            e.wait_ge(ys_out, nj * 32 + 48)
            e.sem_inc(ys_ready, 1)
            e.dma_start(gpost[:, :], row_broadcast(a["g_post_ffn"][1], [[1, D]])).then_inc(gp_in, 16)
            for i in range(NT):
                e.wait_ge(f_y, i + 1)
                e.dma_start(y_prompt[0, i * P:(i + 1) * P, :], fo[:, i, :]).then_inc(y_out, 16)
            e.wait_ge(f_y, NT + 1)
            e.dma_start(y_sample.rearrange("b s d -> (b s) d"), fo[0:B, NT, :]).then_inc(y_out, 16)
            e.wait_ge(y_out, 16 * (NT + 1))
            e.wait_ge(outs, 48)
            e.wait_ge(kv_out, 64)

        @block.gpsimd
        def _(e):
            e.memset(ident[:, :], 0.0).then_inc(const_ready, 1)
            e.memset(zero[:, :], 0.0).then_inc(const_ready, 1)
            e.memset(eps[:, :], EPS).then_inc(const_ready, 1)
            e.memset(ones[:, :], 1.0).then_inc(const_ready, 1)
            e.memset(negone[:, :], -1.0).then_inc(const_ready, 1)
            e.memset(negtri[:, :], -1.0).then_inc(const_ready, 1)
            e.memset(before[:, :], 1.0).then_inc(const_ready, 1)
            e.wait_ge(const_ready, 7)
            e.affine_select(out=ident[:, :], in_=ident[:, :], compare_op=ALU.not_equal, fill=1.0, base=0,
                            pattern=[[-1, P]], channel_multiplier=1).then_inc(const_ready, 1)
            e.affine_select(out=negtri[:, :], in_=negtri[:, :], compare_op=ALU.is_ge, fill=0.0, base=0,
                            pattern=[[-1, P]], channel_multiplier=1).then_inc(const_ready, 1)
            e.affine_select(out=before[:, :], in_=before[:, :], compare_op=ALU.is_gt, fill=0.0, base=0,
                            pattern=[[1, P]], channel_multiplier=-1).then_inc(const_ready, 1)

            def lo_of(g):
                s = g % 2
                e.wait_ge(w_hi, g + 1)
                e.tensor_tensor(out=wlo[:, s, :], in0=raw[:, s, :], in1=whi[:, s, :].bitcast(F32), op=ALU.subtract).then_inc(w_lo, 1)

            def lo_of_at(c, i, n):
                s = c % 2
                e.wait_ge(w_hi, i * n + (c + 1))
                e.tensor_tensor(out=wlo[:, s, :], in0=raw[:, s, :], in1=whi[:, s, :].bitcast(F32), op=ALU.subtract).then_inc(w_lo, 1)

            def lo_tiles(t0, ks):
                for n, k in enumerate(ks):
                    t = t0 + n
                    e.wait_ge(hi_ready, HI_AT[t] + 1)
                    e.tensor_tensor(out=hl[:, k, :], in0=tmp[:, t % NTMP, :],
                                           in1=hh[:, k, :].bitcast(F32), op=ALU.subtract)\
                     .then_inc(tmp_used, 1)

            def add_tiles(t0):
                for k in range(KD):
                    t = t0 + k
                    e.wait_ge(tmp_ready, t + 1)
                    e.tensor_tensor(out=x[:, k, :], in0=tmp[:, t % NTMP, :], in1=x[:, k, :], op=ALU.add).then_inc(tmp_used, 1)

            lo_of(0)
            lo_tiles(T_N0, range(KD))
            for g in range(U_MEM, U_IN):
                lo_of(g + 1)
            e.wait_ge(mkv_out, 64)
            for i in range(2):
                e.memset(ubuf[:, 3 * i:3 * i + 3, 0:PAST], 0.0).then_inc(u_ready, 1)
            with e.Fori(0, 3) as i:
                for j in range(2):
                    lo_of_at(U_IN + j + 1, i, 2)
                    e.wait_ge(tile_free[0], i * 2 + (M_IN // 2 + j + 1))
                    e.wait_ge(tile_free[1], i * 2 + (M_IN // 2 + j + 1))
                    e.tensor_tensor(out=ubuf[:, bass.ds(i * 2 + j, 1), PAST:PAST + T],
                                           in0=tmp[:, 2 + j:3 + j, :], in1=tmp[:, j:j + 1, :], op=ALU.mult).then_inc(u_ready, 1)
            lo_of(U_OUTA)

            def mem_pool(layer):
                if layer == 0:
                    e.wait_ge(tile_done, M_IN)
                else:
                    e.wait_ge(sb_pv, NH)
                e.memset(mem[layer].qz[:, :, :], 0.0).then_inc(mqz_zero, 1)

            mem_pool(0)
            f = FS - 1
            e.wait_ge(u_ready, 2 + FS)
            e.wait_ge(tp_free[(TP_ST + 2) % 2], (TP_ST + 2) // 2 + 1)
            e.tensor_scalar(cT[:, f, 0:TP], ubuf[:, f, 0:TP], cwT[:, 0, f:f + 1], gT[:, G_CB + f:G_CB + f + 1],
                            ALU.mult, ALU.add).then_inc(cvp, 1)
            e.sem_inc(cvp, 1)
            cwf = cwT[:, :, :].rearrange("p j f -> p (j f)")
            with e.Fori(1, CW) as j:
                e.wait_ge(cvp, j * 2)
                e.tensor_tensor(cprod[:, :], ubuf[:, f, bass.ds(j, TP)], cwf[:, bass.ds(j * FS + f, 1)].to_broadcast([P, TP]),
                                ALU.mult).then_inc(cvp, 1)
                e.wait_ge(cvp, j * 2 + 1)
                e.tensor_tensor(cT[:, f, 0:TP], cT[:, f, 0:TP], cprod[:, :], ALU.add).then_inc(cvp, 1)
            lo_tiles(T_MIXA, MIX_A)
            for g in range(U_OUTA, U_GU):
                lo_of(g + 1)
            add_tiles(T_P0)
            lo_tiles(T_N1, range(KD))

            def lo_hidden(i, j):
                e.wait_ge(ga_hi, i * 2 + (j + 1))
                e.tensor_tensor(out=actl[:, bass.ds(i * 2 + j, 1), :], in0=tmp[:, 2 + j:3 + j, :],
                                       in1=acth[:, bass.ds(i * 2 + j, 1), :].bitcast(F32), op=ALU.subtract).then_inc(ga_lo, 1)

            with e.Fori(0, KF // 2) as i:
                for j in range(2):
                    lo_of_at(U_GU + j + 1, i, 2)
                    lo_hidden(i, j)
            with e.Fori(0, 2) as i:
                for j in range(6):
                    lo_of_at(U_DN + j + 1, i, 6)
            add_tiles(T_P1)
            lo_tiles(T_N2, range(KD))
            with e.Fori(0, 3) as i:
                for j in range(2):
                    lo_of_at(U_KV + j + 1, i, 2)
            lo_tiles(T_N3, range(KD))
            with e.Fori(0, 2) as i:
                for j in range(2):
                    lo_of_at(U_Q + j + 1, i, 2)
            e.wait_ge(kv_out, 64)
            e.memset(qd2[:, :, :, :], 0.0).then_inc(qd_zero, 1)

            def keep_past(buf, ready):
                for i in range(NT):
                    blk = buf[:, SEG_AT[i]:SEG_AT[i] + P]
                    e.affine_select(out=blk, in_=blk, compare_op=ALU.is_gt, fill=0.0, base=0,
                                    pattern=[[1, P]], channel_multiplier=-1).then_inc(ready, 1)

            for h in range(NH + 1):
                if h < NH:
                    e.wait_ge(sb_s, h + 1)
                    keep_past(sp[h % 2], sb_sp)
                if h >= 1:
                    e.wait_ge(sb_w, h)
                    keep_past(wt[(h - 1) % 2], sb_wm)
                    if h % 2 == 1 and h >= 3:
                        lo_tiles(T_MIXB + (h - 3) // 2, [(h - 3) // 2])
            lo_tiles(T_MIXB + FS - 1, [FS - 1])
            mem_pool(1)
            lo_tiles(T_MIXB + FS, [6, 7])
            for g in range(U_OUTB, U_END - 1):
                lo_of(g + 1)
            add_tiles(T_P2)

            e.wait_ge(tile_done, M_END)
            e.wait_ge(tmp_used, T_P2 + KD)
            e.iota(ioe[:, :, :], pattern=[[0, NT + 1], [1, E]], base=0, channel_multiplier=0).then_inc(io_int, 1)
            e.iota(ioi[:, :, :], pattern=[[1, MAXJOBS], [0, E]], base=0, channel_multiplier=0).then_inc(io_int, 1)
            e.memset(valid[:, :], 1.0).then_inc(io_int, 1)
            e.wait_ge(io_int, 3)
            e.tensor_copy(io8[:, :, :], ioe[:, :, :]).then_inc(io_ready, 1)
            e.tensor_copy(ioj[:, :, :], ioi[:, :, :]).then_inc(io_ready, 1)
            e.affine_select(out=valid[:, NT:NT + 1], in_=valid[:, NT:NT + 1], compare_op=ALU.is_ge, fill=0.0,
                            base=B - 1, pattern=[[0, 1]], channel_multiplier=-1).then_inc(io_ready, 1)
            e.wait_ge(slots_ready, 1)
            e.wait_ge(xs_zero, 64)
            for i in range(NT + 1):
                n = P if i < NT else B
                copied_out(e, TP_HT + 2 * i)
                copied_out(e, TP_HT + 2 * i + 1)
                for s in range(2):
                    e.indirect_dma_start(out=xs, out_offset=bass.IndirectOffsetOnAxis(ap=sloti[0:n, s, i:i + 1], axis=0),
                                         in_=htok[0:n, i, :], in_offset=None).then_inc(xs_in, 16)
            e.wait_ge(xs_in, 160)
            e.dma_start(gtok[:, 0, :], xs[C:C + P, :]).then_inc(g0_in, 16)
            e.dma_start(gtok[0:CB, 1, :], xs[C + P:2 * C, :]).then_inc(g0_in, 16)
            nj = e.value_load(jobi[0:1, MAXJOBS:MAXJOBS + 1], min_val=E, max_val=MAXJOBS)
            e.sem_inc(ea_lo, 1)
            with e.Fori(0, nj) as j:
                for m in range(KE):
                    e.wait_ge(ea_hi, j * KE + (m + 1))
                    e.tensor_tensor(out=eal[:, m, :], in0=eat[:, m % 2, :],
                                           in1=eah[:, m, :].bitcast(F32), op=ALU.subtract)\
                     .then_inc(ea_lo, 1)
            e.wait_ge(ys_ready, 1)
            for i in range(NT + 1):
                n = P if i < NT else B
                for s in range(2):
                    e.indirect_dma_start(out=yr[0:n, i, s, :], out_offset=None, in_=ys,
                                         in_offset=bass.IndirectOffsetOnAxis(ap=sloti[0:n, s, i:i + 1], axis=0))\
                     .then_inc(yr_in[i], 16)

        @block.scalar
        def _(e):
            def hi_of(g):
                s = g % 2
                e.wait_ge(w_in[s], 32 * (g // 2 + 1))
                if g >= 2:
                    e.wait_ge(tile_done, 2 * (g - 1) if g < U_DN else M_KV + 2 * (g - 1 - U_KV))
                e.activation(whi[:, s, :], raw[:, s, :], ACT.Copy).then_inc(w_hi, 1)

            def hi_of_at(c, i, n):
                s = c % 2
                e.wait_ge(w_in[s], i * (16 * n) + 32 * (c // 2 + 1))
                e.wait_ge(tile_done, i * (2 * n) + (2 * (c - 1) if c <= U_DN else M_KV + 2 * (c - 1 - U_KV)))
                e.activation(whi[:, s, :], raw[:, s, :], ACT.Copy).then_inc(w_hi, 1)

            def hi_tile(t, k):
                e.wait_ge(tmp_ready, t + 1)
                e.activation(hh[:, k, :], tmp[:, t % NTMP, :], ACT.Copy).then_inc(hi_ready, 1)

            def square(q, src):
                if q >= 2:
                    e.wait_ge(sq_used, q - 1)
                e.activation(sq[:, q % 2, :] if src is not None else halves(sq[:, q % 2, :]),
                             src if src is not None else zero[:, :].unsqueeze(1).to_broadcast([P, 2, HALF]),
                             ACT.Square).then_inc(sq_ready, 1)

            def root(n):
                e.wait_ge(sq_used, SUM_END[n])
                e.activation(halves(rstd[:, :]), ps[:, 4:6, 0:HALF], ACT.Sqrt, scale=1.0 / D, bias=eps[:, :])\
                 .then_inc(root_ready, 1)

            e.wait_ge(const_ready, 7)
            e.wait_ge(mem_in, 16)
            for i in range(MT):
                e.activation(mT[:, 4 * i:4 * i + 4, :].rearrange("p k n -> p (k n)"), memtok[:, i, :], ACT.Square,
                             accum_out=ms[:, i:i + 1]).then_inc(mem_ss, 1)
            e.wait_ge(mem_ss, 2)
            e.activation(ms[:, 2:4], ms[:, 0:2], ACT.Sqrt, scale=1.0 / D, bias=eps[:, :]).then_inc(mem_root, 1)
            copied_out(e, TP_X + KD - 1)
            copied_out(e, TP_X + KD)
            for k in range(KD):
                square(S_X0 + k, x[:, k, :])
            root(0)
            for layer in range(2):
                for k in range(KD):
                    copied_out(e, TP_MEM + k // 2)
                    e.activation(hmh[:, layer, k, :], mT[:, k, :], ACT.Copy, scale=gain(G_MEM + 8 * layer, k))\
                     .then_inc(hm_hi, 1)
            hi_of(0)
            for k in range(KD):
                hi_tile(T_N0 + k, k)
            for g in range(U_MEM, U_IN):
                hi_of(g + 1)
            with e.Fori(0, 3) as i:
                for j in range(2):
                    hi_of_at(U_IN + j + 1, i, 2)
                    e.wait_ge(u_ready, i * 2 + (j + 1))
                    e.wait_ge(tile_done, i * 4 + (M_IN + 2 * j + 1))
                    e.activation(halves(tmp[:, 2 + j, :]), pair(0), ACT.Copy).then_inc(tile_free[0], 1)
                    e.wait_ge(tile_done, i * 4 + (M_IN + 2 * j + 2))
                    e.activation(halves(tmp[:, j, :]), pair(1), ACT.Sigmoid).then_inc(tile_free[1], 1)
            hi_of(U_OUTA)
            for t in range(FM):
                e.wait_ge(tile_done, M_QM + t + 1)
                e.activation(halves(qmA[:, t, :]), pair(t), ACT.Copy, scale=HD ** -0.5).then_inc(tile_free[t], 1)
            for n, (lo, hi) in enumerate(((0, 4), (4, 6))):
                f = TP_UT + n
                e.wait_ge(tp_done, f + 1)
                e.activation(utail[0:PAST + B, lo * P:hi * P], ps[0:PAST + B, 6 + f % 2, 0:(hi - lo) * P], ACT.Copy)\
                 .then_inc(tp_free[f % 2], 1)

            def mem_act(layer):
                m = mem[layer]
                f = (TP_MA, TP_MB)[layer]
                e.wait_ge(tp_done, f + 1)
                e.activation(m.kT[:, :, :].rearrange("p f n -> p (f n)"), ps[:, 6 + f % 2, :], ACT.Copy)\
                 .then_inc(tp_free[f % 2], 1)
                for b in range(0, B, 1 + layer):
                    e.wait_ge(tp_done, f + b + 2)
                    e.activation(m.cT[:, b, :, :].rearrange("p f n -> p (f n)"), ps[:, 6 + (f + b + 1) % 2, :], ACT.Copy)\
                     .then_inc(tp_free[(f + b + 1) % 2], 1)
                e.wait_ge(md_max, layer + 1)
                e.activation(m.pd[:, :], ps[0:32, 4, 0:NMEM], ACT.Exp, bias=stm[0:32, 0, 0:1],
                             accum_out=sts[0:32, 0, 0:1]).then_inc(md_e, 1)
                for h in range(MH + 1):
                    if h < MH:
                        s = h % 2
                        e.wait_ge(mp_max, MH * layer + h + 1)
                        for i in range(NT):
                            ins = e.activation(m.p[:, s, i, :], ps[:, 2 * s + i // 2, (i % 2) * NMEM:(i % 2 + 1) * NMEM],
                                               ACT.Exp, bias=stm[:, s, i:i + 1], accum_out=sts[:, s, i:i + 1])
                            ins.then_inc(mp_e, 1)
                    if h >= 1:
                        e.wait_ge(mp_t, MH * layer + h)
                        e.wait_ge(mp_o, MH * layer + h - 1)
                        e.activation(m.pT[:, 0, :], ps[:, 4, :], ACT.Copy).then_inc(mp_pT, 1)

            mem_act(0)
            hi_tile(T_MIXA, 6)
            hi_tile(T_MIXA + 1, 7)
            for k in range(FS):
                e.wait_ge(ln_xc, k + 1)
                if k >= 2:
                    e.wait_ge(ln_used, k - 1)
                e.activation(sq[:, k % 2, :], cT[:, k, :], ACT.Square).then_inc(ln_sq, 1)
            e.wait_ge(ln_used, FS)
            e.activation(halves(rstd[:, :]), ps[:, 4:6, 0:HALF], ACT.Sqrt, scale=1.0 / (FS * P), bias=eps[:, :])\
             .then_inc(ln_root, 1)
            for k in range(FS):
                t = T_MIXA + 2 + k
                e.wait_ge(ln_y, k + 1)
                e.wait_ge(tmp_used, t - NTMP + 1)
                e.activation(tmp[:, t % NTMP, :], cT[:, k, :], ACT.Silu, scale=gT[:, G_LNG + k:G_LNG + k + 1],
                             bias=gT[:, G_LNB + k:G_LNB + k + 1]).then_inc(tmp_ready, 1)
                hi_tile(t, k)

            def y_squares(q0, m0, y, ks):
                for k in ks:
                    e.wait_ge(tile_free[k % 2], (m0 + k) // 2 + 1)
                    square(q0 + 2 + k, y[:, k, :])

            def x_squares(q0, t0):
                for k in range(KD):
                    e.wait_ge(tmp_used, t0 + k + 1)
                    square(q0 + k, x[:, k, :])

            square(S_YA, None)
            square(S_YA + 1, None)
            for g in range(U_OUTA, U_GU):
                hi_of(g + 1)
                y_squares(S_YA, M_OUTA, y_mix, (2 * (g - U_OUTA), 2 * (g - U_OUTA) + 1))
            nfill = SLOTS * D // P // 256
            xsz = xs.rearrange("s d -> (s d)").rearrange("(p a n) -> p a n", p=P, n=256)
            for i in range(4):
                lo, hi = nfill * i // 4, nfill * (i + 1) // 4
                e.dma_start(xsz[:, lo:hi, :], zero[:, 0:256].unsqueeze(1).to_broadcast([P, hi - lo, 256]))\
                 .then_inc(xs_zero, 16)
            nfill = (MAXJOBS + 1 - E) * C * D // P // 256
            ysz = ys[(E + 1) * C:SLOTS, :].rearrange("s d -> (s d)").rearrange("(p a n) -> p a n", p=P, n=256)
            e.dma_start(ysz, zero[:, 0:256].unsqueeze(1).to_broadcast([P, nfill, 256])).then_inc(ys_zero, 16)
            root(1)
            x_squares(S_XA, T_P0)
            root(2)
            for k in range(KD):
                hi_tile(T_N1 + k, k)

            def hidden(i, j, first):
                if not first:
                    e.wait_ge(tile_free[1], i * 2 + (M_GU // 2 + j - 1))
                e.wait_ge(tile_done, i * 4 + (M_GU + 2 * j + 1))
                e.activation(halves(tmp[:, j, :]), pair(0), ACT.Silu).then_inc(tile_free[0], 1)
                e.wait_ge(tile_free[1], i * 2 + (M_GU // 2 + j + 1))
                e.activation(acth[:, bass.ds(i * 2 + j, 1), :], tmp[:, 2 + j:3 + j, :], ACT.Copy).then_inc(ga_hi, 1)

            for j in range(2):
                hi_of(U_GU + j + 1)
                hidden(0, j, True)
            with e.Fori(1, KF // 2) as i:
                for j in range(2):
                    hi_of_at(U_GU + j + 1, i, 2)
                    hidden(i, j, False)
            square(S_YF, None)
            square(S_YF + 1, None)
            with e.Fori(0, 2) as i:
                for j in range(6):
                    c = U_DN + j + 1
                    e.wait_ge(w_in[c % 2], i * 96 + 32 * (c // 2 + 1))
                    if j % 3 == 0:
                        e.wait_ge(tile_done, i * 4 + (M_DN + 2 * (j // 3)))
                    else:
                        e.wait_ge(w_used, i * 4 + (2 * (j // 3) + j % 3))
                    e.activation(whi[:, c % 2, :], raw[:, c % 2, :], ACT.Copy).then_inc(w_hi, 1)
                    if j % 3 == 2:
                        for t in range(2):
                            k = 2 * (j // 3) + t
                            e.wait_ge(tile_free[t], i * 2 + ((M_DN + k) // 2 + 1))
                            e.wait_ge(sq_used, i * 4 + (S_YF + 2 + k - 1))
                            e.activation(sq[:, k % 2:k % 2 + 1, :], y_dn[:, bass.ds(i * 4 + k, 1), :], ACT.Square)\
                             .then_inc(sq_ready, 1)
            root(3)
            x_squares(S_XF, T_P1)
            root(4)
            for k in range(KD):
                hi_tile(T_N2 + k, k)
            with e.Fori(0, 3) as i:
                for j in range(2):
                    hi_of_at(U_KV + j + 1, i, 2)
            for n in range(0, 20, 2):
                f, dst, src = kv_fill(n)
                e.wait_ge(tp_done, f + 1)
                e.activation(dst, src, ACT.Copy).then_inc(tp_free[f % 2], 1)
                if n == 4:
                    e.wait_ge(tile_done, M_Q)
                    for k in range(KD):
                        hi_tile(T_N3 + k, k)
            copied_out(e, TP_KV + 18)
            copied_out(e, TP_KV + 19)
            e.dma_start(v_prompt[0].rearrange("(i p) h d -> p i (h d)", p=P), vtok[:, :, :]).then_inc(kv_out, 16)
            e.dma_start(k_prompt[0].rearrange("(i p) h d -> p i (h d)", p=P), ktok[:, :, :]).then_inc(kv_out, 16)
            e.dma_start(v_sample.rearrange("b s h d -> b (s h d)"), kvdec[0:B, 0, :]).then_inc(kv_out, 16)
            e.dma_start(k_sample.rearrange("b s h d -> b (s h d)"), kvdec[0:B, 1, :]).then_inc(kv_out, 16)
            with e.Fori(0, 2) as i:
                for j in range(2):
                    hi_of_at(U_Q + j + 1, i, 2)
            e.wait_ge(kv_out, 64)
            for n in range(1, 3 * B, 2):
                f, b, c = TP_PG + n, n // 3, n % 3
                e.wait_ge(tp_done, f + 1)
                if b >= 2:
                    e.wait_ge(pg_qk, b - 1)
                e.activation(pgT[:, b % 2, 2 * c:2 * c + 2, :].rearrange("p f n -> p (f n)"), ps[:, 6 + f % 2, :],
                             ACT.Copy).then_inc(tp_free[f % 2], 1)
            e.wait_ge(sd_zc, 1)
            e.activation(zd[:, 1, :], zd[:, 1, :], ACT.Exp).then_inc(sd_e, 1)
            e.wait_ge(sd_e, 1)
            e.activation(zd[:, 1, :], zd[:, 1, :], ACT.Ln, bias=ones[:, 0:1]).then_inc(sd_l, 1)
            e.wait_ge(sd_x, 1)
            e.activation(zd[:, 3, :], zd[:, 0, :], ACT.Exp).then_inc(sd_w, 1)
            for h in range(NH + 1):
                if h < NH:
                    c = zc[h % 2]
                    e.wait_ge(sb_zc, h + 1)
                    e.activation(c[:, :], c[:, :], ACT.Exp).then_inc(sb_e, 1)
                    e.wait_ge(sb_e, h + 1)
                    e.activation(c[:, :], c[:, :], ACT.Ln, bias=ones[:, 0:1]).then_inc(sb_l, 1)
                if h >= 1:
                    e.wait_ge(sb_c, h)
                    if h >= 3:
                        e.wait_ge(sb_pv, h - 2)
                    g = h - 1
                    e.activation(wt[g % 2][:, :], flat[:, 1536 * (g % 2):1536 * (g % 2) + SEG], ACT.Exp,
                                 bias=bias[:, 0, g:g + 1]).then_inc(sb_w, 1)
                    if h % 2 == 1 and h >= 3:
                        hi_tile(T_MIXB + (h - 3) // 2, (h - 3) // 2)
            hi_tile(T_MIXB + FS - 1, FS - 1)
            mem_act(1)
            hi_tile(T_MIXB + FS, 6)
            hi_tile(T_MIXB + FS + 1, 7)
            square(S_YB, None)
            square(S_YB + 1, None)
            for g in range(U_OUTB, U_END):
                if g + 1 < U_END:
                    hi_of(g + 1)
                y_squares(S_YB, M_OUTB, y_mix, (2 * (g - U_OUTB), 2 * (g - U_OUTB) + 1))
            root(5)
            x_squares(S_XB, T_P2)
            root(6)

            e.wait_ge(rr_m1, 1)
            e.activation(rt[:, 6, :, :], rt[:, 2, :, :], ACT.Exp).then_inc(rr_exp, 1)
            for n in range(20):
                f = TP_HT + n
                dst, i = ((htok, xtk)[n // 10], (n % 10) // 2)
                rows_ = P if i < NT else B
                e.wait_ge(tp_done, f + 1)
                e.activation(dst[0:rows_, i, 512 * (n % 2):512 * (n % 2) + 512], ps[0:rows_, 6 + f % 2, :], ACT.Copy)\
                 .then_inc(tp_free[f % 2], 1)

            e.wait_ge(slots_ready, 1)
            nj = e.value_load(jobi[0:1, MAXJOBS:MAXJOBS + 1], min_val=E, max_val=MAXJOBS)

            def expert_hi(j, u):
                s = u % SPLIT
                n = 2048 if u < KE else DN_CUTS[u - KE] * D
                e.wait_ge(ew_in[u % RAW], j * (32 * PER_JOB // RAW) + 32 * (u // RAW + 1))
                v = u - SPLIT
                if v == -1:
                    e.wait_ge(ed_done, j + 1)
                elif 0 <= v < KE:
                    e.wait_ge(eg_done, j * (2 * KE) + (2 * v + 2))
                else:
                    per = len(DN_CUTS) - 1
                    e.wait_ge(ew_used, j * per + (per + v + 2 if v < 0 else per + v - KE + 1))
                e.activation(ewh[:, s, 0:n], eraw[:, u % RAW, 0:n], ACT.Copy).then_inc(ew_hi, 1)

            def rows_hi(c, filled):
                e.wait_ge(er_done, filled)
                e.activation(ejx[:, 2 * c:2 * c + 2, 0, :],
                             ps[:, EB[eb_at(2 * KE + c)[0]], 0:2 * C].rearrange("p (k n) -> p k n", k=2),
                             ACT.Copy).then_inc(ej_hi, 1)

            for c in range(4):
                rows_hi(c, c + 1)
            with e.Fori(0, nj) as j:
                expert_hi(j, 0)
                expert_hi(j, 1)
                for u in range(PER_JOB):
                    if u + 2 < PER_JOB:
                        expert_hi(j, u + 2)
                    if 1 <= u <= KE:
                        v = u - 1
                        q, n = eb_at(2 * v)
                        e.wait_ge(eb_free[q], j * EB_USES[q] + (n + 2))
                        e.activation(esg[:, v % 2, :], esg[:, v % 2, :], ACT.Silu).then_inc(eg_silu, 1)
                    if 2 <= u <= KE + 1:
                        v = u - 2
                        if v == 0:
                            e.wait_ge(ed_done, j + 1)
                        e.wait_ge(ea_tmp, j * KE + (v + 2))
                        e.activation(eah[:, v, :], eat[:, v % 2, :], ACT.Copy).then_inc(ea_hi, 1)
                    if u == KE + 1:
                        for c in range(4):
                            rows_hi(c, j * 4 + (4 + c + 1))
            for i in range(NT + 2):
                if i <= NT:
                    n = P if i < NT else B
                    e.wait_ge(yr_in[i], 32)
                    e.activation(fo[0:n, i, :], yr[0:n, i, 0, :], ACT.Copy, scale=gate[0:n, 0, i:i + 1]).then_inc(f_1, 1)
                if i >= 1:
                    t = i - 1
                    n = P if t < NT else B
                    e.wait_ge(f_2, t + 1)
                    e.activation(fs[0:n, t % 2, :], fo[0:n, t, :], ACT.Square, accum_out=frs[0:n, t, 0:1]).then_inc(f_ss, 1)
                    e.wait_ge(f_ss, t + 1)
                    e.activation(frs[0:n, t, 1:2], frs[0:n, t, 0:1], ACT.Sqrt, scale=1.0 / D, bias=eps[0:n, :])\
                     .then_inc(f_root, 1)

        @block.vector
        def _(e):
            def copy_out(f, dst, src):
                e.wait_ge(tp_done, f + 1)
                e.tensor_copy(dst, src).then_inc(tp_free[f % 2], 1)

            def bank(f):
                return 6 + f % 2

            def inverse(n):
                e.wait_ge(root_ready, n + 1)
                e.reciprocal(rstd[:, :], rstd[:, :]).then_inc(rstd_ready, 1)
                e.wait_ge(rstd_ready, n + 1)

            def norm_tiles(t0, src, off):
                for k in range(KD):
                    t = t0 + k
                    if t >= NTMP:
                        e.wait_ge(tmp_used, t - NTMP + 1)
                    e.scalar_tensor_tensor(out=tmp[:, t % NTMP, :], in0=src[:, k, :], scalar=gain(off, k), in1=rstd[:, :],
                                           op0=ALU.mult, op1=ALU.mult).then_inc(tmp_ready, 1)

            copy_out(TP_CTL, gT[:, :], ps[:, bank(TP_CTL), 0:G_ROWS])
            copy_out(TP_CTL + 1, cwT[:, :, :].rearrange("p j f -> p (j f)"), ps[:, bank(TP_CTL + 1), 0:CW * FS])
            e.wait_ge(mem_root, 1)
            e.reciprocal(ms[:, 2:4], ms[:, 2:4]).then_inc(mem_inv, 1)
            e.wait_ge(mem_inv, 1)
            for i in range(MT):
                e.tensor_scalar(memtok[:, i, :], memtok[:, i, :], ms[:, 2 + i:3 + i], None, ALU.mult).then_inc(mem_sc, 1)
            for k in range(KD):
                copy_out(TP_X + k, x[:, k, 0:TP], ps[:, bank(TP_X + k), :])
            f = TP_X + KD
            copy_out(f, x[:, :, TP:T], ps[:, bank(f), 0:KD * B].rearrange("p (k b) -> p k b", k=KD))
            for c in range(4):
                f = TP_MEM + c
                copy_out(f, mT[:, 2 * c:2 * c + 2, :], ps[:, bank(f), :].rearrange("p (k m) -> p k m", k=2))
            for layer in range(2):
                for k in range(KD):
                    e.wait_ge(hm_hi, KD * layer + k + 1)
                    e.scalar_tensor_tensor(out=hml[:, layer, k, :], in0=mT[:, k, :], scalar=gain(G_MEM + 8 * layer, k),
                                           in1=hmh[:, layer, k, :].bitcast(F32), op0=ALU.mult, op1=ALU.subtract)\
                     .then_inc(hm_lo, 1)
            inverse(0)
            norm_tiles(T_N0, x, G_PRE_MIX)
            for n in range(8):
                e.wait_ge(tile_done, M_MEM + n + 1)
                e.tensor_copy(mkv[:, n // 4, (n // 2) % 2, n % 2, :], ps[:, 2 * (n % 2), 0:NMEM])\
                 .then_inc(tile_free[n % 2], 1)
            for c in range(3):
                f = TP_ST + c
                for h in range(2):
                    e.wait_ge(tp_done, f + 1)
                    ins = e.tensor_copy(udec[:, 2 * c + h, :, 0:PAST],
                                        ps[:, bank(f), 240 * h:240 * h + 240].rearrange("p (b r) -> p b r", b=B))
                    if h == 0:
                        ins.then_inc(cd, 1)
                ins.then_inc(tp_free[f % 2], 1)

            def conv_start(f0, n):
                e.wait_ge(u_ready, 2 + f0 + n)
                for f in range(f0, f0 + n):
                    e.tensor_scalar(cT[:, f, 0:TP], ubuf[:, f, 0:TP], cwT[:, 0, f:f + 1], gT[:, G_CB + f:G_CB + f + 1],
                                    ALU.mult, ALU.add).then_inc(cv, 1)

            def conv_taps(f0, n, j0, j1):
                n0 = CW * f0
                with e.Fori(j0, j1) as j:
                    for t in range(n):
                        f = f0 + t
                        e.wait_ge(cv, j * n + (n0 + t + 1 - n))
                        e.scalar_tensor_tensor(out=cT[:, f, 0:TP], in0=ubuf[:, f, bass.ds(j, TP)],
                                               scalar=cwf[:, bass.ds(j * FS + f, 1)], in1=cT[:, f, 0:TP],
                                               op0=ALU.mult, op1=ALU.add).then_inc(cv, 1)

            def conv_decode():
                for f in range(FS):
                    e.tensor_copy(udec[:, f, :, PAST:CW], ubuf[:, f, PAST + TP:PAST + T].unsqueeze(2)).then_inc(ud_new, 1)
                for f in range(FS):
                    e.wait_ge(ud_new, FS)
                    if f == 0:
                        copied_out(e, TP_ST + 2)
                    if f >= 1:
                        e.wait_ge(cd, 3 + 2 * f)
                    e.tensor_tensor(ctmp[:, :, :], udec[:, f, :, :],
                                    cwT[:, :, f].unsqueeze(1).to_broadcast([P, B, CW]), ALU.mult).then_inc(cd, 1)
                    e.wait_ge(cd, 4 + 2 * f)
                    e.tensor_reduce(cT[:, f, TP:T], ctmp[:, :, :], AX, ALU.add).then_inc(cd, 1)
                e.wait_ge(cd, 3 + 2 * FS)
                for f in range(FS):
                    e.tensor_scalar(cT[:, f, TP:T], cT[:, f, TP:T], gT[:, G_CB + f:G_CB + f + 1], None, ALU.add)\
                     .then_inc(cd_sum, 1)

            def mem_dve(layer, q, t0, meanwhile=lambda: None):
                m = mem[layer]
                e.wait_ge(mqz_zero, layer + 1)
                e.wait_ge(tile_free[0], (M_OUTA if layer == 0 else M_OUTB) // 2)
                e.wait_ge(tile_free[1], (M_OUTA if layer == 0 else M_OUTB) // 2)
                qz = m.qz[:, :, :].rearrange("p a b -> p (a b)")
                for f in range(FM):
                    for h in range(2):
                        at0 = 34 * f + h
                        e.tensor_copy(qz[64 * h:64 * h + 64, at0:at0 + 68 * (B - 1) + 1:68],
                                      q[64 * h:64 * h + 64, f, TP:T]).then_inc(mqz_ready, 1)
                if layer == 1:
                    for b in range(1, B, 2):
                        f = TP_MB + 1 + b
                        copy_out(f, m.cT[:, b, :, :].rearrange("p f n -> p (f n)"), ps[:, 6 + f % 2, :])
                meanwhile()
                e.wait_ge(md_s, layer + 1)
                e.tensor_reduce(stm[0:32, 0, 0:1], ps[0:32, 4, 0:NMEM], AX, ALU.max, negate=True).then_inc(md_max, 1)
                e.wait_ge(md_e, layer + 1)
                e.reciprocal(sts[0:32, 0, 0:1], sts[0:32, 0, 0:1]).then_inc(md_inv, 1)
                e.wait_ge(md_inv, layer + 1)
                e.tensor_scalar(m.pd[:, :], m.pd[:, :], sts[0:32, 0, 0:1], None, ALU.mult).then_inc(md_p, 1)
                e.wait_ge(md_t, layer + 1)
                e.tensor_copy(m.pdT[:, :, :], ps[:, 5, 0:64].rearrange("p (m r) -> p m r", m=MT)).then_inc(md_pT, 1)
                e.wait_ge(md_o, layer + 1)
                o_ps = ps[:, 4, 0:2 * FM * B].rearrange("p (b f h) -> p h f b", b=B, f=FM)
                for h in range(2):
                    e.tensor_copy(od[64 * h:64 * h + 64, 0:FM, :], o_ps[64 * h:64 * h + 64, h, :, :]).then_inc(md_od, 1)
                for h in range(MH + 2):
                    if h < MH:
                        s = h % 2
                        e.wait_ge(mp_s, MH * layer + h + 1)
                        e.tensor_reduce(stm[:, s, :], flat[:, 1024 * s:1024 * s + 1024].rearrange("p (i n) -> p i n", i=NT),
                                        AX, ALU.max, negate=True).then_inc(mp_max, 1)
                        if h == 0:
                            meanwhile()
                    if 1 <= h <= MH:
                        g = h - 1
                        s = g % 2
                        e.wait_ge(mp_e, NT * (MH * layer + g + 1))
                        e.reciprocal(sts[:, s, :], sts[:, s, :]).then_inc(mp_inv, 1)
                        e.wait_ge(mp_inv, MH * layer + g + 1)
                        for i in range(NT):
                            e.tensor_scalar(m.p[:, s, i, :], m.p[:, s, i, :], sts[:, s, i:i + 1], None, ALU.mult)\
                             .then_inc(mp_p, 1)
                        meanwhile()
                        e.wait_ge(mp_t, MH * layer + g + 1)
                        e.wait_ge(mp_o, MH * layer + g)
                        e.tensor_copy(m.pT[:, 1, :], ps[:, 5, :]).then_inc(mp_pT, 1)
                    if h >= 2 and h % 2 == 1:
                        f = (h - 3) // 2
                        t = t0 + f
                        e.wait_ge(mp_o, MH * layer + h - 1)
                        e.wait_ge(md_od, 2 * layer + 2)
                        e.wait_ge(tmp_used, t - NTMP + 1)
                        e.tensor_copy(tmp[:, t % NTMP, TP:T], od[:, f, :]).then_inc(mp_out, 1)
                        e.wait_ge(mp_out, FM * layer + f + 1)
                        e.tensor_copy(tmp[:, t % NTMP, 0:TP], ps[:, 6 + f, :]).then_inc(tmp_ready, 1)

            cwf = cwT[:, :, :].rearrange("p j f -> p (j f)")
            conv_start(0, 2)
            conv_taps(0, 2, 1, CW)
            conv_start(2, 3)
            conv_taps(2, 3, 1, 7)
            parts = iter([(7 + 4 * n, 11 + 4 * n) for n in range(6)])
            mem_dve(0, qmA, T_MIXA, lambda: conv_taps(2, 3, *next(parts)))
            conv_decode()
            e.wait_ge(ln_sum, 1)
            e.tensor_scalar(halves(mean[:, :]), ps[:, 4:6, 0:HALF], 1.0 / (FS * P), None, ALU.mult).then_inc(ln_mean, 1)
            e.wait_ge(ln_mean, 1)
            for k in range(FS):
                e.tensor_tensor(cT[:, k, :], cT[:, k, :], mean[:, :], ALU.subtract).then_inc(ln_xc, 1)
            e.wait_ge(ln_root, 1)
            e.reciprocal(rstd[:, :], rstd[:, :]).then_inc(ln_rstd, 1)
            e.wait_ge(ln_rstd, 1)
            e.wait_ge(ln_sq, FS)
            for k in range(FS):
                e.tensor_tensor(cT[:, k, :], cT[:, k, :], rstd[:, :], ALU.mult).then_inc(ln_y, 1)

            def out_tiles(m0, y, n=KD):
                for k in range(n):
                    e.wait_ge(tile_done, m0 + k + 1)
                    e.tensor_copy(halves(y[:, k, :]), pair(k % 2)).then_inc(tile_free[k % 2], 1)

            out_tiles(M_OUTA, y_mix)
            inverse(1)
            norm_tiles(T_P0, y_mix, G_POST_MIX)
            inverse(2)
            norm_tiles(T_N1, x, G_PRE_FFN)

            def hidden(i, j, first):
                if not first:
                    e.wait_ge(ga_lo, i * 2 + (j - 1))
                e.wait_ge(tile_free[0], i * 2 + (M_GU // 2 + j + 1))
                e.wait_ge(tile_done, i * 4 + (M_GU + 2 * j + 2))
                e.tensor_tensor(halves(tmp[:, 2 + j, :]), pair(1), halves(tmp[:, j, :]), ALU.mult).then_inc(tile_free[1], 1)

            for j in range(2):
                hidden(0, j, True)
            with e.Fori(1, KF // 2) as i:
                for j in range(2):
                    hidden(i, j, False)
            with e.Fori(0, 2) as i:
                for k in range(4):
                    e.wait_ge(tile_done, i * 4 + (M_DN + k + 1))
                    e.tensor_copy(y_dn[:, bass.ds(i * 4 + k, 1), :].rearrange("p o (h n) -> p (o h) n", h=2), pair(k % 2))\
                     .then_inc(tile_free[k % 2], 1)
            inverse(3)
            norm_tiles(T_P1, y_dn, G_POST_FFN)
            inverse(4)
            norm_tiles(T_N2, x, G_KV)
            for m in range(2 * FS):
                e.wait_ge(tile_done, M_KV + m + 1)
                e.tensor_copy(halves((kT, vT)[m // FS][:, m % FS, :]), pair(m % 2)).then_inc(tile_free[m % 2], 1)
            def kv_rows(ns):
                for n in ns:
                    copy_out(*kv_fill(n))

            kv_rows((1, 3))
            norm_tiles(T_N3, x, G_PRE_MIX + 8)
            kv_rows(range(5, 20, 2))
            for m in range(KD):
                e.wait_ge(tile_done, M_Q + m + 1)
                e.tensor_scalar(halves(qT[:, m, :]), pair(m % 2), HD ** -0.5, None, ALU.mult)\
                 .then_inc(tile_free[m % 2], 1)

            e.wait_ge(qd_zero, 1)
            e.wait_ge(tile_free[0], M_OUTB // 2)
            e.wait_ge(tile_free[1], M_OUTB // 2)
            for h in range(2):
                e.tensor_copy(qd2[64 * h:64 * h + 64, :, :, h],
                              qT[64 * h:64 * h + 64, 0:FS, TP:T].rearrange("p f b -> p b f")).then_inc(qd_ready, 1)
            bias2 = bias[:, :, :].rearrange("p b h -> p (b h)").unsqueeze(1).to_broadcast([P, NPG, B * NH])

            def pages(ap):
                return ap.rearrange("p (g r) -> p g r", g=NPG)

            e.wait_ge(kv_out, 64)
            for n in range(0, 3 * B, 2):
                f, b, c = TP_PG + n, n // 3, n % 3
                if b >= 2:
                    e.wait_ge(pg_qk, b - 1)
                copy_out(f, pgT[:, b % 2, 2 * c:2 * c + 2, :].rearrange("p f n -> p (f n)"), ps[:, 6 + f % 2, :])
            e.wait_ge(small_in, 64)
            e.wait_ge(pg_qk, B)
            e.tensor_tensor(pages(zd[:, 0, :]), pages(ps[:, 0, 0:192]), bias2, ALU.add).then_inc(sd_zb, 1)
            e.wait_ge(sd_zb, 1)
            e.tensor_scalar(zd[:, 1, :], zd[:, 0, :], CLAMP, None, ALU.min).then_inc(sd_zc, 1)
            e.wait_ge(sd_l, 1)
            e.tensor_tensor(zd[:, 2, :], zd[:, 0, :], zd[:, 1, :], ALU.max).then_inc(sd_sp, 1)
            e.wait_ge(sd_c, 1)
            e.wait_ge(sd_sp, 1)
            e.tensor_tensor(pages(zd[:, 0, :]), pages(ps[:, 0, 0:192]), bias2, ALU.add).then_inc(sd_x, 1)
            e.wait_ge(pg_used, B)
            o_ps = ps[:, 1, 0:2 * FS * B].rearrange("p (b f h) -> p h f b", b=B, f=FS)
            for h in range(2):
                e.tensor_copy(od[64 * h:64 * h + 64, :, :], o_ps[64 * h:64 * h + 64, h, :, :]).then_inc(sd_od, 1)
            for h in range(NH + 2):
                if h < NH:
                    z = flat[:, 1536 * (h % 2):1536 * (h % 2) + SEG]
                    e.wait_ge(sb_z, h + 1)
                    if h >= 2:
                        e.wait_ge(sb_s, h - 1)
                    e.tensor_scalar(zc[h % 2][:, :], z, bias[:, 0, h:h + 1], CLAMP, ALU.add, ALU.min).then_inc(sb_zc, 1)
                    e.wait_ge(sb_l, h + 1)
                    if h >= 2:
                        e.wait_ge(sb_c, h - 1)
                    e.scalar_tensor_tensor(out=sp[h % 2][:, :], in0=z, scalar=bias[:, 0, h:h + 1], in1=zc[h % 2][:, :],
                                           op0=ALU.add, op1=ALU.max).then_inc(sb_s, 1)
                if h % 2 == 1 and h >= 3:
                    f = (h - 3) // 2
                    t = T_MIXB + f
                    e.wait_ge(sb_pv, h - 1)
                    e.wait_ge(sd_od, 2)
                    e.wait_ge(tmp_used, t - NTMP + 1)
                    e.tensor_copy(tmp[:, t % NTMP, TP:T], od[:, f, :]).then_inc(sb_out, 1)
                    e.wait_ge(sb_out, f + 1)
                    e.tensor_copy(tmp[:, t % NTMP, 0:TP], ps[:, 6 + f % 2, :]).then_inc(tmp_ready, 1)
            mem_dve(1, qT[:, FS:KD, :], T_MIXB + FS)
            out_tiles(M_OUTB, y_mix)
            inverse(5)
            norm_tiles(T_P2, y_mix, G_POST_MIX + 8)
            inverse(6)
            for k in range(KD):
                e.scalar_tensor_tensor(out=hf[:, k, :], in0=x[:, k, :], scalar=gain(G_PRE_FFN + 8, k), in1=rstd[:, :],
                                       op0=ALU.mult, op1=ALU.mult).then_inc(hf_ready, 1)

            lg, eq, dl, oh1, oh2, msk, pr, sl = (rt[:, n, :, :] for n in range(8))
            m1, i1, m2, i2, zs, p1, p2, pp = (r5[:, n, :] for n in range(8))
            links = [0]

            def link(ins):
                links[0] += 1
                ins.then_inc(rr, 1)
                e.wait_ge(rr, links[0])

            def over_e(v):
                return v.unsqueeze(2).to_broadcast([P, NT + 1, E])

            e.wait_ge(io_ready, 3)
            link(e.memset(lg, 0.0))
            e.wait_ge(lg_done, 1)
            link(e.tensor_tensor(lg[:, 0:NT, :], ps[:, 4, 0:NT * E].rearrange("p (i e) -> p i e", e=E),
                                 br[:, :].unsqueeze(1).to_broadcast([P, NT, E]), ALU.add))
            link(e.tensor_tensor(lg[0:B, NT, :], ps[0:B, 4, NT * E:(NT + 1) * E], br[0:B, :], ALU.add))

            def first_max(vals, mx, idx, onehot):
                link(e.tensor_reduce(mx, vals, AX, ALU.max))
                link(e.tensor_tensor(eq, vals, over_e(mx), ALU.is_ge))
                link(e.scalar_tensor_tensor(out=eq, in0=eq, scalar=-float(E), in1=io8[:, :, :], op0=ALU.mult, op1=ALU.add))
                link(e.tensor_reduce(idx, eq, AX, ALU.min))
                link(e.tensor_scalar(idx, idx, float(E), None, ALU.add))
                link(e.tensor_tensor(onehot, io8[:, :, :], over_e(idx), ALU.is_equal))

            first_max(lg, m1, i1, oh1)
            e.tensor_tensor(dl, lg, over_e(m1), ALU.subtract).then_inc(rr_m1, 1)
            link(e.scalar_tensor_tensor(out=sl, in0=oh1, scalar=-1e30, in1=lg, op0=ALU.mult, op1=ALU.add))
            first_max(sl, m2, i2, oh2)
            link(e.tensor_tensor(msk, oh1, oh2, ALU.add))
            e.tensor_tensor(msk, msk, over_e(valid[:, :]), ALU.mult).then_inc(mask_ready, 1)
            e.wait_ge(rr_exp, 1)
            link(e.tensor_reduce(zs, pr, AX, ALU.add))
            link(e.reciprocal(zs, zs))
            link(e.tensor_tensor(pr, pr, over_e(zs), ALU.mult))
            link(e.tensor_tensor(dl, pr, oh1, ALU.mult))
            link(e.tensor_reduce(p1, dl, AX, ALU.add))
            link(e.tensor_tensor(dl, pr, oh2, ALU.mult))
            link(e.tensor_reduce(p2, dl, AX, ALU.add))
            link(e.tensor_tensor(pp, p1, p2, ALU.add))
            link(e.reciprocal(pp, pp))
            link(e.tensor_tensor(gate[:, 0, :], p1, pp, ALU.mult))
            link(e.tensor_tensor(gate[:, 1, :], p2, pp, ALU.mult))
            cnt, nb, je, jb = (r8[:, n, :] for n in range(4))
            e.wait_ge(cnt_done, 1)
            link(e.tensor_copy(cnt, ps[:, 5, (NT + 1) * E:(NT + 2) * E]))
            link(e.tensor_scalar(nb, cnt, float(C), 1.0, ALU.is_gt, ALU.add))
            for n in range(2, (T + C - 1) // C):
                link(e.scalar_tensor_tensor(out=nb, in0=cnt, scalar=float(n * C), in1=nb, op0=ALU.is_gt, op1=ALU.add))
            link(e.tensor_copy(je, nb))
            for n in range(1, E):
                link(e.tensor_tensor(je[:, n:n + 1], je[:, n - 1:n], nb[:, n:n + 1], ALU.add))
            link(e.tensor_tensor(jb, je, nb, ALU.subtract))
            link(e.tensor_scalar(jb, jb, 1.0, float(C), ALU.add, ALU.mult))
            link(e.tensor_tensor(sl, ps[:, 5, 0:(NT + 1) * E].rearrange("p (i e) -> p i e", e=E),
                                 jb.unsqueeze(1).to_broadcast([P, NT + 1, E]), ALU.add))
            for s, oh in enumerate((oh1, oh2)):
                link(e.tensor_tensor(dl, sl, oh, ALU.mult))
                link(e.tensor_reduce(m1 if s == 0 else m2, dl, AX, ALU.add))
                link(e.tensor_copy(sloti[:, s, :], m1 if s == 0 else m2))
            link(e.tensor_tensor(jcmp[:, :, :], ioj[:, :, :], je.unsqueeze(1).to_broadcast([P, MAXJOBS, E]), ALU.is_ge))
            link(e.tensor_reduce(jobf[:, 0:MAXJOBS], jcmp[:, :, :], AX, ALU.add))
            link(e.tensor_scalar(jobf[:, 0:MAXJOBS], jobf[:, 0:MAXJOBS], float(E - 1), None, ALU.min))
            link(e.tensor_copy(jobf[:, MAXJOBS:MAXJOBS + 1], je[:, E - 1:E]))
            e.tensor_copy(jobi[:, :], jobf[:, :]).then_inc(slots_ready, 1)
            e.wait_ge(slots_ready, 1)

            nj = e.value_load(jobi[0:1, MAXJOBS:MAXJOBS + 1], min_val=E, max_val=MAXJOBS)
            e.wait_ge(tile_done, M_END)
            e.sem_inc(ew_lo, RAW)
            e.sem_inc(ea_tmp, 1)

            def expert_lo(j, u):
                n = 2048 if u < KE else DN_CUTS[u - KE] * D
                s = u % SPLIT
                e.wait_ge(ew_hi, j * PER_JOB + (u + 1))
                e.tensor_tensor(ewl[:, s, 0:n], eraw[:, u % RAW, 0:n], ewh[:, s, 0:n].bitcast(F32), ALU.subtract)\
                 .then_inc(ew_lo, 1)

            def rows_lo(c, his):
                e.wait_ge(ej_hi, his)
                q = eb_at(2 * KE + c)[0]
                e.tensor_tensor(ejx[:, 2 * c:2 * c + 2, 1, :], ps[:, EB[q], 0:2 * C].rearrange("p (k n) -> p k n", k=2),
                                ejx[:, 2 * c:2 * c + 2, 0, :].bitcast(F32), ALU.subtract).then_inc(eb_free[q], 1)

            def result_rows(done, stored):
                e.wait_ge(ed_done, done)
                e.wait_ge(ys_out, stored)
                for n in range(4):
                    own = slice(0, P) if n < 2 else slice(P - CB, P)
                    e.tensor_copy(etok[own, n // 2, 512 * (n % 2):512 * (n % 2) + 512], ps[own, 2 + n, :])\
                     .then_inc(ey_ready, 1)

            def tile_sum(j, u, t, dst):
                q, n = eb_at(2 * u + t)
                e.wait_ge(eg_done, j * (2 * KE) + (2 * u + t + 1))
                e.tensor_reduce(dst[:, u % 2, :], ps[:, EB[q], 0:2 * C].rearrange("p (h n) -> p n h", h=2), AX, ALU.add)\
                 .then_inc(eb_free[q], 1)

            for c in range(4):
                rows_lo(c, c + 1)
            with e.Fori(0, nj) as j:
                expert_lo(j, 0)
                result_rows(j + 1, j * 32 + 16)
                expert_lo(j, 1)
                for u in range(PER_JOB):
                    if 2 <= u <= KE + 1:
                        v = u - 2
                        e.wait_ge(eg_silu, j * KE + (v + 1))
                        q, n = eb_at(2 * v + 1)
                        e.wait_ge(eb_free[q], j * EB_USES[q] + (n + 2))
                        e.wait_ge(ea_lo, j * KE + (max(v - 1, 0) + 1))
                        e.tensor_tensor(eat[:, v % 2, :], eup[:, v % 2, :], esg[:, v % 2, :], ALU.mult)\
                         .then_inc(ea_tmp, 1)
                    if u + 2 < PER_JOB:
                        expert_lo(j, u + 2)
                    if u < KE:
                        if u >= 2:
                            e.wait_ge(ea_tmp, j * KE + u)
                        tile_sum(j, u, 0, esg)
                        tile_sum(j, u, 1, eup)
                    if u == KE + 1:
                        for c in range(4):
                            rows_lo(c, j * 4 + (4 + c + 1))
            result_rows(nj + 1, nj * 32 + 16)

            e.wait_ge(gp_in, 16)
            for i in range(NT + 2):
                if i <= NT:
                    n = P if i < NT else B
                    e.wait_ge(f_1, i + 1)
                    e.scalar_tensor_tensor(out=fo[0:n, i, :], in0=yr[0:n, i, 1, :], scalar=gate[0:n, 1, i:i + 1],
                                           in1=fo[0:n, i, :], op0=ALU.mult, op1=ALU.add).then_inc(f_2, 1)
                if i >= 1:
                    t = i - 1
                    n = P if t < NT else B
                    e.wait_ge(f_root, t + 1)
                    e.reciprocal(frs[0:n, t, 1:2], frs[0:n, t, 1:2]).then_inc(f_inv, 1)
                    e.wait_ge(f_inv, t + 1)
                    e.scalar_tensor_tensor(out=fo[0:n, t, :], in0=fo[0:n, t, :], scalar=frs[0:n, t, 1:2],
                                           in1=gpost[0:n, :], op0=ALU.mult, op1=ALU.mult).then_inc(f_n, 1)
                    e.wait_ge(f_n, t + 1)
                    e.tensor_tensor(fo[0:n, t, :], fo[0:n, t, :], xtk[0:n, t, :], ALU.add).then_inc(f_y, 1)

        @block.tensor
        def _(e):
            def fill(f, parts):
                if f >= 2:
                    e.wait_ge(tp_free[f % 2], f // 2)
                for dst, src in parts:
                    n = src.shape[0]
                    ins = e.transpose(dst, src, ident[0:n, 0:n])
                ins.then_inc(tp_done, 1)

            def bank(f):
                return ps[:, 6 + f % 2, :]

            def sum_squares(q, first, last):
                e.wait_ge(sq_ready, q + 1)
                for h in range(2):
                    ins = e.matmul(ps[:, 4 + h, 0:HALF], ones[:, :], sq[:, q % 2, h * HALF:(h + 1) * HALF],
                                   start=first, stop=last, skip_group_check=True)
                ins.then_inc(sq_used, 1)
                return ins

            def sum_all(q0, n, inst):
                if inst:
                    e.wait_ge(root_ready, inst)
                for k in range(n):
                    sum_squares(q0 + k, k == 0, k == n - 1)

            def open_sums(inst):
                e.wait_ge(root_ready, inst)
                for h in range(2):
                    e.matmul(ps[:, 4 + h, 0:HALF], ones[:, :], zero[:, :], start=True, stop=False,
                             skip_group_check=True)

            def close_sums(q):
                sum_squares(q, False, False)
                sum_squares(q + 1, False, True)

            def three(dst, w_hi_, w_lo_, x_hi, x_lo, first, last, check=False):
                e.matmul(dst, w_hi_, x_hi, start=first, stop=False, skip_group_check=check)
                e.matmul(dst, w_hi_, x_lo, start=False, stop=False, skip_group_check=check)
                return e.matmul(dst, w_lo_, x_hi, start=False, stop=last, skip_group_check=check)

            def tile(q, s, col, ks, first=True, last=True, xh=hh, xl=hl, k0=0, ready=None):
                for h in range(2):
                    c = slice(h * HALF, (h + 1) * HALF)
                    for n, k in enumerate(ks):
                        if ready and h == 0:
                            e.wait_ge(*ready[n])
                        o = (k - k0) * 2 * P + col
                        ins = three(ps[:, 2 * q + h, 0:HALF], whi[:, s, o:o + P], wlo[:, s, o:o + P],
                                    xh[:, k, c], xl[:, k, c], first and n == 0, last and n == len(ks) - 1)
                return ins

            def inputs(t0, ks=range(KD)):
                return [(tmp_used, t0 + n + 1) for n, _ in enumerate(ks)]

            def chunk_tiles(g, m, i, gi, mi, ks=range(KD), ready=None):
                s = g % 2
                e.wait_ge(w_lo, i * gi + (g + 1))
                for t in range(2):
                    e.wait_ge(tile_free[t], i * (mi // 2) + m // 2)
                    ins = tile(t, s, t * P, ks, ready=ready if t == 0 else None)
                    ins.then_inc(tile_done, 1)

            e.wait_ge(const_ready, 10)
            e.wait_ge(tabs_in, 176)
            fill(TP_CTL, [(bank(TP_CTL)[:, 0:G_ROWS], grow[0:G_ROWS, :])])
            fill(TP_CTL + 1, [(bank(TP_CTL + 1)[:, 93 * i:93 * i + 93], crow[0:93, i, :]) for i in range(2)])
            e.wait_ge(x_in, 80)
            for k in range(KD):
                f = TP_X + k
                fill(f, [(bank(f)[:, i * P:(i + 1) * P], xtok[:, i, k * P:(k + 1) * P]) for i in range(NT)])
            f = TP_X + KD
            fill(f, [(bank(f)[:, k * B:(k + 1) * B], xdec[0:B, k * P:(k + 1) * P]) for k in range(KD)])
            e.wait_ge(mem_sc, 2)
            for c in range(4):
                f = TP_MEM + c
                fill(f, [(bank(f)[:, (2 * k + i) * P:(2 * k + i + 1) * P], memtok[:, i, (2 * c + k) * P:(2 * c + k + 1) * P])
                         for k in range(2) for i in range(MT)])
            sum_all(S_X0, KD, 0)
            for g in range(4):
                e.wait_ge(w_lo, g + 1)
                e.wait_ge(hm_lo, KD * (g // 2 + 1))
                for t in range(MT):
                    m = 2 * g + t
                    if m >= 2:
                        e.wait_ge(tile_free[t], m // 2)
                    for k in range(KD):
                        c = slice(t * P, (t + 1) * P)
                        wv = slice(k * 2 * P, (k + 1) * 2 * P)
                        ins = three(ps[:, 2 * t, 0:NMEM], hmh[:, g // 2, k, c], hml[:, g // 2, k, c],
                                    whi[:, g % 2, wv], wlo[:, g % 2, wv], k == 0, k == KD - 1)
                    ins.then_inc(tile_done, 1)
            e.wait_ge(state_in, 32)
            for c in range(3):
                f = TP_ST + c
                fill(f, [(bank(f)[:, 240 * h + 120 * i:240 * h + 120 * i + 120],
                          sttok[0:4 * PAST, i, (2 * c + h) * P:(2 * c + h + 1) * P]) for h in range(2) for i in range(2)])
            with e.Fori(0, 3) as i:
                for j in range(2):
                    chunk_tiles(U_IN + j, M_IN + 2 * j, i, 2, 4, ready=inputs(T_N0) if j == 0 else None)
            chunk_tiles(U_QM, M_QM, 0, 0, 0)
            e.wait_ge(u_ready, 2 + FS)
            for n, (lo, hi) in enumerate(((0, 4), (4, 6))):
                f = TP_UT + n
                fill(f, [(bank(f)[0:PAST + B, (c - lo) * P:(c - lo + 1) * P], ubuf[:, c, TP:PAST + T]) for c in range(lo, hi)])

            def mem_pe(layer, q):
                m = mem[layer]
                f = (TP_MA, TP_MB)[layer]
                e.wait_ge(mk_in, 32 * (layer + 1))
                fill(f, [(bank(f)[:, (2 * c + i) * P:(2 * c + i + 1) * P], m.ktok[:, i, c * P:(c + 1) * P])
                         for c in range(FM) for i in range(MT)])
                e.wait_ge(mc_in, 16 * B * (layer + 1))
                for b in range(B):
                    g = f + 1 + b
                    fill(g, [(bank(g)[:, (2 * c + i) * P:(2 * c + i + 1) * P], m.cache[:, b, i, c * P:(c + 1) * P])
                             for c in range(FM) for i in range(MT)])
                e.wait_ge(mqz_ready, 4 * (layer + 1))
                copied_out(e, f + 7)
                copied_out(e, f + 8)
                for b in range(B):
                    for c in range(FM):
                        ins = e.matmul(ps[0:32, 4, 0:NMEM], m.qz[:, FM * b + c, :], m.cT[:, b, c, :],
                                       start=(b == 0 and c == 0), stop=(b == B - 1 and c == FM - 1))
                ins.then_inc(md_s, 1)
                e.wait_ge(md_p, layer + 1)
                for i in range(MT):
                    ins = e.transpose(ps[:, 5, 32 * i:32 * i + 32], m.pd[:, i * P:(i + 1) * P], ident[0:32, 0:32])
                ins.then_inc(md_t, 1)
                e.wait_ge(md_pT, layer + 1)
                e.wait_ge(mv_in, 16 * B * (layer + 1))
                for b in range(B):
                    for c in range(FM):
                        o = 2 * (FM * b + c)
                        for i in range(MT):
                            ins = e.matmul(ps[:, 4, o:o + 2], m.cache[:, b, i, c * P:(c + 1) * P],
                                           m.pdT[:, i, 4 * b + 2 * c:4 * b + 2 * c + 2],
                                           start=(o == 0 and i == 0), stop=(i == MT - 1), skip_group_check=True)
                ins.then_inc(md_o, 1)

                def scores(h):
                    c, r = h // 2, slice(64 * (h % 2), 64 * (h % 2) + 64)
                    s = h % 2
                    if h >= 2:
                        e.wait_ge(mp_e, NT * (MH * layer + h - 1))
                    for i in range(NT):
                        ins = e.matmul(ps[:, 2 * s + i // 2, (i % 2) * NMEM:(i % 2 + 1) * NMEM],
                                       q[r, c, i * P:(i + 1) * P], m.kT[r, c, :], start=True, stop=True)
                    ins.then_inc(mp_s, 1)

                scores(0)
                for h in range(MH):
                    if h + 1 < MH:
                        scores(h + 1)
                    s = h % 2
                    e.wait_ge(mp_p, NT * (MH * layer + h + 1))
                    if h >= 1:
                        e.wait_ge(mp_pT, 2 * (MH * layer + h))
                    e.wait_ge(md_od, 2 * (layer + 1))
                    for i in range(MT):
                        for t in range(NT):
                            ins = e.transpose(ps[:, 4 + i, t * P:(t + 1) * P], m.p[:, s, t, i * P:(i + 1) * P], ident[:, :])
                    ins.then_inc(mp_t, 1)
                    e.wait_ge(mp_pT, 2 * (MH * layer + h + 1))
                    for i in range(MT):
                        ins = e.matmul(ps[64 * s:64 * s + 64, 6 + h // 2, :], m.vtok[:, i, h * HD:(h + 1) * HD],
                                       m.pT[:, i, :], start=(i == 0), stop=(i == MT - 1))
                    ins.then_inc(mp_o, 1)

            mem_pe(0, qmA)
            e.wait_ge(cv, (FS - 1) * CW)
            e.wait_ge(cvp, 2 * CW)
            e.wait_ge(cd_sum, FS)
            e.wait_ge(mp_pT, 2 * MH)
            for k in range(FS):
                for h in range(2):
                    ins = e.matmul(ps[:, 4 + h, 0:HALF], ones[:, :], cT[:, k, h * HALF:(h + 1) * HALF],
                                   start=(k == 0), stop=(k == FS - 1), skip_group_check=True)
            ins.then_inc(ln_sum, 1)
            e.wait_ge(ln_mean, 1)
            for k in range(FS):
                e.wait_ge(ln_sq, k + 1)
                for h in range(2):
                    ins = e.matmul(ps[:, 4 + h, 0:HALF], ones[:, :], sq[:, k % 2, h * HALF:(h + 1) * HALF],
                                   start=(k == 0), stop=(k == FS - 1), skip_group_check=True)
                ins.then_inc(ln_used, 1)

            def out_projection(u0, m0, t0, q0, ks, inst):
                e.wait_ge(tmp_used, t0 + 1)
                open_sums(inst)
                for g in range(4):
                    chunk_tiles(u0 + g, m0 + 2 * g, 0, 0, 0, ks, inputs(t0) if g == 0 else None)
                    for t in range(2):
                        sum_squares(q0 + 2 * g + t, False, False)
                close_sums(q0 + 8)

            e.wait_ge(ln_root, 1)
            out_projection(U_OUTA, M_OUTA, T_MIXA, S_YA, MIX_A, 1)
            sum_all(S_XA, KD, 2)
            with e.Fori(0, KF // 2) as i:
                for j in range(2):
                    chunk_tiles(U_GU + j, M_GU + 2 * j, i, 2, 4, ready=inputs(T_N1) if j == 0 else None)
            open_sums(3)
            e.wait_ge(ga_lo, KF)
            with e.Fori(0, 2) as i:
                for c in range(2):
                    for r in range(3):
                        g = U_DN + 3 * c + r
                        ks = range(8 * r, min(8 * r + 8, KF))
                        e.wait_ge(w_lo, i * 6 + (g + 1))
                        for t in range(2):
                            if r == 0:
                                e.wait_ge(tile_free[t], i * 2 + (M_DN // 2 + c))
                            ins = tile(t, g % 2, t * P, ks, r == 0, r == 2, acth, actl, 8 * r)
                            if r == 2:
                                ins.then_inc(tile_done, 1)
                            elif t == 1:
                                ins.then_inc(w_used, 1)
                        if r == 0:
                            for t in range(2):
                                e.wait_ge(sq_ready, i * 4 + (S_YF + 2 * c + t + 1))
                                for h in range(2):
                                    ins = e.matmul(ps[:, 4 + h, 0:HALF], ones[:, :], sq[:, t, h * HALF:(h + 1) * HALF],
                                                   start=False, stop=False, skip_group_check=True)
                                ins.then_inc(sq_used, 1)
            close_sums(S_YF + 8)
            sum_all(S_XF, KD, 4)
            with e.Fori(0, 3) as i:
                for j in range(2):
                    chunk_tiles(U_KV + j, M_KV + 2 * j, i, 2, 4, ready=inputs(T_N2) if j == 0 else None)
            e.wait_ge(tile_free[0], M_Q // 2)
            e.wait_ge(tile_free[1], M_Q // 2)
            for n in range(20):
                w, i, half = n // 10, (n % 10) // 2, n % 2
                f = TP_KV + n
                c0, c1 = (0, 4) if half == 0 else (4, 6)
                src, lo, hi = ((vT, kT)[w], i * P, i * P + P) if i < NT else ((vT, kT)[w], TP, T)
                fill(f, [(bank(f)[0:hi - lo, (c - c0) * P:(c - c0 + 1) * P], src[:, c, lo:hi]) for c in range(c0, c1)])
            with e.Fori(0, 2) as i:
                for j in range(2):
                    chunk_tiles(U_Q + j, M_Q + 2 * j, i, 2, 4, ready=inputs(T_N3) if j == 0 else None)

            e.wait_ge(qd_ready, 2)
            for b in range(B + 1):
                if b < B:
                    e.wait_ge(pg_in[b % 2], 32 * (b // 2 + 1))
                    for c in range(3):
                        f = TP_PG + 3 * b + c
                        parts = [(bank(f)[:, (2 * n + g) * P:(2 * n + g + 1) * P],
                                  pgs[:, b % 2, g, (2 * c + n) * P:(2 * c + n + 1) * P]) for n in range(2) for g in range(NPG)]
                        fill(f, parts)
                if b >= 1:
                    d = b - 1
                    for c in range(3):
                        copied_out(e, TP_PG + 3 * d + c)
                    for c in range(FS):
                        for g in range(NPG):
                            o = 96 * g + NH * d + 2 * c
                            ins = e.matmul(ps[:, 0, o:o + 2], pgT[:, d % 2, c, g * P:(g + 1) * P], qd2[:, d, c, :],
                                           start=(d == 0 and c == 0 and g == 0), stop=False, skip_group_check=True)
                    ins.then_inc(pg_qk, 1)
            e.wait_ge(sd_sp, 1)
            e.matmul(ps[:, 0, 0:96], negtri[:, :], zd[:, 2, 0:96], start=False, stop=False, skip_group_check=True)
            e.matmul(ps[:, 0, 0:96], negone[:, :], zd[:, 2, 96:192], start=False, stop=False, skip_group_check=True)
            e.matmul(ps[:, 0, 96:192], negtri[:, :], zd[:, 2, 96:192], start=False, stop=True, skip_group_check=True)\
             .then_inc(sd_c, 1)
            e.wait_ge(sd_w, 1)
            for b in range(B):
                e.wait_ge(pg_in[b % 2], 32 * (B // 2 + b // 2 + 1))
                for c in range(FS):
                    o = 2 * (FS * b + c)
                    for g in range(NPG):
                        p0 = 96 * g + NH * b + 2 * c
                        ins = e.matmul(ps[:, 1, o:o + 2], pgs[:, b % 2, g, c * P:(c + 1) * P], zd[:, 3, p0:p0 + 2],
                                       start=(o == 0 and g == 0), stop=(g == NPG - 1), skip_group_check=True)
                ins.then_inc(pg_used, 1)
            e.wait_ge(sd_od, 2)

            def segment(buf, i, c0=0):
                return buf[:, SEG_AT[i] + c0:SEG_AT[i] + seg_w[i]]

            for h in range(NH + 2):
                if h < NH:
                    c, r = h // 2, slice(64 * (h % 2), 64 * (h % 2) + 64)
                    z = flat[:, 1536 * (h % 2):1536 * (h % 2) + SEG]
                    if h >= 2:
                        e.wait_ge(sb_w, h - 1)
                    for i in (0, 1, 3, 2):
                        ins = e.matmul(segment(z, i), kT[r, c, i * P:(i + 1) * P], qT[r, c, i * P:TP],
                                       start=(i != 3), stop=False, skip_group_check=True)
                    ins.then_inc(sb_z, 1)
                if 1 <= h <= NH:
                    g = h - 1
                    z = flat[:, 1536 * (g % 2):1536 * (g % 2) + SEG]
                    e.wait_ge(sb_sp, NT * (g + 1))
                    for i in (0, 1, 3, 2):
                        ins = e.matmul(segment(z, i), negtri[:, :], segment(sp[g % 2], i), start=False, stop=False,
                                       skip_group_check=True)
                        for n in range(i + 1, NT):
                            ins = e.matmul(segment(z, i, (n - i) * P), negone[:, :], segment(sp[g % 2], n),
                                           start=False, stop=False, skip_group_check=True)
                    ins.then_inc(sb_c, 1)
                if h >= 2:
                    g = h - 2
                    c, r = g // 2, slice(64 * (g % 2), 64 * (g % 2) + 64)
                    e.wait_ge(sb_wm, NT * (g + 1))
                    if c >= 2:
                        e.wait_ge(tmp_ready, T_MIXB + c - 1)
                    for i in range(NT):
                        ins = e.matmul(ps[r, 6 + c % 2, i * P:TP], vtok[:, i, g * HD:(g + 1) * HD], segment(wt[g % 2], i),
                                       start=(i == 0), stop=(i == NT - 1), skip_group_check=True)
                    ins.then_inc(sb_pv, 1)
            e.wait_ge(tmp_ready, T_MIXB + FS)
            mem_pe(1, qT[:, FS:KD, :])
            out_projection(U_OUTB, M_OUTB, T_MIXB, S_YB, range(KD), 5)
            sum_all(S_XB, KD, 6)

            e.wait_ge(hf_ready, KD)
            e.wait_ge(root_ready, 7)
            for i in range(NT + 1):
                n = P if i < NT else B
                for k in range(KD):
                    ins = e.matmul(ps[0:n, 4, i * E:(i + 1) * E], hf[:, k, i * P:i * P + n], wr[:, k, :],
                                   start=(i == 0 and k == 0), stop=(k == KD - 1), skip_group_check=True)
            ins.then_inc(lg_done, 1)
            for n in range(10):
                f, i = TP_HT + n, n // 2
                w = P if i < NT else B
                fill(f, [(bank(f)[0:w, k * P:(k + 1) * P], hf[:, 4 * (n % 2) + k, i * P:i * P + w]) for k in range(4)])
            e.wait_ge(mask_ready, 1)
            msk = rt[:, 5, :, :]
            for i in range(NT + 1):
                ins = e.matmul(ps[:, 5, i * E:(i + 1) * E], before[:, :], msk[:, i, :], start=(i == 0), stop=False,
                               skip_group_check=True)
                for n in range(i):
                    e.matmul(ps[:, 5, i * E:(i + 1) * E], ones[:, :], msk[:, n, :], start=False, stop=False,
                             skip_group_check=True)
            for n in range(NT + 1):
                ins = e.matmul(ps[:, 5, (NT + 1) * E:(NT + 2) * E], ones[:, :], msk[:, n, :], start=False,
                               stop=(n == NT), skip_group_check=True)
            ins.then_inc(cnt_done, 1)
            for n in range(10):
                f, i = TP_XT + n, n // 2
                w = P if i < NT else B
                fill(f, [(bank(f)[0:w, k * P:(k + 1) * P], x[:, 4 * (n % 2) + k, i * P:i * P + w]) for k in range(4)])

            e.wait_ge(slots_ready, 1)
            nj = e.value_load(jobi[0:1, MAXJOBS:MAXJOBS + 1], min_val=E, max_val=MAXJOBS)
            e.sem_inc(ew_used, len(DN_CUTS) - 1)
            copied_out(e, TP_XT + 8)
            copied_out(e, TP_XT + 9)

            def eb_wait(j, n):
                q, use = eb_at(n)
                e.wait_ge(eb_free[q], j * EB_USES[q] + (use + 1))

            def rows_in(loaded, landed, j):
                e.wait_ge(loaded, landed)
                for c in range(4):
                    q = EB[eb_at(2 * KE + c)[0]]
                    if j is not None:
                        eb_wait(j, 2 * KE + c)
                    for k in range(2):
                        kk = 2 * c + k
                        e.transpose(ps[:, q, k * C:k * C + P], gtok[:, 0, kk * P:(kk + 1) * P], ident[:, :])
                        ins = e.transpose(ps[:, q, k * C + P:(k + 1) * C], gtok[0:CB, 1, kk * P:(kk + 1) * P],
                                          ident[0:CB, 0:CB])
                    ins.then_inc(er_done, 1)

            rows_in(g0_in, 32, None)
            for c in range(4):
                for h in range(2):
                    ins = e.matmul(ps[:, 2 + c, 256 * h:256 * h + 256], ones[:, :], zero[:, 0:256], start=True, stop=True)
            ins.then_inc(ed_done, 1)
            with e.Fori(0, nj) as j:
                for u in range(PER_JOB):
                    s = u % SPLIT
                    e.wait_ge(ew_lo, j * PER_JOB + (RAW + u + 1))
                    if u < KE:
                        if u == 0:
                            e.wait_ge(ej_hi, j * 4 + 4)
                            for c in range(4):
                                eb_wait(j, c)
                        for t in range(2):
                            eb_wait(j, 2 * u + t)
                            q = EB[eb_at(2 * u + t)[0]]
                            for k in range(KD):
                                o = k * 2 * P + t * P
                                e.matmul(ps[:, q, 0:2 * C], ewh[:, s, o:o + P],
                                         ejx[:, k, :, :].rearrange("p h n -> p (h n)"), start=(k == 0),
                                         stop=(k == KD - 1), skip_group_check=True)
                                ins = e.matmul(ps[:, q, C:2 * C], ewl[:, s, o:o + P], ejx[:, k, 0, :], start=False,
                                               stop=(k == KD - 1), skip_group_check=True)
                            ins.then_inc(eg_done, 1)
                        if u == KE - 1:
                            rows_in(gt_in, j * 32 + 32, j)
                    else:
                        n, k0 = DN_CUTS[u - KE], DN_K0[u - KE]
                        if u == KE:
                            e.wait_ge(ey_ready, j * 4 + 4)
                        for i in range(n):
                            k = k0 + i
                            e.wait_ge(ea_lo, j * KE + (k + 2))
                            for c in range(4):
                                o, m = CB * (c // 2), i * D + 512 * (c % 2)
                                ins = three(ps[:, 2 + c, :], eah[:, k, o:o + P], eal[:, k, o:o + P],
                                            ewh[:, s, m:m + 512], ewl[:, s, m:m + 512], k == 0, k == KE - 1, True)
                        ins.then_inc(ew_used if u < PER_JOB - 1 else ed_done, 1)


_OUTS = [(1, TP, D), (B, 1, D), (1, 1, PAST, FS * P), (1, TP, NH, HD), (1, TP, NH, HD), (2, 1, NMEM, MH, HD),
         (2, 1, NMEM, MH, HD), (1, B, PAST, FS * P), (B, 1, NH, HD), (B, 1, NH, HD)]


def kernel(**inputs):
    import numpy as _np
    import concourse.bacc as _bacc
    from concourse.bass_utils import run_bass_kernel_spmd as _run

    nc = _bacc.Bacc("TRN2", target_bir_lowering=False, num_devices=1)
    arrays, args = {}, {}
    for name, value in inputs.items():
        v = _np.ascontiguousarray(value)
        arrays[f"in_{name}"] = v
        args[name] = nc.dram_tensor(f"in_{name}", v.shape, mybir.dt.from_np(v.dtype), kind="ExternalInput").ap()
    outs = [nc.dram_tensor(f"out_{i}", shape, F32, kind="ExternalOutput").ap() for i, shape in enumerate(_OUTS)]
    build(nc, args, outs)
    r = _run(nc, [arrays], core_ids=[0])
    return tuple(r.results[0][f"out_{i}"] for i in range(len(_OUTS)))
```
